# Optimizing a Trainium2 kernel written in Bass

```python
import math
import jax, jax.numpy as jnp
from jax import lax
import numpy as np

D_MODEL = 2048
BATCH = 1
SEQ = 256
DEPTH = 2

HEAD_DIM = 128
ATTN_WIDTH = D_MODEL // 2
N_HEADS_A = ATTN_WIDTH // HEAD_DIM
IDX_HEADS = 16
IDX_DIM = 64
INDEX_TOPK = 256
Q_BLOCK = 128
REL_BUCKETS = 32
REL_MAX_DIST = 128
CONV_CH = D_MODEL // 2
CONV_WIDTH = 31
POOL_WINDOWS = (2, 4, 8, 16)
POOL_GROUPS = len(POOL_WINDOWS)
POOL_CH = D_MODEL // POOL_GROUPS
N_GROUPS = 4
EXPERTS_PER_GROUP = 4
N_EXPERTS = N_GROUPS * EXPERTS_PER_GROUP
EXPERT_FF = D_MODEL // 4
INNER_TOPK = 2
IN_SPLITS = (ATTN_WIDTH, HEAD_DIM, HEAD_DIM, IDX_HEADS * IDX_DIM, IDX_DIM, IDX_HEADS, 2 * CONV_CH)
IN_WIDTH = sum(IN_SPLITS)
MIX_WIDTH = ATTN_WIDTH + CONV_CH
N_EVEN = (DEPTH + 1) // 2
N_ODD = DEPTH // 2
NORM_EPS = 1e-6

kernel_name = "dsa_conformer_pool_hmoe_hybrid"

def rms_norm(x, w):
    xf = x.astype(jnp.float32)
    y = xf * lax.rsqrt(jnp.mean(xf * xf, axis=-1, keepdims=True) + NORM_EPS)
    return (y * w.astype(jnp.float32)).astype(x.dtype)

def rel_bucket(dist):
    n = jnp.maximum(dist, 0)
    max_exact = REL_BUCKETS // 2
    nf = jnp.maximum(n, 1).astype(jnp.float32)
    large = max_exact + (jnp.log(nf / max_exact) / math.log(REL_MAX_DIST / max_exact)
                         * (REL_BUCKETS - max_exact)).astype(jnp.int32)
    large = jnp.minimum(large, REL_BUCKETS - 1)
    return jnp.where(n < max_exact, n, large)

def dsa_attention(q, k, v, iq, ik, iw, rel_bias, k_top):
    B, S = q.shape[0], q.shape[1]
    nb = S // Q_BLOCK

    def to_blocks(a):
        return jnp.moveaxis(a.reshape((B, nb, Q_BLOCK) + a.shape[2:]), 1, 0)

    pos = jnp.arange(S)
    starts = jnp.arange(nb) * Q_BLOCK

    def block(args):
        qb, iqb, iwb, t0 = args
        t = t0 + jnp.arange(Q_BLOCK)
        il = jnp.einsum('bqhd,bsd->bqhs', iqb, ik, preferred_element_type=jnp.float32) * (IDX_DIM ** -0.5)
        score = jnp.einsum('bqhs,bqh->bqs', jax.nn.relu(il), iwb.astype(jnp.float32))
        causal = pos[None, :] <= t[:, None]
        score = jnp.where(causal[None], score, -jnp.inf)
        _, sel = lax.top_k(score, k_top)
        valid = sel <= t[None, :, None]
        k_sel = jax.vmap(lambda a, i: a[i])(k, sel)
        v_sel = jax.vmap(lambda a, i: a[i])(v, sel)
        logits = jnp.einsum('bqhd,bqkd->bqhk', qb, k_sel, preferred_element_type=jnp.float32) * (HEAD_DIM ** -0.5)
        bias = rel_bias[rel_bucket(t[None, :, None] - sel)]
        logits = logits + jnp.moveaxis(bias, -1, 2).astype(jnp.float32)
        logits = jnp.where(valid[:, :, None, :], logits, -jnp.inf)
        p = jax.nn.softmax(logits, axis=-1)
        o = jnp.einsum('bqhk,bqkd->bqhd', p.astype(v.dtype), v_sel)
        return o.reshape(B, Q_BLOCK, N_HEADS_A * HEAD_DIM)

    out = lax.map(block, (to_blocks(q), to_blocks(iq), to_blocks(iw), starts))
    return jnp.moveaxis(out, 0, 1).reshape(B, S, N_HEADS_A * HEAD_DIM)

def conformer_conv(glu_in, conv_w, conv_b, ln_g, ln_b):
    a, g = jnp.split(glu_in, 2, axis=-1)
    u = a * jax.nn.sigmoid(g)
    u = lax.conv_general_dilated(u, conv_w[:, None, :].astype(u.dtype), window_strides=(1,),
                                 padding=[(CONV_WIDTH - 1, 0)],
                                 dimension_numbers=('NWC', 'WIO', 'NWC'),
                                 feature_group_count=CONV_CH)
    uf = u.astype(jnp.float32) + conv_b.astype(jnp.float32)
    mu = jnp.mean(uf, axis=-1, keepdims=True)
    var = jnp.mean(jnp.square(uf - mu), axis=-1, keepdims=True)
    uf = (uf - mu) * lax.rsqrt(var + NORM_EPS) * ln_g.astype(jnp.float32) + ln_b.astype(jnp.float32)
    return jax.nn.silu(uf).astype(glu_in.dtype)

def even_layer(x, rel_bias, norm_w, w_in, q_norm_w, k_norm_w, conv_w, conv_b, ln_g, ln_b, w_out, k_top):
    B, S, _ = x.shape
    h = rms_norm(x, norm_w)
    proj = h @ w_in
    cuts = [int(c) for c in np.cumsum(IN_SPLITS)[:-1]]
    q, k, v, iq, ik, iw, glu_in = jnp.split(proj, cuts, axis=-1)
    q = rms_norm(q.reshape(B, S, N_HEADS_A, HEAD_DIM), q_norm_w)
    k = rms_norm(k, k_norm_w)
    iq = iq.reshape(B, S, IDX_HEADS, IDX_DIM)
    iw = iw * (IDX_HEADS ** -0.5)
    attn = dsa_attention(q, k, v, iq, ik, iw, rel_bias, k_top)
    conv = conformer_conv(glu_in, conv_w, conv_b, ln_g, ln_b)
    return x + jnp.concatenate([attn, conv], axis=-1) @ w_out

def odd_layer(x, norm_w, pool_w, pool_scale):
    B, S, _ = x.shape
    h = rms_norm(x, norm_w)
    hf = h.astype(jnp.float32).reshape(B, S, POOL_GROUPS, POOL_CH)
    c = jnp.concatenate([jnp.zeros((B, 1, POOL_GROUPS, POOL_CH), jnp.float32),
                         jnp.cumsum(hf, axis=1)], axis=1)
    t = jnp.arange(S)
    outs = []
    for g, w in enumerate(POOL_WINDOWS):
        cg = c[:, :, g]
        prev = jnp.maximum(t + 1 - w, 0)
        count = jnp.minimum(t + 1, w).astype(jnp.float32)[None, :, None]
        mean = (cg[:, 1:] - cg[:, prev]) / count
        outs.append(mean - hf[:, :, g])
    d = jnp.stack(outs, axis=2).astype(x.dtype)
    mixed = jnp.einsum('bsgc,gce->bsge', d, pool_w).reshape(B, S, D_MODEL)
    return x + pool_scale * mixed

def hier_moe(x, norm_w, wg, bg, we, be, w_gate, w_up, w_down):
    B, S, D = x.shape
    h = rms_norm(x, norm_w).reshape(-1, D)
    T = h.shape[0]
    g_prob = jax.nn.softmax((h @ wg).astype(jnp.float32) + bg.astype(jnp.float32), axis=-1)
    g_p, g_idx = lax.top_k(g_prob, 1)
    e_logits = ((h @ we).astype(jnp.float32) + be.astype(jnp.float32)).reshape(T, N_GROUPS, EXPERTS_PER_GROUP)
    e_logits = jnp.take_along_axis(e_logits, g_idx[:, :, None], axis=1)[:, 0]
    e_p, e_idx = lax.top_k(jax.nn.softmax(e_logits, axis=-1), INNER_TOPK)
    e_p = e_p / jnp.sum(e_p, axis=-1, keepdims=True)
    gate = g_p * e_p
    flat = g_idx * EXPERTS_PER_GROUP + e_idx
    combine = jnp.sum(jax.nn.one_hot(flat, N_EXPERTS, dtype=jnp.float32) * gate[..., None], axis=1)
    y = jnp.zeros((T, D), jnp.float32)
    for e in range(N_EXPERTS):
        a = jax.nn.silu(h @ w_gate[e]) * (h @ w_up[e])
        y = y + combine[:, e:e + 1] * (a @ w_down[e]).astype(jnp.float32)
    return x + y.reshape(B, S, D).astype(x.dtype)

def setup_inputs(seed: int = 0) -> dict:
    key = jax.random.key(seed)
    ks = jax.random.split(key, 24)

    def nrm(k, shape, scale):
        return jax.random.normal(k, shape, jnp.float32) * scale

    def gain(k, shape):
        return 1.0 + 0.05 * jax.random.normal(k, shape, jnp.float32)

    return {
        "x": nrm(ks[0], (BATCH, SEQ, D_MODEL), 1.0),
        "rel_bias": nrm(ks[1], (REL_BUCKETS, N_HEADS_A), 0.5),
        "mix_norm_e": gain(ks[2], (N_EVEN, D_MODEL)),
        "w_in_e": nrm(ks[3], (N_EVEN, D_MODEL, IN_WIDTH), D_MODEL ** -0.5),
        "q_norm_e": gain(ks[4], (N_EVEN, HEAD_DIM)),
        "k_norm_e": gain(ks[5], (N_EVEN, HEAD_DIM)),
        "conv_w_e": nrm(ks[6], (N_EVEN, CONV_WIDTH, CONV_CH), CONV_WIDTH ** -0.5),
        "conv_b_e": nrm(ks[7], (N_EVEN, CONV_CH), 0.02),
        "conv_ln_g_e": gain(ks[8], (N_EVEN, CONV_CH)),
        "conv_ln_b_e": nrm(ks[9], (N_EVEN, CONV_CH), 0.02),
        "w_out_e": nrm(ks[10], (N_EVEN, MIX_WIDTH, D_MODEL), MIX_WIDTH ** -0.5),
        "mix_norm_o": gain(ks[11], (N_ODD, D_MODEL)),
        "pool_w_o": nrm(ks[12], (N_ODD, POOL_GROUPS, POOL_CH, POOL_CH), POOL_CH ** -0.5),
        "pool_scale_o": gain(ks[13], (N_ODD, D_MODEL)),
        "ffn_norm": gain(ks[14], (DEPTH, D_MODEL)),
        "router_group_w": nrm(ks[15], (DEPTH, D_MODEL, N_GROUPS), D_MODEL ** -0.5),
        "router_group_b": nrm(ks[16], (DEPTH, N_GROUPS), 0.01),
        "router_expert_w": nrm(ks[17], (DEPTH, D_MODEL, N_EXPERTS), D_MODEL ** -0.5),
        "router_expert_b": nrm(ks[18], (DEPTH, N_EXPERTS), 0.01),
        "w_gate": nrm(ks[19], (DEPTH, N_EXPERTS, D_MODEL, EXPERT_FF), D_MODEL ** -0.5),
        "w_up": nrm(ks[20], (DEPTH, N_EXPERTS, D_MODEL, EXPERT_FF), D_MODEL ** -0.5),
        "w_down": nrm(ks[21], (DEPTH, N_EXPERTS, EXPERT_FF, D_MODEL), EXPERT_FF ** -0.5),
    }

def reference(x, rel_bias, mix_norm_e, w_in_e, q_norm_e, k_norm_e, conv_w_e, conv_b_e,
              conv_ln_g_e, conv_ln_b_e, w_out_e, mix_norm_o, pool_w_o, pool_scale_o,
              ffn_norm, router_group_w, router_group_b, router_expert_w, router_expert_b,
              w_gate, w_up, w_down):
    k_top = min(INDEX_TOPK, x.shape[1] // 4)
    for l in range(DEPTH):
        i = l // 2
        if l % 2 == 0:
            x = even_layer(x, rel_bias, mix_norm_e[i], w_in_e[i], q_norm_e[i], k_norm_e[i],
                           conv_w_e[i], conv_b_e[i], conv_ln_g_e[i], conv_ln_b_e[i], w_out_e[i], k_top)
        else:
            x = odd_layer(x, mix_norm_o[i], pool_w_o[i], pool_scale_o[i])
        x = hier_moe(x, ffn_norm[l], router_group_w[l], router_group_b[l], router_expert_w[l],
                     router_expert_b[l], w_gate[l], w_up[l], w_down[l])
    return x


_drawn_inputs = setup_inputs


def setup_inputs(seed=0):
    import zlib

    import numpy as np

    out = dict(_drawn_inputs(seed))
    spreads = {}
    factors = {'q_norm_e': 2.822,
     'k_norm_e': 2.755,
     'conv_ln_b_e': 3.107,
     'router_group_b': 3.613,
     'router_expert_b': 4.706}
    for name, (base, spread) in spreads.items():
        noise = np.random.default_rng([zlib.crc32(name.encode()), seed]).standard_normal(out[name].shape)
        drawn = base * np.exp(spread * noise) if base else spread * noise
        out[name] = __import__('jax').numpy.asarray(drawn.astype(out[name].dtype))
    for name, factor in factors.items():
        out[name] = (out[name] * factor).astype(out[name].dtype)
    return out
```

```python
from contextlib import ExitStack

import numpy as np

import concourse.bass as bass
from concourse import mybir

ALU = mybir.AluOpType
ACT = mybir.ActivationFunctionType
F32 = mybir.dt.float32
I32 = mybir.dt.int32
X = mybir.AxisListType.X

P = 128
D = 2048
SEQ = 256
NT = SEQ // P
KC = D // P
HEADS, HD = 8, 128
IH, ID = 16, 64
TOPK = SEQ // 4
BUCKETS = 32
TAPS, CCH = 31, 1024
CC = CCH // P
PAD = TAPS - 1
WINDOWS = (2, 4, 8, 16)
NG, EPG = 4, 4
NE = NG * EPG
FF = 512
FC = FF // P
EPS = 1e-6
NEG = -1e30
TAKEN = -3e38

Q0 = 0
K0 = 1024
IQ0 = 1280
IK0 = 2304
GA0 = 2384
GG0 = 3408
KVW = 256
IKW = 80

RING = 12
BLK = 4 * 512
ROUND = NG * EPG * 12
PASS_BLOCKS = EPG * 12
UNITS = [(0, "g"), (0, "u"), (1, "g"), (0, "d"), (1, "u"), (2, "g"), (1, "d"), (2, "u"), (3, "g"), (2, "d"),
         (3, "u"), (3, "d")]
BANK_U, BANK_T, BANK_Y = 2, 3, 4
GATHER_BANK = (0, 3, 0, 3)
NPASS = 2 * NG + 1

V_CB, V_LG, V_LB, V_QN, V_KN, V_POOL = 0, CC, 2 * CC, 3 * CC, 3 * CC + 1, 3 * CC + 2
V_ROWS = 3 * CC + 2 + KC
CW_ROWS = TAPS * CC
CW_HALF = CW_ROWS // 2


def mixer0_jobs():
    jobs = [("a0", (0, 1, 2, 3)), ("g0", (4, 5, 6, 7)), ("a1", (0, 1, 2, 3)), ("g1", (4, 5, 6, 7)),
            ("flip", (0, 1, 2, 3)),
            ("kvi", (4, 5)), ("iq0", (0, 1, 2, 3)), ("kT", (6,)), ("iq1", (4, 5, 7, 0))]
    jobs += [(f"il{i}", ((3 + i) % 8,)) for i in range(12)]
    jobs += [("q0", (0, 1)), ("q1", (2, 3))]
    jobs += [(f"qT{i}", (4 + i,)) for i in range(4)]
    jobs += [("lg0", (0, 1)), ("lg1", (2, 3, 4, 5)), ("mean", (6,)), ("var", (7,))]
    jobs += [(f"wc{n}", ((6, 7), (0, 1))[n % 2]) for n in range(4)]
    jobs += [(f"pT{i}", (2 + i % 4,)) for i in range(6)]
    jobs += [(f"oT{i}", (2 + (i + 2) % 4,)) for i in range(4)]
    jobs += [(f"wa{n}", ((6, 7), (0, 1))[n % 2]) for n in range(4)]
    return jobs


JOBS = mixer0_jobs()
JOB_AT = {name: i for i, (name, _) in enumerate(JOBS)}
BANKS = dict(JOBS)


STREAM = [("a0", 4), ("g0", 4), ("a1", 4), ("g1", 4), ("kvi", 4), ("iq0", 4), ("iq1", 4), ("q0", 4), ("q1", 4)]
STREAM += [(f"wc{n}", 2) for n in range(4)] + [(f"wa{n}", 2) for n in range(4)]
STREAM_END = {name: sum(k for _, k in STREAM[:i + 1]) for i, (name, _) in enumerate(STREAM)}


def job_number(name):
    return sum(n not in STREAM_END for n, _ in JOBS[:JOB_AT[name] + 1])


def owner_before(name, bank):
    before = [n for n, banks in JOBS[:JOB_AT[name]] if bank in banks]
    return before[-1] if before else None


def indexer_heads(i):
    if i < 4:
        return 0, [8 * (i // 2) + 2 * m + i % 2 for m in range(4)]
    i -= 4
    return 1, [4 * (i // 2) + 2 * m + i % 2 for m in range(2)]


def build(nc, a):
    x_in, out = a["x"], a["out"]
    ctx = ExitStack()
    with ctx:
        def sb(name, shape, dt=F32):
            return ctx.enter_context(nc.sbuf_tensor(name, shape, dt))

        def sem(name):
            return ctx.enter_context(nc.semaphore(name))

        x_sb = sb("x_sb", [P, NT, D])
        xn = sb("xn", [P, NT * D])
        hT = sb("hT", [P, KC, SEQ])
        ring = sb("ring", [P, RING, BLK])
        const_sb = sb("const_sb", [P, 4 * P + SEQ + 8])
        vec_sb = sb("vec_sb", [P, V_ROWS])
        cw_sb = sb("cw_sb", [P, CW_ROWS])
        norm_cols = sb("norm_cols", [P, 3, KC])
        router_w = sb("router_w", [P, 2, KC, 20])
        router_b = sb("router_b", [P, 2, 20])
        ones = sb("ones", [P, P])
        sumsq = sb("sumsq", [P, 4, NT])
        meansq = sb("meansq", [P, 4, NT])
        rstd = sb("rstd", [P, 4, NT])
        minus_half = sb("minus_half", [P, SEQ])
        tick = sb("tick", [P, 24])
        upside = const_sb[:, 3 * P + SEQ + 8:]
        ident = const_sb[:, 0:P]
        before = const_sb[:, P:2 * P]
        slot_no = const_sb[:, 2 * P:3 * P]
        causal = const_sb[:, 3 * P:3 * P + SEQ]
        prio = const_sb[:, 3 * P + SEQ:3 * P + SEQ + 4]

        WORK = 13140
        work = sb("work", [P, WORK])

        def cut(at, *shape):
            n = int(np.prod(shape))
            assert at + n <= WORK, (at, n)
            flat = work[:, at:at + n]
            if len(shape) == 2:
                flat = flat.rearrange("p (a b) -> p a b", b=shape[1])
            if len(shape) == 3:
                flat = flat.rearrange("p (a b c) -> p a b c", b=shape[1], c=shape[2])
            return flat, at + n

        uT, o = cut(0, CC, PAD + SEQ)
        conv, o = cut(o, CC, SEQ)
        iqT, o = cut(o, CC, SEQ)
        ikT, o = cut(o, SEQ)
        kT, o = cut(o, SEQ)
        v_sb, o = cut(o, NT, P)
        k_sb, o = cut(o, NT, P)
        ik2, o = cut(o, NT, P)
        iw_sb, o = cut(o, NT, IH)
        il_relu, o = cut(o, 2, 512)
        score, o = cut(o, NT, SEQ)
        picked, o = cut(o, NT, SEQ)
        top8, o = cut(o, NT, 8)
        ksq, o = cut(o, 8)
        hsq, o = cut(o, NT, HEADS)
        hms, o = cut(o, NT, HEADS)
        hrs, o = cut(o, NT, HEADS)
        smax, o = cut(o, NT, HEADS)
        ssum, o = cut(o, NT, HEADS)
        srec, o = cut(o, NT, HEADS)
        bias_sb, o = cut(o, HEADS, SEQ)
        logits0, o = cut(o, HEADS, P)
        bias_up = iqT
        th_glu = conv[:, 0:4, :]
        th_conv = uT.rearrange("p a b -> p (a b)")[:, 0:CC * SEQ].rearrange("p (h s) -> p h s", h=CC)
        mean_sb = il_relu[:, 0, 0:SEQ]
        rvar = il_relu[:, 1, 0:SEQ]
        vsq = iqT
        qn = xn[:, 0:NT * HEADS * HD].rearrange("p (t c) -> p t c", t=NT)
        qT = xn[:, NT * HEADS * HD:].rearrange("p (h s) -> p h s", h=HEADS)
        hT_flat = hT[:].rearrange("p k s -> p (k s)")
        pT0 = qn.rearrange("p t c -> p (t c)")[:, 0:HEADS * P]
        pT1 = hT_flat[:, 0:2 * HEADS * P].rearrange("p (s c) -> p s c", s=2)
        attnT = hT_flat[:, 2 * HEADS * P:].rearrange("p (h s) -> p h s", h=HEADS)
        qsq = il_relu

        scale_bc, o2 = cut(8020, D)
        band, o2 = cut(o2, NT, 4 * SEQ)
        mixed, o2 = cut(o2, 2, 512)

        hgT, o3 = cut(0, KC, P)
        th_gate, o3 = cut(o3, 2, 512)
        gated, o3 = cut(o3, 2, 512)
        act, o3 = cut(o3, 512)
        actT, o3 = cut(o3, FC, P)
        y_sb, o3 = cut(o3, D)
        pick, o3 = cut(o3, NT, P)
        pickT, o3 = cut(o3, NT, P)
        comb_now, o3 = cut(o3, NT, EPG)
        comb_slot, o3 = cut(o3, EPG)
        lgt, o3 = cut(o3, NT, 20)
        oneh, o3 = cut(o3, NT, NG)
        sel1, o3 = cut(o3, NT, NG)
        sel2, o3 = cut(o3, NT, NG)
        t4a, o3 = cut(o3, NT, NG)
        t4b, o3 = cut(o3, NT, NG)
        el, o3 = cut(o3, NT, EPG)
        ex_g, o3 = cut(o3, NT, NG)
        ex_e, o3 = cut(o3, NT, EPG)
        wgt, o3 = cut(o3, NT, EPG)
        prod, o3 = cut(o3, NT, NE)
        comb, o3 = cut(o3, NT, NPASS * EPG)
        rank_in, o3 = cut(o3, NT, NPASS)
        gmax, o3 = cut(o3, NT, 1)
        stat, o3 = cut(o3, 8, NT)
        cnt, o3 = cut(o3, NG)
        assert o3 <= 8020
        vec_rows = conv.rearrange("p a b -> p (a b)")[:, 0:3 * P].rearrange("p (a b) -> p a b", a=3)
        one_hot = conv.rearrange("p a b -> p (a b)")[0:BUCKETS, 512:1024]
        rel_sb = conv.rearrange("p a b -> p (a b)")[0:BUCKETS, 1024:1024 + HEADS]
        bias_row = conv.rearrange("p a b -> p (a b)")[0:HEADS, 1536:2048]
        npass_i = sb("npass_i", [P, 4], I32)

        ps = ctx.enter_context(nc.psum_tensor("ps", [P, 8, 512], F32))
        bias_dram = nc.dram_tensor("bias_dram", [HEADS, 512], F32, kind="Internal").ap()

        const_in = sem("const_in")
        rows_in = sem("rows_in")
        x_loaded = sem("x_loaded")
        scale_in = sem("scale_in")
        bias_stored = sem("bias_stored")
        bias_loaded = sem("bias_loaded")
        bias_out = sem("bias_out")
        x_stored = sem("x_stored")
        set_up = sem("set_up")
        vec_done = sem("vec_done")
        vec_out = sem("vec_out")
        x_ready = sem("x_ready")
        sq_done = sem("sq_done")
        ms_done = sem("ms_done")
        rstd_done = sem("rstd_done")
        xn_done = sem("xn_done")
        xT_done = sem("xT_done")
        xT_out = sem("xT_out")
        job_done = sem("job_done")
        th_done = sem("th_done")
        u_done = sem("u_done")
        conv_step = sem("conv_step")
        kvi_out = sem("kvi_out")
        k_scaled = sem("k_scaled")
        kT_out = sem("kT_out")
        iq_out = sem("iq_out")
        head_ms = sem("head_ms")
        head_rs = sem("head_rs")
        relu_done = sem("relu_done")
        score_step = sem("score_step")
        topk_step = sem("topk_step")
        qsq_done = sem("qsq_done")
        hsq_done = sem("hsq_done")
        qn_done = sem("qn_done")
        qT_out = sem("qT_out")
        logit_step = sem("logit_step")
        exp_done = sem("exp_done")
        prob_step = sem("prob_step")
        prob_done = sem("prob_done")
        pT_out = sem("pT_out")
        oT_out = sem("oT_out")
        ln_step = sem("ln_step")
        ln_pool = sem("ln_pool")
        y_half = sem("y_half")
        th_conv_done = sem("th_conv_done")
        conv_done = sem("conv_done")
        x_added = sem("x_added")
        dT_done = sem("dT_done")
        dT_out = sem("dT_out")
        mix_done = sem("mix_done")
        mix_step = sem("mix_step")
        mixer_in = [sem(f"mixer_in{s}") for s in range(RING)]
        mixer_used = sem("mixer_used")
        pool_in = [sem(f"pool_in{s}") for s in range(NG)]
        moe = []
        for l in range(2):
            moe.append({n: sem(f"{n}_{l}") for n in (
                "router_done", "route_step", "exp_out", "exp_in", "rank_done", "route_done", "pick_ready", "gathered", "gather_out",
                "rank_in", "misc_done", "misc_out", "th_gate_done", "gated_done", "act_done",
                "actT_done", "actT_out", "y_out", "scattered", "x_moved", "used")})
            moe[l]["in"] = [sem(f"moe_in{l}_{s}") for s in range(RING)]

        w_in = a["w_in_e"][0].rearrange("(p k) n -> p k n", k=KC)
        w_out = a["w_out_e"][0].rearrange("(c p) n -> p c n", p=P)

        def in_block(kq, col, n):
            return lambda slot: [(ring[:, slot, 0:4 * n].rearrange("p (k n) -> p k n", k=4),
                                  w_in[:, 4 * kq:4 * kq + 4, col:col + n])]

        def kvi_block(kq):
            return lambda slot: [
                (ring[:, slot, 0:4 * KVW].rearrange("p (k n) -> p k n", k=4),
                 w_in[:, 4 * kq:4 * kq + 4, K0:K0 + KVW]),
                (ring[:, slot, 4 * KVW:4 * (KVW + IKW)].rearrange("p (k n) -> p k n", k=4),
                 w_in[:, 4 * kq:4 * kq + 4, IK0:IK0 + IKW])]

        def out_block(cq, n):
            return lambda slot: [(ring[:, slot, :].rearrange("p (k n) -> p k n", k=4),
                                  w_out[:, 4 * cq:4 * cq + 4, n * 512:n * 512 + 512])]

        mixer_blocks = []
        for col in (GA0, GG0, GA0 + 512, GG0 + 512):
            mixer_blocks += [in_block(kq, col, 512) for kq in range(4)]
        mixer_blocks += [kvi_block(kq) for kq in range(4)]
        for col in (IQ0, IQ0 + 512, Q0, Q0 + 512):
            mixer_blocks += [in_block(kq, col, 512) for kq in range(4)]
        for half in (2, 0):
            mixer_blocks += [out_block(half + q, n) for n in range(4) for q in range(2)]
        NMIX = len(mixer_blocks)
        MOE0 = [NMIX, NMIX + ROUND + NG]
        POOL0 = NMIX + ROUND
        kvi_at = [16 + i for i in range(4)]

        def moe_source(l, g, j):
            e, kind = UNITS[j // 4]
            name, rows = {"g": ("w_gate", KC), "u": ("w_up", KC), "d": ("w_down", FC)}[kind]
            w = a[name][l].rearrange("e (p k) n -> p e (k n)", k=rows)
            return w[:, bass.ds(g * EPG + e, 1), (j % 4) * BLK:(j % 4 + 1) * BLK]

        def unit_done(eng, l, p, e, kind):
            eng.wait_ge(moe[l]["used"], p * PASS_BLOCKS + 4 * (UNITS.index((e, kind)) + 1))

        def moe_slot(l, j):
            return (MOE0[l] + j) % RING

        def wait_for_job(eng, name):
            if name in STREAM_END:
                eng.wait_ge(mixer_used, STREAM_END[name])
            else:
                eng.wait_ge(job_done, job_number(name))

        heads_before = [0]
        for i in range(12):
            heads_before.append(heads_before[-1] + len(indexer_heads(i)[1]))

        def emptied(name):
            kind, i = name.rstrip("0123456789"), int(name[-1] if name[-1].isdigit() else 0)
            if name in ("il10", "il11"):
                i = int(name[2:])
            return {"a": (u_done, i + 1), "g": (th_done, i + 1), "flip": (bias_out, 1), "kvi": (k_scaled, 2), "iq": (iq_out, i + 1),
                    "kT": (kT_out, 1), "il": (relu_done, i + 1), "q": (qn_done, 2 * i + 2), "qT": (qT_out, i + 1),
                    "lg": (logit_step, 3 + 3 * i), "mean": (ln_step, 1), "var": (ln_step, 3),
                    "wc": (x_added, 2 * i + 2), "wa": (x_added, 2 * i + 10), "pT": (pT_out, i + 1),
                    "oT": (oT_out, i + 1)}[kind]

        block = ctx.enter_context(nc.Block())

        @block.sync
        def _(sp):
            sp.dma_start(x_sb[:], x_in[0].rearrange("(t p) d -> p t d", p=P)).then_inc(x_loaded, 16)
            for b, parts in enumerate(mixer_blocks):
                s = b % RING
                if b >= RING:
                    sp.wait_ge(mixer_used, b - RING + 1)
                for dst, src in parts(s):
                    sp.dma_start(dst, src).then_inc(mixer_in[s], 16)

            def load_moe(l, g, j):
                sp.dma_start(ring[:, moe_slot(l, j):moe_slot(l, j) + 1, :], moe_source(l, g, j)) \
                    .then_inc(moe[l]["in"][moe_slot(l, j)], 16)

            def stream_round(l, base):
                used = moe[l]["used"]
                with sp.Fori(0, NG - 1) as g:
                    for j in range(RING, PASS_BLOCKS):
                        sp.wait_ge(used, g * PASS_BLOCKS + (base + j - RING + 1))
                        load_moe(l, g, j)
                    for j in range(RING):
                        sp.wait_ge(used, g * PASS_BLOCKS + (base + PASS_BLOCKS + j - RING + 1))
                        load_moe(l, g + 1, j)
                for j in range(RING, PASS_BLOCKS):
                    sp.wait_ge(used, (NG - 1) * PASS_BLOCKS + base + j - RING + 1)
                    load_moe(l, NG - 1, j)

            for l in range(2):
                for j in range(RING):
                    owner = MOE0[l] + j - RING
                    if l == 0:
                        sp.wait_ge(mixer_used, owner + 1)
                    elif owner < POOL0:
                        sp.wait_ge(moe[0]["used"], blocks_more + (owner - MOE0[0] + 1))
                    else:
                        sp.wait_ge(mix_done, NT * (owner - POOL0 + 1))
                    load_moe(l, 0, j)
                stream_round(l, 0)
                sp.wait_ge(moe[l]["route_done"], 1)
                more = sp.value_load(npass_i[0:1, 2 * l + 1:2 * l + 2], min_val=0, max_val=NG)
                with sp.If(more > 0):
                    for j in range(RING):
                        sp.wait_ge(moe[l]["used"], ROUND + j - RING + 1)
                        load_moe(l, 0, j)
                    stream_round(l, ROUND)
                if l == 0:
                    blocks_more = more * PASS_BLOCKS
                    for g in range(NG):
                        sp.wait_ge(moe[0]["used"], blocks_more + (ROUND - RING + g + 1))
                        sp.dma_start(ring[:, (POOL0 + g) % RING, :].rearrange("p (k n) -> p k n", k=4),
                                     a["pool_w_o"][0, g].rearrange("(k p) n -> p k n", p=P)) \
                            .then_inc(pool_in[g], 16)
            sp.wait_ge(x_ready, 4)
            sp.dma_start(out[0].rearrange("(t p) d -> p t d", p=P), x_sb[:]).then_inc(x_stored, 16)
            sp.wait_ge(x_stored, 16)

        @block.gpsimd
        def _(pool):
            def root(i):
                pool.wait_ge(sq_done, NT * (i + 1))
                nc.gpsimd.tensor_scalar(meansq[:, i], sumsq[:, i], 1.0 / D, EPS, ALU.mult, ALU.add) \
                    .then_inc(ms_done, 1)
                pool.wait_ge(ms_done, i + 1)
                nc.gpsimd.tensor_tensor(rstd[:, i], meansq[:, i], minus_half[:, 0:NT], ALU.pow) \
                    .then_inc(rstd_done, 1)

            def head_root(n, dst, tmp, src, width):
                nc.gpsimd.tensor_scalar(tmp, src, 1.0 / HD, EPS, ALU.mult, ALU.add).then_inc(head_ms, 1)
                pool.wait_ge(head_ms, n + 1)
                nc.gpsimd.tensor_tensor(dst, tmp, minus_half[:, 0:width], ALU.pow).then_inc(head_rs, 1)

            pool.wait_ge(set_up, 1)
            root(0)
            pool.wait_ge(kvi_out, 2)
            head_root(0, ksq[:, 4:6], ksq[:, 2:4], ksq[:, 0:2], 2)
            for i in range(2):
                for t in range(NT):
                    pool.wait_ge(hsq_done, NT * i + t + 1)
                    heads = slice(4 * i, 4 * i + 4)
                    head_root(1 + NT * i + t, hrs[:, t, heads], hms[:, t, heads], hsq[:, t, heads], 4)
            pool.wait_ge(ln_step, 3)
            nc.gpsimd.tensor_tensor(rvar, rvar, minus_half[:], ALU.pow).then_inc(ln_pool, 1)
            root(1)
            root(2)
            root(3)

        @block.scalar
        def _(act):
            def copy(out, in_, scale=1.0):
                return nc.scalar.activation(out, in_, ACT.Copy, scale=scale)

            act.dma_start(const_sb[:], a["const"]).then_inc(const_in, 16)
            for dst, name in ((rel_sb, "rel_bias"), (one_hot, "one_hot")):
                act.dma_start(dst, a[name]).then_inc(rows_in, 16)
            row = lambda name, n: a[name][0].rearrange("(c p) -> c p", p=P)
            for at, src, n in ((V_CB, row("conv_b_e", CC), CC), (V_LG, row("conv_ln_g_e", CC), CC),
                               (V_LB, row("conv_ln_b_e", CC), CC), (V_QN, a["q_norm_e"], 1),
                               (V_KN, a["k_norm_e"], 1), (V_POOL, row("mix_norm_o", KC), KC)):
                act.dma_start(vec_rows[at:at + n, 0, :], src).then_inc(rows_in, 16)
            taps = a["conv_w_e"][0].rearrange("w (c p) -> (w c) p", p=P)
            for h in range(2):
                act.dma_start(vec_rows[0:CW_HALF, 1 + h, :], taps[h * CW_HALF:(h + 1) * CW_HALF, :]).then_inc(rows_in, 16)
            act.dma_start(norm_cols[:, 0, :], a["mix_norm_e"][0].rearrange("(p k) -> p k", k=KC)).then_inc(const_in, 16)
            for l in range(2):
                act.dma_start(norm_cols[:, 1 + l, :], a["ffn_norm"][l].rearrange("(p k) -> p k", k=KC)).then_inc(const_in, 16)
                act.dma_start(router_w[:, l, :, 0:NG], a["router_group_w"][l].rearrange("(p k) g -> p k g", k=KC)) \
                    .then_inc(const_in, 16)
                act.dma_start(router_w[:, l, :, NG:20], a["router_expert_w"][l].rearrange("(p k) g -> p k g", k=KC)) \
                    .then_inc(const_in, 16)
                act.dma_start(router_b[:, l, 0:NG], a["router_group_b"][l:l + 1, :].partition_broadcast(P)) \
                    .then_inc(const_in, 16)
                act.dma_start(router_b[:, l, NG:20], a["router_expert_b"][l:l + 1, :].partition_broadcast(P)) \
                    .then_inc(const_in, 16)

            def norm(i, permuted):
                if i:
                    act.wait_ge(x_ready, i)
                else:
                    act.wait_ge(x_loaded, 16)
                nc.scalar.activation(xn[:, D:2 * D], x_sb[:, 1, :], ACT.Square,
                                     accum_out=sumsq[:, i, 1:2]).then_inc(sq_done, 1)
                act.wait_ge(rstd_done, i + 1)
                dst = xn[:, D:2 * D]
                src = x_sb[:, 1, :]
                if permuted:
                    dst = dst.rearrange("p (k j) -> p k j", k=KC)
                    src = src.rearrange("p (j k) -> p k j", k=KC)
                act.wait_ge(sq_done, NT * (i + 1))
                copy(dst, src, rstd[:, i, 1:2]).then_inc(xn_done, 1)

            act.wait_ge(vec_done, 1)
            copy(vec_sb[:, 0:V_LG], ps[:, 0, 0:V_LG])
            copy(vec_sb[:, V_LG:V_QN], ps[:, 0, V_LG:V_QN], 0.5)
            copy(vec_sb[:, V_QN:V_ROWS], ps[:, 0, V_QN:V_ROWS])
            copy(cw_sb[:], ps[:, 0, 64:64 + CW_ROWS], 0.5).then_inc(vec_out, 1)
            act.wait_ge(vec_done, 2)
            copy(bias_row, ps[0:HEADS, 1, :]).then_inc(vec_out, 1)
            act.wait_ge(vec_out, 2)
            act.dma_start(bias_dram, bias_row).then_inc(bias_stored, 16)
            act.wait_ge(bias_stored, 16)
            act.dma_start(bias_up, bass.AP(tensor=bias_dram.tensor, offset=0,
                                           ap=[[1, P], [512, HEADS], [1, SEQ]])).then_inc(bias_loaded, 16)
            norm(0, True)

            def wait_job(name):
                wait_for_job(act, name)

            for i in range(2):
                wait_job(f"g{i}")
                if i:
                    act.wait_ge(u_done, 1)
                nc.scalar.activation(th_glu, ps[:, 4:8, 0:SEQ], ACT.Tanh, scale=0.5).then_inc(th_done, 1)
            wait_job("flip")
            copy(bias_sb.rearrange("p h s -> p (h s)"), ps[:, 0:4, :].rearrange("p b n -> p (b n)")).then_inc(bias_out, 1)
            wait_job("kvi")
            copy(v_sb, ps[:, 4:6, P:2 * P])
            for h in range(2):
                copy(ik2[:, :, h * ID:(h + 1) * ID], ps[:, 4:6, KVW:KVW + ID])
            copy(iw_sb, ps[:, 4:6, KVW + ID:KVW + IKW], IH ** -0.5 * ID ** -0.5).then_inc(kvi_out, 1)
            for t in range(NT):
                sq = nc.scalar.activation(il_relu[:, t, 0:P], ps[:, 4 + t, 0:P], ACT.Square, accum_out=ksq[:, t:t + 1])
            sq.then_inc(kvi_out, 1)
            wait_job("iq0")
            copy(iqT[:, 0:4, :], ps[:, 0:4, 0:SEQ]).then_inc(iq_out, 1)
            wait_job("kT")
            copy(kT, ps[:, 6, 0:SEQ], vec_sb[:, V_KN:V_KN + 1])
            copy(ikT, ps[:, 6, SEQ:2 * SEQ]).then_inc(kT_out, 1)
            wait_job("iq1")
            copy(iqT[:, 4:6, :], ps[:, 4:6, 0:SEQ])
            copy(iqT[:, 6, :], ps[:, 7, 0:SEQ])
            copy(iqT[:, 7, :], ps[:, 0, 0:SEQ]).then_inc(iq_out, 1)
            for i in range(12):
                wait_job(f"il{i}")
                if i >= 2:
                    act.wait_ge(score_step, heads_before[i - 1])
                nc.scalar.activation(il_relu[:, i % 2, :], ps[:, BANKS[f"il{i}"][0], :], ACT.Relu).then_inc(relu_done, 1)
            act.wait_ge(score_step, heads_before[12])
            for i in range(2):
                wait_job(f"q{i}")
                for t in range(NT):
                    if i:
                        act.wait_ge(hsq_done, t + 1)
                    nc.scalar.activation(qsq[:, t, :], ps[:, 2 * i + t, :], ACT.Square).then_inc(qsq_done, 1)
            for i in range(4):
                t, hq = i // 2, i % 2
                wait_job(f"qT{i}")
                copy(qT[:, 4 * hq:4 * hq + 4, t * P:(t + 1) * P], ps[:, 4 + i, :].rearrange("p (h s) -> p h s", h=4),
                     vec_sb[:, V_QN:V_QN + 1]).then_inc(qT_out, 1)

            act.wait_ge(ln_step, 2)
            nc.scalar.activation(vsq, conv, ACT.Square).then_inc(y_half, 1)
            act.wait_ge(ln_step, 4)
            for c in range(CC):
                last = nc.scalar.activation(conv[:, c, :], conv[:, c, :], ACT.Identity,
                                            scale=vec_sb[:, V_LG + c:V_LG + c + 1], bias=vec_sb[:, V_LB + c:V_LB + c + 1])
            last.then_inc(y_half, 1)
            act.wait_ge(y_half, 2)
            nc.scalar.activation(th_conv, conv, ACT.Tanh).then_inc(th_conv_done, 1)

            for t, lg in enumerate((logits0, bias_sb)):
                act.wait_ge(logit_step, 5 + 3 * t)
                for h in range(HEADS):
                    last = nc.scalar.activation(lg[:, h, :], lg[:, h, :], ACT.Exp, bias=smax[:, t, h:h + 1],
                                                accum_out=ssum[:, t, h:h + 1])
                last.then_inc(exp_done, 1)
            for i in range(6):
                wait_job(f"pT{i}")
                dst = pT0[:, i * 512:(i + 1) * 512] if i < 2 else pT1[:, (i - 2) // 2, (i % 2) * 512:(i % 2) * 512 + 512]
                copy(dst, ps[:, BANKS[f"pT{i}"][0], :]).then_inc(pT_out, 1)
            for i in range(4):
                t, hq = i // 2, i % 2
                wait_job(f"oT{i}")
                copy(attnT[:, 4 * hq:4 * hq + 4, t * P:(t + 1) * P],
                     ps[:, BANKS[f"oT{i}"][0], :].rearrange("p (h s) -> p h s", h=4)).then_inc(oT_out, 1)
            act.wait_ge(x_ready, 1)
            act.dma_start(scale_bc, a["pool_scale_o"][0:1, :].partition_broadcast(P)).then_inc(scale_in, 16)
            act.dma_start(band, a["band"]).then_inc(scale_in, 16)

            def moe_act(l):
                m = moe[l]
                norm(1 if l == 0 else 3, True)
                act.wait_ge(m["exp_in"], 1)
                nc.scalar.activation(ex_g, oneh, ACT.Exp).then_inc(m["exp_out"], 1)
                act.wait_ge(m["exp_in"], 2)
                nc.scalar.activation(ex_e, el, ACT.Exp).then_inc(m["exp_out"], 1)
                act.wait_ge(m["route_done"], 1)
                n = act.value_load(npass_i[0:1, 2 * l:2 * l + 1], min_val=NG, max_val=2 * NG)
                with act.Fori(0, n) as p:
                    act.wait_ge(m["misc_done"], p + 1)
                    copy(pickT, ps[:, BANK_T, 0:NT * P].rearrange("p (t s) -> p t s", t=NT))
                    copy(comb_slot, ps[:, BANK_T, NT * P:NT * P + EPG]).then_inc(m["misc_out"], 1)

                    def turn(e):
                        act.wait_ge(m["actT_done"], p * EPG + (e + 1))
                        copy(actT, ps[:, BANK_T, :].rearrange("p (k s) -> p k s", k=FC)).then_inc(m["actT_out"], 1)

                    for e in range(EPG):
                        unit_done(act, l, p, e, "g")
                        nc.scalar.activation(th_gate[:, e % 2, :], ps[:, e % 2, :], ACT.Tanh, scale=0.5) \
                            .then_inc(m["th_gate_done"], 1)
                        if e:
                            turn(e - 1)
                    turn(EPG - 1)
                    unit_done(act, l, p, EPG - 1, "d")
                    for b in range(4):
                        copy(y_sb[:, b * 512:(b + 1) * 512], ps[:, BANK_Y + b, :]).then_inc(m["y_out"], 1)

            moe_act(0)
            norm(2, False)
            moe_act(1)

        @block.vector
        def _(dve):
            tt = nc.vector.tensor_tensor
            ts = nc.vector.tensor_scalar
            stt = nc.vector.scalar_tensor_tensor

            nc.vector.memset(minus_half[:], -0.5)
            nc.vector.memset(uT[:, :, 0:PAD], 0.0)
            nc.vector.memset(ones[:], 1.0).then_inc(set_up, 1)

            ticks = [0]

            def tick_off():
                ticks[0] += 1
                return nc.vector.memset(tick[:, ticks[0] - 1:ticks[0]], 0.0)

            def norm(i, permuted):
                if i:
                    dve.wait_ge(x_ready, i)
                else:
                    dve.wait_ge(x_loaded, 16)
                stt(out=xn[:, 0:D], in0=x_sb[:, 0, :], scalar=1.0, in1=x_sb[:, 0, :], op0=ALU.mult, op1=ALU.mult,
                    accum_out=sumsq[:, i, 0:1]).then_inc(sq_done, 1)
                dve.wait_ge(rstd_done, i + 1)
                dst = xn[:, 0:D]
                src = x_sb[:, 0, :]
                if permuted:
                    dst = dst.rearrange("p (k j) -> p k j", k=KC)
                    src = src.rearrange("p (j k) -> p k j", k=KC)
                ts(dst, src, rstd[:, i, 0:1], None, ALU.mult).then_inc(xn_done, 1)

            def normed_channels(n, col):
                for q in range(8):
                    t, kq = q // 4, q % 4
                    dve.wait_ge(xT_done, 8 * n + q + 1)
                    w = norm_cols[:, col, 4 * kq:4 * kq + 4].unsqueeze(2).to_broadcast([P, 4, P])
                    tt(hT[:, 4 * kq:4 * kq + 4, t * P:(t + 1) * P], ps[:, q, :].rearrange("p (k s) -> p k s", k=4),
                       w, ALU.mult).then_inc(xT_out, 1)

            def wait_job(name):
                wait_for_job(dve, name)

            norm(0, True)
            dve.wait_ge(const_in, 16 * 12)
            normed_channels(0, 0)

            for i in range(2):
                wait_job(f"a{i}")
                dve.wait_ge(th_done, i + 1)
                stt(out=uT[:, 4 * i:4 * i + 4, PAD:PAD + SEQ], in0=th_glu, scalar=1.0, in1=ps[:, 0:4, 0:SEQ],
                    op0=ALU.add, op1=ALU.mult).then_inc(u_done, 1)
            dve.wait_ge(u_done, 2)
            dve.wait_ge(vec_out, 1)

            conv_ops = [(4 * half + c, w) for half in range(2) for w in range(TAPS) for c in range(4)]

            def convolve(first, last):
                for n in range(first, last):
                    c, w = conv_ops[n]
                    tap = cw_sb[:, w * CC + c:w * CC + c + 1]
                    if w == 0:
                        ts(conv[:, c, :], uT[:, c, 0:SEQ], tap, vec_sb[:, V_CB + c:V_CB + c + 1], ALU.mult, ALU.add) \
                            .then_inc(conv_step, 1)
                    else:
                        dve.wait_ge(conv_step, n - 3)
                        stt(out=conv[:, c, :], in0=uT[:, c, w:w + SEQ], scalar=tap, in1=conv[:, c, :],
                            op0=ALU.mult, op1=ALU.add).then_inc(conv_step, 1)

            convolve(0, 124)
            wait_job("kvi")
            dve.wait_ge(kvi_out, 2)
            dve.wait_ge(head_rs, 1)
            for t in range(NT):
                last = ts(k_sb[:, t, :], ps[:, 4 + t, 0:P], ksq[:, 4 + t:5 + t], None, ALU.mult)
                if t == 0:
                    last.then_inc(k_scaled, 1)
            last.then_inc(k_scaled, 1)
            convolve(124, 180)

            n = 0
            for i in range(12):
                t, heads = indexer_heads(i)
                S = (t + 1) * P
                dve.wait_ge(relu_done, i + 1)
                for m, h in enumerate(heads):
                    start = n in (0, IH)
                    if not start:
                        dve.wait_ge(score_step, n)
                    last = stt(out=score[:, t, 0:S], in0=il_relu[:, i % 2, m * S:(m + 1) * S], scalar=iw_sb[:, t, h:h + 1],
                               in1=causal[:, SEQ - S:SEQ] if start else score[:, t, 0:S], op0=ALU.mult, op1=ALU.add)
                    last.then_inc(score_step, 1)
                    n += 1

            dve.wait_ge(score_step, n)
            n = 0
            for r in range(TOPK // 8):
                for t in range(NT):
                    S = (t + 1) * P
                    src = picked if r else score
                    if r:
                        dve.wait_ge(topk_step, n - 2)
                    nc.vector.max(top8[:, t, :], src[:, t, 0:S]).then_inc(topk_step, 1)
                    n += 1
                    dve.wait_ge(topk_step, n)
                    nc.vector.match_replace(picked[:, t, 0:S], top8[:, t, :], src[:, t, 0:S], TAKEN).then_inc(topk_step, 1)
                    n += 1
            dve.wait_ge(topk_step, n)
            for t in range(NT):
                S = (t + 1) * P
                ts(picked[:, t, 0:S], picked[:, t, 0:S], TAKEN, -NEG, ALU.is_equal, ALU.mult).then_inc(topk_step, 1)
            dve.wait_ge(topk_step, n + 2)
            for t in range(NT):
                S = (t + 1) * P
                stt(out=picked[:, t, 0:S], in0=picked[:, t, 0:S], scalar=NEG, in1=causal[:, SEQ - S:SEQ],
                    op0=ALU.add, op1=ALU.add).then_inc(topk_step, 1)
            dve.wait_ge(topk_step, n + 4)
            dve.wait_ge(bias_out, 1)
            for t, (dst, src) in enumerate(((logits0, bias_sb[:, :, P:SEQ]), (bias_sb, bias_sb))):
                S = (t + 1) * P
                tt(dst, src, picked[:, t, 0:S].unsqueeze(1).to_broadcast([P, HEADS, S]), ALU.add).then_inc(logit_step, 1)
                dve.wait_ge(logit_step, t + 1)

            convolve(180, 248)
            for i in range(2):
                for t in range(NT):
                    dve.wait_ge(qsq_done, NT * i + t + 1)
                    nc.vector.tensor_reduce(hsq[:, t, 4 * i:4 * i + 4], qsq[:, t, :].rearrange("p (h d) -> p h d", h=4),
                                            X, ALU.add).then_inc(hsq_done, 1)
                for t in range(NT):
                    dve.wait_ge(head_rs, 2 + NT * i + t)
                    r = hrs[:, t, 4 * i:4 * i + 4].unsqueeze(2).to_broadcast([P, 4, HD])
                    tt(qn[:, t, 512 * i:512 * i + 512].rearrange("p (h d) -> p h d", h=4),
                       ps[:, 2 * i + t, :].rearrange("p (h d) -> p h d", h=4), r, ALU.mult).then_inc(qn_done, 1)

            dve.wait_ge(conv_step, 248)
            wait_job("mean")
            ts(mean_sb, ps[:, 6, 0:SEQ], 1.0 / CCH, None, ALU.mult).then_inc(ln_step, 1)
            dve.wait_ge(ln_step, 1)
            tt(conv, conv, mean_sb.unsqueeze(1).to_broadcast([P, CC, SEQ]), ALU.subtract).then_inc(ln_step, 1)
            wait_job("var")
            ts(rvar, ps[:, 7, 0:SEQ], 1.0 / CCH, EPS, ALU.mult, ALU.add).then_inc(ln_step, 1)
            dve.wait_ge(ln_pool, 1)
            tt(conv, conv, rvar.unsqueeze(1).to_broadcast([P, CC, SEQ]), ALU.mult).then_inc(ln_step, 1)

            flat0 = logits0.rearrange("p h s -> p (h s)")
            flat1 = bias_sb.rearrange("p h s -> p (h s)")
            dve.wait_ge(logit_step, 2)
            for t, (flat, lg, banks) in enumerate(((flat0, logits0, (0, 2)), (flat1, bias_sb, (2, 6)))):
                wait_job(f"lg{t}")
                src = ps[:, banks[0]:banks[1], :].rearrange("p b n -> p (b n)")
                stt(out=flat, in0=src, scalar=HD ** -0.5, in1=flat, op0=ALU.mult, op1=ALU.add).then_inc(logit_step, 1)
                dve.wait_ge(logit_step, 3 + 3 * t)
                nc.vector.tensor_reduce(hms[:, t, :], lg, X, ALU.max).then_inc(logit_step, 1)
                dve.wait_ge(logit_step, 4 + 3 * t)
                ts(smax[:, t, :], hms[:, t, :], -1.0, None, ALU.mult).then_inc(logit_step, 1)

            dve.wait_ge(th_conv_done, 1)
            stt(out=conv, in0=th_conv, scalar=1.0, in1=conv, op0=ALU.add, op1=ALU.mult).then_inc(conv_done, 1)

            def add_x(n, t, bank):
                cols = x_sb[:, t, n * 512:(n + 1) * 512]
                tt(cols, ps[:, bank, :], cols, ALU.add).then_inc(x_added, 1)

            def normalise(t, lg):
                dve.wait_ge(exp_done, t + 1)
                nc.vector.reciprocal(srec[:, t, :], ssum[:, t, :]).then_inc(prob_step, 1)
                dve.wait_ge(prob_step, t + 1)
                tt(lg, lg, srec[:, t, :].unsqueeze(2).to_broadcast([P, HEADS, (t + 1) * P]), ALU.mult).then_inc(prob_done, 1)

            normalise(0, logits0)
            normalise(1, bias_sb)
            for n in range(4):
                wait_job(f"wc{n}")
                for t, bank in enumerate(BANKS[f"wc{n}"]):
                    add_x(n, t, bank)
            for n in range(4):
                wait_job(f"wa{n}")
                if n == 0:
                    dve.wait_ge(x_added, 8)
                for t, bank in enumerate(BANKS[f"wa{n}"]):
                    add_x(n, t, bank)
            dve.wait_ge(x_added, 16)
            tick_off().then_inc(x_ready, 1)

            def moe_dve(l):
                m = moe[l]
                norm(1 if l == 0 else 3, True)
                normed_channels(1 + l, 1 + l)
                steps = [0]

                def chain(ins):
                    steps[0] += 1
                    ins.then_inc(m["route_step"], 1)
                    dve.wait_ge(m["route_step"], steps[0])

                def first_max(dst, src, val):
                    chain(nc.vector.tensor_reduce(val, src, X, ALU.max))
                    chain(tt(t4a, src, val.to_broadcast([P, NT, 4]), ALU.is_equal))
                    chain(tt(t4a, t4a, prio.unsqueeze(1).to_broadcast([P, NT, 4]), ALU.mult))
                    chain(nc.vector.tensor_reduce(gmax, t4a, X, ALU.max))
                    chain(tt(dst, t4a, gmax.to_broadcast([P, NT, 4]), ALU.is_equal))

                col = lambda i: stat[:, i, :].unsqueeze(2)
                dve.wait_ge(m["router_done"], 1)
                src = ps[:, 2, 0:64].rearrange("p (t c) -> p t c", t=NT)[:, :, 0:20]
                chain(tt(lgt, src, router_b[:, l, :].unsqueeze(1).to_broadcast([P, NT, 20]), ALU.add))
                glog = lgt[:, :, 0:NG]
                chain(nc.vector.tensor_reduce(col(0), glog, X, ALU.max))
                chain(tt(oneh, glog, col(0).to_broadcast([P, NT, NG]), ALU.subtract))
                tick_off().then_inc(m["exp_in"], 1)
                dve.wait_ge(m["exp_out"], 1)
                chain(nc.vector.tensor_reduce(col(1), ex_g, X, ALU.add))
                chain(nc.vector.reciprocal(col(2), col(1)))
                first_max(oneh, glog, col(0))
                tick_off().then_inc(m["rank_in"], 1)
                p4 = prod.rearrange("p t (g e) -> p t g e", g=NG)
                chain(tt(p4, lgt[:, :, NG:20].rearrange("p t (g e) -> p t g e", g=NG),
                         oneh.unsqueeze(3).to_broadcast([P, NT, NG, EPG]), ALU.mult))
                chain(nc.vector.tensor_reduce(el, prod.rearrange("p t (g e) -> p t e g", g=NG), X, ALU.add))
                first_max(sel1, el, col(3))
                chain(stt(out=t4b, in0=sel1, scalar=NEG, in1=el, op0=ALU.mult, op1=ALU.add))
                first_max(sel2, t4b, col(4))
                chain(tt(el, el, col(3).to_broadcast([P, NT, EPG]), ALU.subtract))
                tick_off().then_inc(m["exp_in"], 1)
                chain(tt(sel1, sel1, sel2, ALU.add))
                dve.wait_ge(m["exp_out"], 2)
                chain(tt(wgt, ex_e, sel1, ALU.mult))
                chain(nc.vector.tensor_reduce(col(5), wgt, X, ALU.add))
                chain(nc.vector.reciprocal(col(6), col(5)))
                chain(tt(col(6), col(6), col(2), ALU.mult))
                chain(tt(wgt, wgt, col(6).to_broadcast([P, NT, EPG]), ALU.mult))
                chain(ts(wgt, wgt, 0.5, None, ALU.mult))
                c4 = comb[:, :, 0:NE].rearrange("p t (g e) -> p t g e", g=NG)
                chain(tt(c4, wgt.unsqueeze(2).to_broadcast([P, NT, NG, EPG]),
                         oneh.unsqueeze(3).to_broadcast([P, NT, NG, EPG]), ALU.mult))
                nc.vector.tensor_copy(comb[:, :, NE:2 * NE], comb[:, :, 0:NE])
                nc.vector.memset(comb[:, :, 2 * NE:], 0.0)
                dve.wait_ge(m["rank_done"], 1)
                rank = ps[:, BANK_T, 0:16].rearrange("p (t c) -> p t c", t=NT)[:, :, 0:NG]
                chain(stt(out=rank_in[:, :, 0:NG], in0=rank, scalar=1.0, in1=oneh, op0=ALU.add, op1=ALU.mult))
                chain(ts(rank_in[:, :, NG:2 * NG], rank_in[:, :, 0:NG], -1.0 - P, None, ALU.add))
                chain(ts(rank_in[:, :, 0:NG], rank_in[:, :, 0:NG], -1.0, None, ALU.add))
                nc.vector.memset(rank_in[:, :, 2 * NG:], -1.0)
                chain(nc.vector.tensor_reduce(cnt[:, 0:1], ps[:, BANK_T, 16:16 + NG], X, ALU.max))
                chain(ts(cnt[:, 1:2], cnt[:, 0:1], float(P), float(NG), ALU.is_gt, ALU.mult))
                chain(nc.vector.tensor_copy(npass_i[:, 2 * l + 1:2 * l + 2], cnt[:, 1:2]))
                chain(ts(cnt[:, 2:3], cnt[:, 1:2], float(NG), None, ALU.add))
                chain(nc.vector.tensor_copy(npass_i[:, 2 * l:2 * l + 1], cnt[:, 2:3]))
                tick_off().then_inc(m["x_moved"], 1)
                tick_off().then_inc(m["route_done"], 1)

                def pick_tokens(p):
                    nc.vector.tensor_copy(comb_now, comb[:, :, bass.ds(p * EPG, EPG)])
                    for t in range(NT):
                        last = ts(pick[:, t, :], slot_no, rank_in[:, t, bass.ds(p, 1)], None, ALU.is_equal)
                    last.then_inc(m["pick_ready"], 1)

                def normed_slots(p):
                    for q in range(4):
                        dve.wait_ge(m["gathered"], p * 4 + (q + 1))
                        w = norm_cols[:, 1 + l, 4 * q:4 * q + 4].unsqueeze(2).to_broadcast([P, 4, P])
                        tt(hgT[:, 4 * q:4 * q + 4, :], ps[:, GATHER_BANK[q], :].rearrange("p (k s) -> p k s", k=4),
                           w, ALU.mult).then_inc(m["gather_out"], 1)

                pick_tokens(0)
                normed_slots(0)
                n = dve.value_load(npass_i[0:1, 2 * l:2 * l + 1], min_val=NG, max_val=2 * NG)
                with dve.Fori(0, n) as p:
                    for e in range(EPG):
                        dve.wait_ge(m["th_gate_done"], p * EPG + (e + 1))
                        stt(out=gated[:, e % 2, :], in0=th_gate[:, e % 2, :], scalar=1.0, in1=ps[:, e % 2, :],
                            op0=ALU.add, op1=ALU.mult).then_inc(m["gated_done"], 1)
                        dve.wait_ge(m["gated_done"], p * EPG + (e + 1))
                        dve.wait_ge(m["misc_out"], p + 1)
                        unit_done(dve, l, p, e, "u")
                        by_j = lambda t: t.rearrange("p (j k) -> p j k", k=FC)
                        stt(out=act.rearrange("p (k j) -> p j k", k=FC), in0=by_j(gated[:, e % 2, :]), scalar=comb_slot[:, e:e + 1],
                            in1=by_j(ps[:, 2, :]), op0=ALU.mult, op1=ALU.mult).then_inc(m["act_done"], 1)
                        if e == 0:
                            dve.wait_ge(m["misc_done"], p + 1)
                            pick_tokens(p + 1)
                    normed_slots(p + 1)
                    for i in range(8):
                        t, b = i // 4, i % 4
                        dve.wait_ge(m["scattered"], p * 8 + (i + 1))
                        cols = x_sb[:, t, b * 512:(b + 1) * 512]
                        tt(cols, ps[:, BANK_Y + b, :], cols, ALU.add).then_inc(m["x_moved"], 1)
                dve.wait_ge(m["x_moved"], n * 8 + 1)
                tick_off().then_inc(x_ready, 1)

            moe_dve(0)

            norm(2, False)
            dve.wait_ge(scale_in, 32)
            for i in range(8):
                dve.wait_ge(dT_done, i + 1)
                w = vec_sb[:, V_POOL + 2 * i:V_POOL + 2 * i + 2].unsqueeze(2).to_broadcast([P, 2, SEQ])
                tt(hT[:, 2 * i:2 * i + 2, :], ps[:, i, :].rearrange("p (c s) -> p c s", c=2), w, ALU.mult).then_inc(dT_out, 1)
            for i in range(8):
                g, t = i // 2, i % 2
                dve.wait_ge(mix_done, i + 1)
                if i >= 2:
                    dve.wait_ge(mix_step, 2 * i - 2)
                tt(mixed[:, i % 2, :], ps[:, i, :], scale_bc[:, g * 512:(g + 1) * 512], ALU.mult).then_inc(mix_step, 1)
                dve.wait_ge(mix_step, 2 * i + 1)
                cols = x_sb[:, t, g * 512:(g + 1) * 512]
                tt(cols, mixed[:, i % 2, :], cols, ALU.add).then_inc(mix_step, 1)
            dve.wait_ge(mix_step, 16)
            tick_off().then_inc(x_ready, 1)

            moe_dve(1)

        @block.tensor
        def _(pe):
            mm = nc.tensor.matmul

            def turn(dst, src, n=P):
                return nc.tensor.transpose(dst, src, ident[0:n, 0:n])

            pe.wait_ge(const_in, 16 * 12)
            pe.wait_ge(rows_in, 16 * 10)
            pe.wait_ge(set_up, 1)
            turn(ps[:, 0, 0:V_ROWS], vec_rows[0:V_ROWS, 0, :], V_ROWS)
            for h in range(2):
                last = turn(ps[:, 0, 64 + h * CW_HALF:64 + (h + 1) * CW_HALF], vec_rows[0:CW_HALF, 1 + h, :], CW_HALF)
            last.then_inc(vec_done, 1)
            mm(ps[0:HEADS, 1, :], rel_sb, one_hot, start=True, stop=True).then_inc(vec_done, 1)
            pe.wait_ge(vec_out, 2)

            def turn_x(i, n):
                pe.wait_ge(xn_done, NT * (i + 1))
                for q in range(8):
                    t, kq = q // 4, q % 4
                    for k in range(4 * kq, 4 * kq + 4):
                        last = turn(ps[:, q, (k % 4) * P:(k % 4 + 1) * P], xn[:, t * D + k * P:t * D + (k + 1) * P])
                    last.then_inc(xT_done, 1)
                pe.wait_ge(xT_out, 8 * (n + 1))

            def start_job(name):
                for b in BANKS[name]:
                    if (owner := owner_before(name, b)) is not None:
                        signal, count = emptied(owner)
                        pe.wait_ge(signal, count)

            stream = [0]

            def next_block():
                b = stream[0]
                stream[0] += 1
                loads = sum(2 if c in kvi_at else 1 for c in range(b % RING, b + 1, RING))
                pe.wait_ge(mixer_in[b % RING], 16 * loads)
                return ring[:, b % RING, :]

            def channels_job(name):
                start_job(name)
                for kq in range(4):
                    w = next_block().rearrange("p (k n) -> p k n", k=4)
                    for k in range(4):
                        for c, b in enumerate(BANKS[name]):
                            last = mm(ps[:, b, 0:SEQ], w[:, k, c * P:(c + 1) * P], hT[:, 4 * kq + k, :],
                                      start=(kq == 0 and k == 0), stop=(kq == 3 and k == 3))
                    last.then_inc(mixer_used, 1)

            def tokens_job(name):
                start_job(name)
                for kq in range(4):
                    w = next_block().rearrange("p (k n) -> p k n", k=4)
                    for k in range(4):
                        for t, b in enumerate(BANKS[name]):
                            last = mm(ps[:, b, :], hT[:, 4 * kq + k, t * P:(t + 1) * P], w[:, k, :],
                                      start=(kq == 0 and k == 0), stop=(kq == 3 and k == 3))
                    last.then_inc(mixer_used, 1)

            def kvi_job():
                start_job("kvi")
                for kq in range(4):
                    slot = next_block()
                    kv = slot[:, 0:4 * KVW].rearrange("p (k n) -> p k n", k=4)
                    ki = slot[:, 4 * KVW:4 * (KVW + IKW)].rearrange("p (k n) -> p k n", k=4)
                    for k in range(4):
                        for t in range(NT):
                            first, end = kq == 0 and k == 0, kq == 3 and k == 3
                            h = hT[:, 4 * kq + k, t * P:(t + 1) * P]
                            mm(ps[:, 4 + t, 0:KVW], h, kv[:, k, :], start=first, stop=end, skip_group_check=True)
                            last = mm(ps[:, 4 + t, KVW:KVW + IKW], h, ki[:, k, :], start=False, stop=end,
                                      skip_group_check=True)
                    last.then_inc(mixer_used, 1)

            def out_job(name, cat):
                start_job(name)
                for q in range(2):
                    w = next_block().rearrange("p (k n) -> p k n", k=4)
                    for k in range(4):
                        for t, b in enumerate(BANKS[name]):
                            last = mm(ps[:, b, :], cat(4 * q + k, t), w[:, k, :],
                                      start=(q == 0 and k == 0), stop=(q == 1 and k == 3))
                    last.then_inc(mixer_used, 1)

            turn_x(0, 0)
            for i in range(2):
                channels_job(f"a{i}")
                channels_job(f"g{i}")
            start_job("flip")
            pe.wait_ge(bias_loaded, 16)
            for c in range(4):
                last = mm(ps[:, c, :], upside, bias_up[:, 2 * c:2 * c + 2, :].rearrange("p h s -> p (h s)"),
                          start=True, stop=True)
            last.then_inc(job_done, 1)
            kvi_job()
            channels_job("iq0")
            start_job("kT")
            pe.wait_ge(k_scaled, 2)
            for t in range(NT):
                turn(ps[:, 6, t * P:(t + 1) * P], k_sb[:, t, :])
            for t in range(NT):
                last = turn(ps[:, 6, SEQ + t * P:SEQ + (t + 1) * P], ik2[:, t, :])
            last.then_inc(job_done, 1)
            channels_job("iq1")
            pe.wait_ge(iq_out, 2)
            pe.wait_ge(kT_out, 1)
            for i in range(12):
                start_job(f"il{i}")
                t, heads = indexer_heads(i)
                S = (t + 1) * P
                for m, h in enumerate(heads):
                    rows = slice((h % 2) * ID, (h % 2 + 1) * ID)
                    last = mm(ps[:, BANKS[f"il{i}"][0], m * S:(m + 1) * S], iqT[rows, h // 2, t * P:(t + 1) * P],
                              ikT[rows, 0:S], start=True, stop=True)
                last.then_inc(job_done, 1)
            tokens_job("q0")
            tokens_job("q1")
            for i in range(4):
                start_job(f"qT{i}")
                t, hq = i // 2, i % 2
                pe.wait_ge(qn_done, 2 * hq + t + 1)
                for h in range(4):
                    last = turn(ps[:, 4 + i, h * P:(h + 1) * P], qn[:, t, (4 * hq + h) * HD:(4 * hq + h + 1) * HD])
                last.then_inc(job_done, 1)
            for t in range(NT):
                start_job(f"lg{t}")
                S = (t + 1) * P
                per = 512 // S
                pe.wait_ge(qT_out, 2 * t + 2)
                for h in range(HEADS):
                    last = mm(ps[:, BANKS[f"lg{t}"][h // per], (h % per) * S:(h % per + 1) * S],
                              qT[:, h, t * P:(t + 1) * P], kT[:, 0:S], start=True, stop=True)
                last.then_inc(job_done, 1)
            for name, src, signal, count in (("mean", conv, conv_step, 248), ("var", vsq, y_half, 1)):
                start_job(name)
                pe.wait_ge(signal, count)
                for c in range(CC):
                    last = mm(ps[:, BANKS[name][0], 0:SEQ], ones[:], src[:, c, :], start=(c == 0), stop=(c == CC - 1))
                last.then_inc(job_done, 1)
            pe.wait_ge(conv_done, 1)
            for n in range(4):
                out_job(f"wc{n}", lambda c, t: conv[:, c, t * P:(t + 1) * P])
            for i in range(6):
                start_job(f"pT{i}")
                t, st, hq = (0, 0, i) if i < 2 else (1, (i - 2) // 2, i % 2)
                pe.wait_ge(prob_done, t + 1)
                lg = (logits0, bias_sb)[t]
                for h in range(4):
                    last = turn(ps[:, BANKS[f"pT{i}"][0], h * P:(h + 1) * P], lg[:, 4 * hq + h, st * P:(st + 1) * P])
                last.then_inc(job_done, 1)
            for i in range(4):
                start_job(f"oT{i}")
                t, hq = i // 2, i % 2
                pe.wait_ge(pT_out, 2 + 4 * t)
                for st in range(t + 1):
                    probs = pT1[:, st, hq * 512:(hq + 1) * 512] if t else pT0[:, hq * 512:(hq + 1) * 512]
                    last = mm(ps[:, BANKS[f"oT{i}"][0], :], v_sb[:, st, :], probs, start=(st == 0), stop=(st == t))
                last.then_inc(job_done, 1)
            pe.wait_ge(oT_out, 4)
            for n in range(4):
                out_job(f"wa{n}", lambda c, t: attnT[:, c, t * P:(t + 1) * P])

            def moe_pe(l):
                m = moe[l]
                turn_x(1 if l == 0 else 3, 1 + l)
                for t in range(NT):
                    for k in range(KC):
                        last = mm(ps[:, 2, 32 * t:32 * t + 20], hT[:, k, t * P:(t + 1) * P], router_w[:, l, k, :],
                                  start=(k == 0), stop=(k == KC - 1))
                last.then_inc(m["router_done"], 1)
                pe.wait_ge(m["rank_in"], 1)
                mm(ps[:, BANK_T, 0:NG], before, oneh[:, 0, :], start=True, stop=True)
                mm(ps[:, BANK_T, 8:8 + NG], ones[:], oneh[:, 0, :], start=True, stop=False)
                mm(ps[:, BANK_T, 8:8 + NG], before, oneh[:, 1, :], start=False, stop=True)
                mm(ps[:, BANK_T, 16:16 + NG], ones[:], oneh[:, 0, :], start=True, stop=False)
                mm(ps[:, BANK_T, 16:16 + NG], ones[:], oneh[:, 1, :], start=False, stop=True).then_inc(m["rank_done"], 1)

                def gather(p):
                    pe.wait_ge(m["pick_ready"], p + 1)
                    for q in range(4):
                        if q >= 2:
                            pe.wait_ge(m["gather_out"], p * 4 + (q - 1))
                        for k in range(4 * q, 4 * q + 4):
                            for t in range(NT):
                                last = mm(ps[:, GATHER_BANK[q], (k % 4) * P:(k % 4 + 1) * P],
                                          xn[:, t * D + k * P:t * D + (k + 1) * P], pick[:, t, :],
                                          start=(t == 0), stop=(t == NT - 1))
                        last.then_inc(m["gathered"], 1)

                pe.wait_ge(m["route_done"], 1)
                gather(0)
                n = pe.value_load(npass_i[0:1, 2 * l:2 * l + 1], min_val=NG, max_val=2 * NG)
                with pe.Fori(0, n) as p:
                    block_no = [0]

                    def weights():
                        j = block_no[0]
                        block_no[0] += 1
                        pe.wait_ge(m["in"][moe_slot(l, j)], p * (16 * PASS_BLOCKS // RING) + 16 * (j // RING + 1))
                        return ring[:, moe_slot(l, j), :]

                    def project(bank):
                        for kq in range(4):
                            w = weights().rearrange("p (k n) -> p k n", k=4)
                            for k in range(4):
                                last = mm(ps[:, bank, :], hgT[:, 4 * kq + k, :], w[:, k, :],
                                          start=(kq == 0 and k == 0), stop=(kq == 3 and k == 3))
                            last.then_inc(m["used"], 1)

                    def turn_act(e):
                        pe.wait_ge(m["act_done"], p * EPG + (e + 1))
                        if e == 0:
                            pe.wait_ge(m["misc_out"], p + 1)
                        if e == EPG - 1:
                            pe.wait_ge(m["gather_out"], p * 4 + 8)
                        for k in range(FC):
                            last = turn(ps[:, BANK_T, k * P:(k + 1) * P], act[:, k * P:(k + 1) * P])
                        last.then_inc(m["actT_done"], 1)

                    def down(e):
                        pe.wait_ge(m["actT_out"], p * EPG + (e + 1))
                        if e == 0:
                            pe.wait_ge(m["x_moved"], p * 8 + 1)
                        for k in range(FC):
                            w = weights()
                            for b in range(4):
                                last = mm(ps[:, BANK_Y + b, :], actT[:, k, :], w[:, b * 512:(b + 1) * 512],
                                          start=(e == 0 and k == 0), stop=(e == EPG - 1 and k == FC - 1))
                            last.then_inc(m["used"], 1)

                    pe.wait_ge(m["gather_out"], p * 4 + 4)
                    for t in range(NT):
                        turn(ps[:, BANK_T, t * P:(t + 1) * P], pick[:, t, :])
                    for t in range(NT):
                        last = mm(ps[:, BANK_T, SEQ:SEQ + EPG], pick[:, t, :], comb_now[:, t, :],
                                  start=(t == 0), stop=(t == NT - 1))
                    last.then_inc(m["misc_done"], 1)
                    for e, kind in UNITS:
                        if kind == "g":
                            project(e % 2)
                        elif kind == "u":
                            project(BANK_U)
                            if e == EPG - 1:
                                gather(p + 1)
                        else:
                            turn_act(e)
                            down(e)
                    for i in range(8):
                        t, b = i // 4, i % 4
                        if t == 0:
                            pe.wait_ge(m["y_out"], p * 4 + (b + 1))
                        else:
                            pe.wait_ge(m["x_moved"], p * 8 + (b + 2))
                        mm(ps[:, BANK_Y + b, :], pickT[:, t, :], y_sb[:, b * 512:(b + 1) * 512],
                           start=True, stop=True).then_inc(m["scattered"], 1)

            moe_pe(0)

            pe.wait_ge(xn_done, NT * 3)
            pe.wait_ge(scale_in, 32)
            for c in range(KC):
                bank, off, g = c // 2, (c % 2) * SEQ, c // 4
                mm(ps[:, bank, off:off + SEQ], xn[:, c * P:(c + 1) * P], band[:, 0, g * SEQ:(g + 1) * SEQ],
                   start=True, stop=False)
                last = mm(ps[:, bank, off + P:off + SEQ], xn[:, D + c * P:D + (c + 1) * P],
                          band[:, 1, g * SEQ + P:(g + 1) * SEQ], start=False, stop=True)
                if c % 2:
                    last.then_inc(dT_done, 1)
            for g in range(NG):
                pe.wait_ge(pool_in[g], 16)
                w = ring[:, (POOL0 + g) % RING, :].rearrange("p (k n) -> p k n", k=4)
                pe.wait_ge(dT_out, min(8, 2 * g + 2))
                for t in range(NT):
                    for k in range(4):
                        last = mm(ps[:, 2 * g + t, :], hT[:, 4 * g + k, t * P:(t + 1) * P], w[:, k, :],
                                  start=(k == 0), stop=(k == 3))
                    last.then_inc(mix_done, 1)

            moe_pe(1)


def shape_constants():
    i = np.arange(P)
    before = (i[:, None] < i[None, :]).astype(np.float32)
    slots = np.broadcast_to(i.astype(np.float32), (P, P))
    s = np.arange(SEQ)
    causal = np.where(s[None, :] - P <= i[:, None], 0.0, NEG).astype(np.float32)
    prio = np.broadcast_to(np.array([4, 3, 2, 1, 0, 0, 0, 0], np.float32), (P, 8))
    const = np.concatenate([np.eye(P, dtype=np.float32), before, slots, causal, prio, np.eye(P, dtype=np.float32)[::-1]], axis=1)
    dist = np.maximum(255 - np.arange(512), 0)
    exact = BUCKETS // 2
    large = exact + (np.log(np.maximum(dist, 1).astype(np.float32) / exact) / np.float32(np.log(128 / exact))
                     * (BUCKETS - exact)).astype(np.int32)
    bucket = np.where(dist < exact, dist, np.minimum(large, BUCKETS - 1))
    one_hot = (np.arange(BUCKETS)[:, None] == bucket[None, :]).astype(np.float32)
    t = np.arange(SEQ)
    band = np.zeros((SEQ, NG, SEQ), np.float32)
    for g, w in enumerate(WINDOWS):
        d = t[None, :] - t[:, None]
        band[:, g] = np.where((d >= 0) & (d < w), 1.0 / np.minimum(t + 1, w)[None, :], 0.0) - (d == 0)
    band = band.reshape(NT, P, NG * SEQ).transpose(1, 0, 2)
    return {"const": np.ascontiguousarray(const), "one_hot": one_hot, "band": np.ascontiguousarray(band)}


def kernel(**inputs):
    import concourse.bacc as bacc
    from concourse.bass_utils import run_bass_kernel_spmd

    nc = bacc.Bacc("TRN2", target_bir_lowering=False, num_devices=1)
    arrays = {f"in_{n}": np.ascontiguousarray(v) for n, v in inputs.items()}
    arrays |= {f"in_{n}": v for n, v in shape_constants().items()}
    aps = {n[3:]: nc.dram_tensor(n, v.shape, mybir.dt.from_np(v.dtype), kind="ExternalInput").ap()
           for n, v in arrays.items()}
    aps["out"] = nc.dram_tensor("out_0", (1, SEQ, D), F32, kind="ExternalOutput").ap()
    build(nc, aps)
    r = run_bass_kernel_spmd(nc, [arrays], core_ids=[0])
    return r.results[0]["out_0"]
```

```python
from contextlib import ExitStack

import numpy as np

import concourse.bass as bass
from concourse import mybir

ALU = mybir.AluOpType
ACT = mybir.ActivationFunctionType
F32 = mybir.dt.float32
I32 = mybir.dt.int32
F32R = mybir.dt.float32r
X = mybir.AxisListType.X

P = 128
D = 2048
SEQ = 256
NT = SEQ // P
KC = D // P
HEADS, HD = 8, 128
IH, ID = 16, 64
TOPK = SEQ // 4
BUCKETS = 32
TAPS, CCH = 31, 1024
CC = CCH // P
PAD = TAPS - 1
WINDOWS = (2, 4, 8, 16)
NG, EPG = 4, 4
NE = NG * EPG
FF = 512
FC = FF // P
EPS = 1e-6
NEG = -1e30
TAKEN = -3e38

Q0 = 0
K0 = 1024
IQ0 = 1280
IK0 = 2304
GA0 = 2384
GG0 = 3408
KVW = 256
IKW = 80

RING = 6
BLK = 4 * 512
HALF = BLK // 2
SPLITS = 4
ROUND = NG * EPG * 12
PASS_BLOCKS = EPG * 12
UNITS = [(0, "g"), (0, "u"), (1, "g"), (0, "d"), (1, "u"), (2, "g"), (1, "d"), (2, "u"), (3, "g"), (2, "d"),
         (3, "u"), (3, "d")]
BANK_U, BANK_T, BANK_Y = 2, 3, 4
GATHER_BANK = (0, 3, 0, 0)
NPASS = 2 * NG + 1

V_CB, V_LG, V_LB, V_QN, V_KN, V_POOL = 0, CC, 2 * CC, 3 * CC, 3 * CC + 1, 3 * CC + 2
V_ROWS = 3 * CC + 2 + KC
CW_ROWS = TAPS * CC
CW_HALF = CW_ROWS // 2


def mixer0_jobs():
    jobs = [("a0", (0, 1)), ("g0", (2, 3)), ("a1", (4, 5)), ("g1", (6, 7)),
            ("flip", (0, 1, 2, 3)),
            ("kvi", (4, 5)), ("iq0", (6, 7)), ("kT", (0,)), ("iq1", (1, 2))]
    jobs += [(f"il{i}", (4 + i % 2,)) for i in range(12)]
    jobs += [("mean", (6,)), ("var", (7,)), ("q0", (0, 1)), ("q1", (2, 3))]
    jobs += [(f"qT{i}", (4 + i,)) for i in range(4)]
    jobs += [("lg0", (0, 1)), ("lg1", (2, 3, 4, 5))]
    jobs += [(f"wc{n}", ((6, 7), (0, 1))[n % 2]) for n in range(4)]
    jobs += [(f"pT{i}", (2 + i % 4,)) for i in range(6)]
    jobs += [(f"oT{i}", (2 + (i + 2) % 4,)) for i in range(4)]
    jobs += [(f"wa{n}", ((6, 7), (0, 1))[n % 2]) for n in range(4)]
    return jobs


JOBS = mixer0_jobs()
JOB_AT = {name: i for i, (name, _) in enumerate(JOBS)}
BANKS = dict(JOBS)


STREAM = [("a0", 4), ("g0", 4), ("a1", 4), ("g1", 4), ("kvi", 4), ("iq0", 4), ("iq1", 4), ("q0", 4), ("q1", 4)]
STREAM += [(f"wc{n}", 2) for n in range(4)] + [(f"wa{n}", 2) for n in range(4)]
STREAM_END = {name: sum(2 * k for _, k in STREAM[:i + 1]) for i, (name, _) in enumerate(STREAM)}


def job_number(name):
    return sum(n not in STREAM_END for n, _ in JOBS[:JOB_AT[name] + 1])


def owner_before(name, bank):
    before = [n for n, banks in JOBS[:JOB_AT[name]] if bank in banks]
    return before[-1] if before else None


def indexer_heads(i):
    if i < 4:
        return 0, [8 * (i // 2) + 2 * m + i % 2 for m in range(4)]
    i -= 4
    return 1, [4 * (i // 2) + 2 * m + i % 2 for m in range(2)]


def build(nc, a):
    x_in, out = a["x"], a["out"]
    ctx = ExitStack()
    with ctx:
        def sb(name, shape, dt=F32):
            return ctx.enter_context(nc.sbuf_tensor(name, shape, dt))

        def sem(name):
            return ctx.enter_context(nc.semaphore(name))

        x_sb = sb("x_sb", [P, NT, D])
        xn = sb("xn", [P, NT * D])
        split_hi = sb("split_hi", [P, SPLITS, HALF], F32R)
        split_lo = sb("split_lo", [P, SPLITS, HALF], F32R)
        cat = sb("cat", [P, 4 * D], F32R)
        ring = sb("ring", [P, RING, BLK])
        const_sb = sb("const_sb", [P, 4 * P + SEQ + 8])
        vec_sb = sb("vec_sb", [P, V_ROWS])
        cw_sb = sb("cw_sb", [P, CW_ROWS])
        norm_cols = sb("norm_cols", [P, 3, KC])
        router_w = sb("router_w", [P, 2, KC, 20])
        router_b = sb("router_b", [P, 2, 20])
        ones = sb("ones", [P, P])
        sumsq = sb("sumsq", [P, 4, NT])
        meansq = sb("meansq", [P, 4, NT])
        rstd = sb("rstd", [P, 4, NT])
        minus_half = sb("minus_half", [P, SEQ])
        tick = sb("tick", [P, 24])
        upside = const_sb[:, 3 * P + SEQ + 8:]
        ident = const_sb[:, 0:P]
        before = const_sb[:, P:2 * P]
        slot_no = const_sb[:, 2 * P:3 * P]
        causal = const_sb[:, 3 * P:3 * P + SEQ]
        prio = const_sb[:, 3 * P + SEQ:3 * P + SEQ + 4]

        WORK = 13448
        work = sb("work", [P, WORK])

        def cut(at, *shape):
            n = int(np.prod(shape))
            assert at + n <= WORK, (at, n)
            flat = work[:, at:at + n]
            if len(shape) == 2:
                flat = flat.rearrange("p (a b) -> p a b", b=shape[1])
            if len(shape) == 3:
                flat = flat.rearrange("p (a b c) -> p a b c", b=shape[1], c=shape[2])
            return flat, at + n

        uT, o = cut(0, CC, PAD + SEQ)
        conv, o = cut(o, CC, SEQ)
        iqT, o = cut(o, CC, SEQ)
        ikT, o = cut(o, SEQ)
        kT, o = cut(o, SEQ)
        v_sb, o = cut(o, NT, P)
        k_sb, o = cut(o, NT, P)
        ik2, o = cut(o, NT, P)
        iw_sb, o = cut(o, NT, IH)
        il_relu, o = cut(o, 2, 512)
        tap_out, o = cut(o, 2, SEQ)
        score, o = cut(o, NT, SEQ)
        picked, o = cut(o, NT, SEQ)
        top8, o = cut(o, NT, 8)
        ksq, o = cut(o, 8)
        hsq, o = cut(o, NT, HEADS)
        hms, o = cut(o, NT, HEADS)
        hrs, o = cut(o, NT, HEADS)
        smax, o = cut(o, NT, HEADS)
        ssum, o = cut(o, NT, HEADS)
        srec, o = cut(o, NT, HEADS)
        bias_sb, o = cut(o, HEADS, SEQ)
        logits0, o = cut(o, HEADS, P)
        bias_up = iqT
        th_glu = logits0.rearrange("p h s -> p (h s)").rearrange("p (c s) -> p c s", s=SEQ)
        th_conv = uT.rearrange("p a b -> p (a b)")[:, 0:CC * SEQ].rearrange("p (h s) -> p h s", h=CC)
        mean_sb = il_relu[:, 0, 0:SEQ]
        rvar = il_relu[:, 1, 0:SEQ]
        vsq = iqT
        qn = xn[:, 0:NT * HEADS * HD].rearrange("p (t c) -> p t c", t=NT)
        qT = xn[:, NT * HEADS * HD:].rearrange("p (h s) -> p h s", h=HEADS)
        pT0 = qn.rearrange("p t c -> p (t c)")[:, 0:HEADS * P]
        pT1 = iqT.rearrange("p a b -> p (a b)").rearrange("p (s c) -> p s c", s=2)
        normed = il_relu

        def cat_cut(at, a, b):
            return [cat[:, at + i * a * b:at + (i + 1) * a * b].rearrange("p (a b) -> p a b", b=b) for i in range(2)]

        hT = cat_cut(0, KC, SEQ)
        convT = cat_cut(0, CC, SEQ)
        attnT = cat_cut(2 * D, HEADS, SEQ)
        dT = cat_cut(0, KC, SEQ)
        hgT = cat_cut(0, KC, P)
        actT = cat_cut(2 * D, FC, P)

        pooled = xn[:, 0:2 * 512].rearrange("p (a b) -> p a b", a=2)
        scale_bc, o2 = cut(8020, D)
        band, o2 = cut(o2, NT, 4 * SEQ)
        mixed, o2 = cut(o2, 2, 512)

        hT32, _ = cut(8020, KC, SEQ)
        th_gate, o3 = cut(0, 2, 512)
        slots_f, o3 = cut(o3, 2, 512)
        gated, o3 = cut(o3, 2, 512)
        act, o3 = cut(o3, 512)
        y_sb, o3 = cut(o3, D)
        pick, o3 = cut(o3, NT, P)
        pickT, o3 = cut(o3, NT, P)
        comb_now, o3 = cut(o3, NT, EPG)
        comb_slot, o3 = cut(o3, EPG)
        lgt, o3 = cut(o3, NT, 20)
        oneh, o3 = cut(o3, NT, NG)
        sel1, o3 = cut(o3, NT, NG)
        sel2, o3 = cut(o3, NT, NG)
        t4a, o3 = cut(o3, NT, NG)
        t4b, o3 = cut(o3, NT, NG)
        el, o3 = cut(o3, NT, EPG)
        ex_g, o3 = cut(o3, NT, NG)
        ex_e, o3 = cut(o3, NT, EPG)
        wgt, o3 = cut(o3, NT, EPG)
        prod, o3 = cut(o3, NT, NE)
        comb, o3 = cut(o3, NT, NPASS * EPG)
        rank_in, o3 = cut(o3, NT, NPASS)
        gmax, o3 = cut(o3, NT, 1)
        stat, o3 = cut(o3, 8, NT)
        cnt, o3 = cut(o3, NG)
        assert o3 <= 8020
        vec_rows = conv.rearrange("p a b -> p (a b)")[:, 0:3 * P].rearrange("p (a b) -> p a b", a=3)
        one_hot = conv.rearrange("p a b -> p (a b)")[0:BUCKETS, 512:1024]
        rel_sb = conv.rearrange("p a b -> p (a b)")[0:BUCKETS, 1024:1024 + HEADS]
        bias_row = conv.rearrange("p a b -> p (a b)")[0:HEADS, 1536:2048]
        npass_i = sb("npass_i", [P, 4], I32)

        ps = ctx.enter_context(nc.psum_tensor("ps", [P, 8, 512], F32))
        bias_dram = nc.dram_tensor("bias_dram", [HEADS, 512], F32, kind="Internal").ap()

        DVE_CHUNKS = ((0, 1, 2), (4, 5, 6))
        POOL_CHUNKS = (3, 7)
        DVE_TAPS = 6 * TAPS

        const_in = sem("const_in")
        rows_in = sem("rows_in")
        x_loaded = sem("x_loaded")
        scale_in = sem("scale_in")
        bias_stored = sem("bias_stored")
        bias_loaded = sem("bias_loaded")
        bias_out = sem("bias_out")
        x_stored = sem("x_stored")
        down_started = sem("down_started")
        set_up = sem("set_up")
        vec_done = sem("vec_done")
        vec_out = sem("vec_out")
        x_ready = sem("x_ready")
        sq_done = sem("sq_done")
        ms_done = sem("ms_done")
        rstd_done = sem("rstd_done")
        xn_done = sem("xn_done")
        xT_done = sem("xT_done")
        xT_out = sem("xT_out")
        job_done = sem("job_done")
        th_done = sem("th_done")
        u_done = sem("u_done")
        conv_step = sem("conv_step")
        pool_step = sem("pool_step")
        kvi_out = sem("kvi_out")
        k_scaled = sem("k_scaled")
        kT_out = sem("kT_out")
        iq_out = sem("iq_out")
        head_ms = sem("head_ms")
        head_rs = sem("head_rs")
        relu_done = sem("relu_done")
        score_step = sem("score_step")
        topk_step = sem("topk_step")
        qsq_done = sem("qsq_done")
        hsq_done = sem("hsq_done")
        qn_done = sem("qn_done")
        qT_out = sem("qT_out")
        logit_step = sem("logit_step")
        exp_done = sem("exp_done")
        prob_step = sem("prob_step")
        prob_done = sem("prob_done")
        pT_out = sem("pT_out")
        oT_out = sem("oT_out")
        attn_lo = sem("attn_lo")
        ln_step = sem("ln_step")
        ln_pool = sem("ln_pool")
        y_half = sem("y_half")
        th_conv_done = sem("th_conv_done")
        conv_done = sem("conv_done")
        x_added = sem("x_added")
        dT_done = sem("dT_done")
        dT_out = sem("dT_out")
        mix_done = sem("mix_done")
        mix_step = sem("mix_step")
        mixer_in = [sem(f"mixer_in{s}") for s in range(RING)]
        mixer_hi = sem("mixer_hi")
        mixer_lo = sem("mixer_lo")
        mixer_used = sem("mixer_used")
        pool_hi = sem("pool_hi")
        pool_lo = sem("pool_lo")
        normed_f = sem("normed_f")
        normed_hi = sem("normed_hi")
        conv_hi_done = sem("conv_hi_done")
        pooled_f = sem("pooled_f")
        pooled_hi = sem("pooled_hi")
        pool_in = [sem(f"pool_in{s}") for s in range(NG)]
        moe = []
        for l in range(2):
            moe.append({n: sem(f"{n}_{l}") for n in (
                "router_done", "route_step", "exp_out", "exp_in", "rank_done", "route_done", "pick_ready", "gathered", "gather_out",
                "rank_in", "misc_done", "misc_out", "th_gate_done", "gated_done", "act_done",
                "actT_done", "actT_out", "slots_in", "slots_hi",
                "actT_hi", "y_out", "scattered", "x_moved", "hi", "lo", "used")})
            moe[l]["in"] = [sem(f"moe_in{l}_{s}") for s in range(RING)]

        w_in = a["w_in_e"][0].rearrange("(p k) n -> p k n", k=KC)
        w_out = a["w_out_e"][0].rearrange("(c p) n -> p c n", p=P)

        def in_block(kq, col, n):
            return lambda slot: [(ring[:, slot, 0:4 * n].rearrange("p (k n) -> p k n", k=4),
                                  w_in[:, 4 * kq:4 * kq + 4, col:col + n])]

        def kvi_block(kq):
            def parts(slot):
                out = []
                for h in range(2):
                    rows = slice(4 * kq + 2 * h, 4 * kq + 2 * h + 2)
                    mid, end = h * HALF + 2 * KVW, h * HALF + 2 * (KVW + IKW)
                    out.append((ring[:, slot, h * HALF:mid].rearrange("p (k n) -> p k n", k=2), w_in[:, rows, K0:K0 + KVW]))
                    out.append((ring[:, slot, mid:end].rearrange("p (k n) -> p k n", k=2), w_in[:, rows, IK0:IK0 + IKW]))
                return out
            return parts

        def out_block(cq, n):
            return lambda slot: [(ring[:, slot, :].rearrange("p (k n) -> p k n", k=4),
                                  w_out[:, 4 * cq:4 * cq + 4, n * 512:n * 512 + 512])]

        mixer_blocks = []
        for col in (GA0, GG0, GA0 + 512, GG0 + 512):
            mixer_blocks += [in_block(kq, col, 512) for kq in range(4)]
        mixer_blocks += [kvi_block(kq) for kq in range(4)]
        for col in (IQ0, IQ0 + 512, Q0, Q0 + 512):
            mixer_blocks += [in_block(kq, col, 512) for kq in range(4)]
        for half in (2, 0):
            mixer_blocks += [out_block(half + q, n) for n in range(4) for q in range(2)]
        NMIX = len(mixer_blocks)
        MOE0 = [NMIX, NMIX + ROUND + NG]
        POOL0 = NMIX + ROUND
        kvi_at = [16 + i for i in range(4)]

        def mixer_landed(b):
            return 16 * sum(4 if c in kvi_at else 1 for c in range(b % RING, b + 1, RING))

        def raw_half(slot, half, n=HALF):
            return ring[:, slot, half * HALF:half * HALF + n]

        def moe_source(l, g, j):
            e, kind = UNITS[j // 4]
            name, rows = {"g": ("w_gate", KC), "u": ("w_up", KC), "d": ("w_down", FC)}[kind]
            w = a[name][l].rearrange("e (p k) n -> p e (k n)", k=rows)
            return w[:, bass.ds(g * EPG + e, 1), (j % 4) * BLK:(j % 4 + 1) * BLK]

        def unit_done(eng, l, p, e, kind):
            eng.wait_ge(moe[l]["used"], p * (2 * PASS_BLOCKS) + (8 * (UNITS.index((e, kind)) + 1) + SPLITS))

        def moe_slot(l, j):
            return (MOE0[l] + j) % RING

        def wait_for_job(eng, name):
            if name in STREAM_END:
                eng.wait_ge(mixer_used, STREAM_END[name])
            else:
                eng.wait_ge(job_done, job_number(name))

        heads_before = [0]
        for i in range(12):
            heads_before.append(heads_before[-1] + len(indexer_heads(i)[1]))

        def emptied(name):
            kind, i = name.rstrip("0123456789"), int(name[-1] if name[-1].isdigit() else 0)
            if name in ("il10", "il11"):
                i = int(name[2:])
            return {"a": (u_done, i + 1), "g": (th_done, i + 1), "flip": (bias_out, 1), "kvi": (k_scaled, 2), "iq": (iq_out, i + 1),
                    "kT": (kT_out, 1), "il": (relu_done, i + 1), "q": (qn_done, 2 * i + 2), "qT": (qT_out, i + 1),
                    "lg": (logit_step, 3 + 3 * i), "mean": (ln_step, 1), "var": (ln_step, 3),
                    "wc": (x_added, 2 * i + 2), "wa": (x_added, 2 * i + 10), "pT": (pT_out, i + 1),
                    "oT": (attn_lo, i + 1)}[kind]

        block = ctx.enter_context(nc.Block())

        @block.sync
        def _(sp):
            sp.dma_start(x_sb[:], x_in[0].rearrange("(t p) d -> p t d", p=P)).then_inc(x_loaded, 16)
            for b, parts in enumerate(mixer_blocks):
                s = b % RING
                if b >= RING:
                    sp.wait_ge(mixer_lo, 2 * (b - RING + 1))
                for dst, src in parts(s):
                    sp.dma_start(dst, src).then_inc(mixer_in[s], 16)

            def load_moe(l, g, j):
                sp.dma_start(ring[:, moe_slot(l, j):moe_slot(l, j) + 1, :], moe_source(l, g, j)) \
                    .then_inc(moe[l]["in"][moe_slot(l, j)], 16)

            def stream_round(l, base):
                split = moe[l]["lo"]
                with sp.Fori(0, NG - 1) as g:
                    for j in range(RING, PASS_BLOCKS):
                        sp.wait_ge(split, g * (2 * PASS_BLOCKS) + 2 * (base + j - RING + 1))
                        if UNITS[j // 4] == (0, "d") and j % 4 == 0:
                            sp.sem_inc(down_started, 1)
                        load_moe(l, g, j)
                    for j in range(RING):
                        sp.wait_ge(split, g * (2 * PASS_BLOCKS) + 2 * (base + PASS_BLOCKS + j - RING + 1))
                        load_moe(l, g + 1, j)
                for j in range(RING, PASS_BLOCKS):
                    sp.wait_ge(split, 2 * ((NG - 1) * PASS_BLOCKS + base + j - RING + 1))
                    load_moe(l, NG - 1, j)

            for l in range(2):
                for j in range(RING):
                    owner = MOE0[l] + j - RING
                    if l == 0:
                        sp.wait_ge(mixer_lo, 2 * (owner + 1))
                    elif owner < POOL0:
                        sp.wait_ge(moe[0]["lo"], splits_more + 2 * (owner - MOE0[0] + 1))
                    else:
                        sp.wait_ge(pool_lo, 2 * (owner - POOL0 + 1))
                    load_moe(l, 0, j)
                stream_round(l, 0)
                sp.wait_ge(moe[l]["route_done"], 1)
                more = sp.value_load(npass_i[0:1, 2 * l + 1:2 * l + 2], min_val=0, max_val=NG)
                with sp.If(more > 0):
                    for j in range(RING):
                        sp.wait_ge(moe[l]["lo"], 2 * (ROUND + j - RING + 1))
                        load_moe(l, 0, j)
                    stream_round(l, ROUND)
                if l == 0:
                    splits_more = more * (2 * PASS_BLOCKS)
                    for g in range(NG):
                        sp.wait_ge(moe[0]["lo"], splits_more + 2 * (ROUND - RING + g + 1))
                        sp.dma_start(ring[:, (POOL0 + g) % RING, :].rearrange("p (k n) -> p k n", k=4),
                                     a["pool_w_o"][0, g].rearrange("(k p) n -> p k n", p=P)) \
                            .then_inc(pool_in[g], 16)
            sp.wait_ge(x_ready, 4)
            sp.dma_start(out[0].rearrange("(t p) d -> p t d", p=P), x_sb[:]).then_inc(x_stored, 16)
            sp.wait_ge(x_stored, 16)

        @block.gpsimd
        def _(pool):
            def root(i):
                pool.wait_ge(sq_done, NT * (i + 1))
                nc.gpsimd.tensor_scalar(meansq[:, i], sumsq[:, i], 1.0 / D, EPS, ALU.mult, ALU.add) \
                    .then_inc(ms_done, 1)
                pool.wait_ge(ms_done, i + 1)
                nc.gpsimd.tensor_tensor(rstd[:, i], meansq[:, i], minus_half[:, 0:NT], ALU.pow) \
                    .then_inc(rstd_done, 1)

            def head_root(n, dst, tmp, src, width):
                nc.gpsimd.tensor_scalar(tmp, src, 1.0 / HD, EPS, ALU.mult, ALU.add).then_inc(head_ms, 1)
                pool.wait_ge(head_ms, n + 1)
                nc.gpsimd.tensor_tensor(dst, tmp, minus_half[:, 0:width], ALU.pow).then_inc(head_rs, 1)

            pool.wait_ge(set_up, 1)
            root(0)
            steps = [0]

            def step(ins):
                ins.then_inc(pool_step, 1)
                steps[0] += 1

            def convolve(c):
                times = lambda w: step(nc.gpsimd.tensor_tensor(
                    tap_out[:, w % 2, :], uT[:, c, w:w + SEQ],
                    cw_sb[:, w * CC + c:w * CC + c + 1].to_broadcast([P, SEQ]), ALU.mult))
                pool.wait_ge(u_done, c // 4 + 1)
                times(0)
                for w in range(TAPS):
                    if w + 1 < TAPS:
                        if w:
                            pool.wait_ge(pool_step, steps[0])
                        times(w + 1)
                    pool.wait_ge(pool_step, steps[0] - (w + 1 < TAPS))
                    before = conv[:, c, :] if w else vec_sb[:, V_CB + c:V_CB + c + 1].to_broadcast([P, SEQ])
                    step(nc.gpsimd.tensor_tensor(conv[:, c, :], tap_out[:, w % 2, :], before, ALU.add))
                pool.wait_ge(pool_step, steps[0])

            pool.wait_ge(vec_out, 1)
            convolve(POOL_CHUNKS[0])
            pool.wait_ge(kvi_out, 2)
            head_root(0, ksq[:, 4:6], ksq[:, 2:4], ksq[:, 0:2], 2)
            convolve(POOL_CHUNKS[1])
            for i in range(2):
                for t in range(NT):
                    pool.wait_ge(hsq_done, NT * i + t + 1)
                    heads = slice(4 * i, 4 * i + 4)
                    head_root(1 + NT * i + t, hrs[:, t, heads], hms[:, t, heads], hsq[:, t, heads], 4)
                if i == 0:
                    pool.wait_ge(ln_step, 3)
                    nc.gpsimd.tensor_tensor(rvar, rvar, minus_half[:], ALU.pow).then_inc(ln_pool, 1)
            root(1)
            root(2)
            root(3)

        @block.scalar
        def _(act):
            def copy(out, in_, scale=1.0):
                return nc.scalar.activation(out, in_, ACT.Copy, scale=scale)

            act.dma_start(const_sb[:], a["const"]).then_inc(const_in, 16)
            for dst, name in ((rel_sb, "rel_bias"), (one_hot, "one_hot")):
                act.dma_start(dst, a[name]).then_inc(rows_in, 16)
            row = lambda name, n: a[name][0].rearrange("(c p) -> c p", p=P)
            for at, src, n in ((V_CB, row("conv_b_e", CC), CC), (V_LG, row("conv_ln_g_e", CC), CC),
                               (V_LB, row("conv_ln_b_e", CC), CC), (V_QN, a["q_norm_e"], 1),
                               (V_KN, a["k_norm_e"], 1), (V_POOL, row("mix_norm_o", KC), KC)):
                act.dma_start(vec_rows[at:at + n, 0, :], src).then_inc(rows_in, 16)
            taps = a["conv_w_e"][0].rearrange("w (c p) -> (w c) p", p=P)
            for h in range(2):
                act.dma_start(vec_rows[0:CW_HALF, 1 + h, :], taps[h * CW_HALF:(h + 1) * CW_HALF, :]).then_inc(rows_in, 16)
            act.dma_start(norm_cols[:, 0, :], a["mix_norm_e"][0].rearrange("(p k) -> p k", k=KC)).then_inc(const_in, 16)
            for l in range(2):
                act.dma_start(norm_cols[:, 1 + l, :], a["ffn_norm"][l].rearrange("(p k) -> p k", k=KC)).then_inc(const_in, 16)
                act.dma_start(router_w[:, l, :, 0:NG], a["router_group_w"][l].rearrange("(p k) g -> p k g", k=KC)) \
                    .then_inc(const_in, 16)
                act.dma_start(router_w[:, l, :, NG:20], a["router_expert_w"][l].rearrange("(p k) g -> p k g", k=KC)) \
                    .then_inc(const_in, 16)
                act.dma_start(router_b[:, l, 0:NG], a["router_group_b"][l:l + 1, :].partition_broadcast(P)) \
                    .then_inc(const_in, 16)
                act.dma_start(router_b[:, l, NG:20], a["router_expert_b"][l:l + 1, :].partition_broadcast(P)) \
                    .then_inc(const_in, 16)

            def norm(i, permuted):
                if i:
                    act.wait_ge(x_ready, i)
                else:
                    act.wait_ge(x_loaded, 16)
                nc.scalar.activation(xn[:, D:2 * D], x_sb[:, 1, :], ACT.Square,
                                     accum_out=sumsq[:, i, 1:2]).then_inc(sq_done, 1)
                act.wait_ge(rstd_done, i + 1)
                dst = xn[:, D:2 * D]
                src = x_sb[:, 1, :]
                if permuted:
                    dst = dst.rearrange("p (k j) -> p k j", k=KC)
                    src = src.rearrange("p (j k) -> p k j", k=KC)
                act.wait_ge(sq_done, NT * (i + 1))
                copy(dst, src, rstd[:, i, 1:2]).then_inc(xn_done, 1)

            act.wait_ge(vec_done, 1)
            copy(vec_sb[:, 0:V_LG], ps[:, 0, 0:V_LG])
            copy(vec_sb[:, V_LG:V_QN], ps[:, 0, V_LG:V_QN], 0.5)
            copy(vec_sb[:, V_QN:V_ROWS], ps[:, 0, V_QN:V_ROWS])
            copy(cw_sb[:], ps[:, 0, 64:64 + CW_ROWS], 0.5).then_inc(vec_out, 1)
            act.wait_ge(vec_done, 2)
            copy(bias_row, ps[0:HEADS, 1, :]).then_inc(vec_out, 1)
            act.wait_ge(vec_out, 2)
            act.dma_start(bias_dram, bias_row).then_inc(bias_stored, 16)
            act.wait_ge(bias_stored, 16)
            act.dma_start(bias_up, bass.AP(tensor=bias_dram.tensor, offset=0,
                                           ap=[[1, P], [512, HEADS], [1, SEQ]])).then_inc(bias_loaded, 16)
            norm(0, True)
            for q in range(8):
                t, kq = q // 4, q % 4
                act.wait_ge(normed_f, q + 1)
                copy(hT[0][:, 4 * kq:4 * kq + 4, t * P:(t + 1) * P],
                     normed[:, q % 2, :].rearrange("p (k s) -> p k s", k=4)).then_inc(normed_hi, 1)

            def wait_job(name):
                wait_for_job(act, name)

            at = [0]

            def split_to(end):
                for u in range(at[0], end):
                    b, n = u // 2, 2 * (KVW + IKW) if u // 2 in kvi_at else HALF
                    if u % 2 == 0:
                        act.wait_ge(mixer_in[b % RING], mixer_landed(b))
                    if u >= SPLITS:
                        act.wait_ge(mixer_used, u - SPLITS + 1)
                    copy(split_hi[:, u % SPLITS, 0:n], raw_half(b % RING, u % 2, n)).then_inc(mixer_hi, 1)
                at[0] = end

            def split_past(name):
                split_to(min(STREAM_END[name] + SPLITS, STREAM_END["wa3"]))

            for i in range(2):
                split_past(f"g{i}")
                wait_job(f"g{i}")
                if i:
                    act.wait_ge(u_done, 1)
                nc.scalar.activation(th_glu, ps[:, 2 + 4 * i:4 + 4 * i, :].rearrange("p b (c s) -> p (b c) s", s=SEQ),
                                     ACT.Tanh, scale=0.5).then_inc(th_done, 1)
            wait_job("flip")
            copy(bias_sb.rearrange("p h s -> p (h s)"), ps[:, 0:4, :].rearrange("p b n -> p (b n)")).then_inc(bias_out, 1)
            split_past("kvi")
            wait_job("kvi")
            copy(v_sb, ps[:, 4:6, P:2 * P])
            for h in range(2):
                copy(ik2[:, :, h * ID:(h + 1) * ID], ps[:, 4:6, KVW:KVW + ID])
            copy(iw_sb, ps[:, 4:6, KVW + ID:KVW + IKW], IH ** -0.5 * ID ** -0.5).then_inc(kvi_out, 1)
            for t in range(NT):
                sq = nc.scalar.activation(il_relu[:, t, 0:P], ps[:, 4 + t, 0:P], ACT.Square, accum_out=ksq[:, t:t + 1])
            sq.then_inc(kvi_out, 1)
            split_past("iq0")
            for i in range(2):
                if i:
                    wait_job("kT")
                    copy(kT, ps[:, 0, 0:SEQ], vec_sb[:, V_KN:V_KN + 1])
                    copy(ikT, ps[:, 0, SEQ:2 * SEQ]).then_inc(kT_out, 1)
                    split_past("iq1")
                wait_job(f"iq{i}")
                copy(iqT[:, 4 * i:4 * i + 4, :].rearrange("p c s -> p (c s)"),
                     ps[:, BANKS[f"iq{i}"][0]:BANKS[f"iq{i}"][1] + 1, :].rearrange("p b n -> p (b n)")).then_inc(iq_out, 1)

            def q_squares(i):
                wait_job(f"q{i}")
                for t in range(NT):
                    nc.scalar.activation(qn[:, t, 512 * i:512 * i + 512], ps[:, 2 * i + t, :], ACT.Square).then_inc(qsq_done, 1)

            for i in range(12):
                wait_job(f"il{i}")
                if i >= 2:
                    act.wait_ge(score_step, heads_before[i - 1])
                nc.scalar.activation(il_relu[:, i % 2, :], ps[:, BANKS[f"il{i}"][0], :], ACT.Relu).then_inc(relu_done, 1)
                split_to(STREAM_END["iq1"] + SPLITS + i + 1)
                if i == 8:
                    q_squares(0)
            act.wait_ge(ln_step, 2)
            nc.scalar.activation(vsq, conv, ACT.Square).then_inc(y_half, 1)
            split_past("q1")
            q_squares(1)
            for i in range(4):
                t, hq = i // 2, i % 2
                wait_job(f"qT{i}")
                copy(qT[:, 4 * hq:4 * hq + 4, t * P:(t + 1) * P], ps[:, 4 + i, :].rearrange("p (h s) -> p h s", h=4),
                     vec_sb[:, V_QN:V_QN + 1]).then_inc(qT_out, 1)

            act.wait_ge(ln_step, 4)
            for c in range(CC):
                last = nc.scalar.activation(conv[:, c, :], conv[:, c, :], ACT.Identity,
                                            scale=vec_sb[:, V_LG + c:V_LG + c + 1], bias=vec_sb[:, V_LB + c:V_LB + c + 1])
            last.then_inc(y_half, 1)
            act.wait_ge(y_half, 2)
            nc.scalar.activation(th_conv, conv, ACT.Tanh).then_inc(th_conv_done, 1)
            act.wait_ge(conv_done, 1)
            copy(convT[0], conv).then_inc(conv_hi_done, 1)

            for t, lg in enumerate((logits0, bias_sb)):
                act.wait_ge(logit_step, 5 + 3 * t)
                for h in range(HEADS):
                    last = nc.scalar.activation(lg[:, h, :], lg[:, h, :], ACT.Exp, bias=smax[:, t, h:h + 1],
                                                accum_out=ssum[:, t, h:h + 1])
                last.then_inc(exp_done, 1)
            split_past("wc3")
            for i in range(6):
                wait_job(f"pT{i}")
                dst = pT0[:, i * 512:(i + 1) * 512] if i < 2 else pT1[:, (i - 2) // 2, (i % 2) * 512:(i % 2) * 512 + 512]
                copy(dst, ps[:, BANKS[f"pT{i}"][0], :]).then_inc(pT_out, 1)
            for i in range(4):
                t, hq = i // 2, i % 2
                wait_job(f"oT{i}")
                copy(attnT[0][:, 4 * hq:4 * hq + 4, t * P:(t + 1) * P],
                     ps[:, BANKS[f"oT{i}"][0], :].rearrange("p (h s) -> p h s", h=4)).then_inc(oT_out, 1)
            split_past("wa3")

            def moe_act(l):
                m = moe[l]
                norm(1 if l == 0 else 3, True)
                act.wait_ge(m["exp_in"], 1)
                nc.scalar.activation(ex_g, oneh, ACT.Exp).then_inc(m["exp_out"], 1)
                act.wait_ge(m["exp_in"], 2)
                nc.scalar.activation(ex_e, el, ACT.Exp).then_inc(m["exp_out"], 1)
                act.wait_ge(m["route_done"], 1)
                if l == 0:
                    act.dma_start(scale_bc, a["pool_scale_o"][0:1, :].partition_broadcast(P)).then_inc(scale_in, 16)
                    act.dma_start(band, a["band"]).then_inc(scale_in, 16)

                def slots_hi(p, q):
                    act.wait_ge(m["slots_in"], p * 4 + (q + 1))
                    copy(hgT[0][:, 4 * q:4 * q + 4, :], slots_f[:, q % 2, :].rearrange("p (k s) -> p k s", k=4)) \
                        .then_inc(m["slots_hi"], 1)

                for q in range(4):
                    slots_hi(0, q)
                n = act.value_load(npass_i[0:1, 2 * l:2 * l + 1], min_val=NG, max_val=2 * NG)
                with act.Fori(0, n) as p:
                    def split(first, last):
                        for u in range(first, last):
                            if u % 2 == 0:
                                act.wait_ge(m["in"][moe_slot(l, u // 2)],
                                            p * (16 * PASS_BLOCKS // RING) + 16 * (u // 2 // RING + 1))
                            act.wait_ge(m["used"], p * (2 * PASS_BLOCKS) + (u + 1))
                            copy(split_hi[:, u % SPLITS, :], raw_half(moe_slot(l, u // 2), u % 2)).then_inc(m["hi"], 1)

                    def turned(e):
                        act.wait_ge(m["actT_done"], p * EPG + (e + 1))
                        copy(actT[0], ps[:, BANK_T, :].rearrange("p (k s) -> p k s", k=FC)).then_inc(m["actT_hi"], 1)

                    def tanh(e):
                        unit_done(act, l, p, e, "g")
                        nc.scalar.activation(th_gate[:, e % 2, :], ps[:, e % 2, :], ACT.Tanh, scale=0.5) \
                            .then_inc(m["th_gate_done"], 1)

                    split(0, 4)
                    act.wait_ge(m["misc_done"], p + 1)
                    copy(pickT, ps[:, BANK_T, 0:NT * P].rearrange("p (t s) -> p t s", t=NT))
                    copy(comb_slot, ps[:, BANK_T, NT * P:NT * P + EPG]).then_inc(m["misc_out"], 1)
                    split(4, 12)
                    tanh(0)
                    for e in range(1, EPG):
                        gate = 8 * UNITS.index((e, "g"))
                        split(12 if e == 1 else gate - 4, gate + 10)
                        turned(e - 1)
                        split(gate + 10, gate + 12)
                        tanh(e)
                        if e < EPG - 1:
                            split(gate + 12, gate + 20)
                    split(gate + 12, 92)
                    for q in range(3):
                        slots_hi(p + 1, q)
                    turned(EPG - 1)
                    split(92, 94)
                    slots_hi(p + 1, 3)
                    split(94, 96)
                    unit_done(act, l, p, EPG - 1, "d")
                    for b in range(4):
                        copy(y_sb[:, b * 512:(b + 1) * 512], ps[:, BANK_Y + b, :]).then_inc(m["y_out"], 1)

            moe_act(0)
            norm(2, False)
            for i in range(8):
                act.wait_ge(pooled_f, i + 1)
                copy(dT[0][:, 2 * i:2 * i + 2, :], pooled[:, i % 2, :].rearrange("p (c s) -> p c s", c=2)).then_inc(pooled_hi, 1)
            for u in range(2 * NG):
                if u % 2 == 0:
                    act.wait_ge(pool_in[u // 2], 16)
                if u >= SPLITS:
                    act.wait_ge(mix_done, 2 * (u // 2 - 1))
                copy(split_hi[:, u % SPLITS, :], raw_half((POOL0 + u // 2) % RING, u % 2)).then_inc(pool_hi, 1)
            moe_act(1)

        @block.vector
        def _(dve):
            tt = nc.vector.tensor_tensor
            ts = nc.vector.tensor_scalar
            stt = nc.vector.scalar_tensor_tensor

            nc.vector.memset(minus_half[:], -0.5)
            nc.vector.memset(uT[:, :, 0:PAD], 0.0)
            nc.vector.memset(ones[:], 1.0).then_inc(set_up, 1)

            ticks = [0]

            def tick_off():
                ticks[0] += 1
                return nc.vector.memset(tick[:, ticks[0] - 1:ticks[0]], 0.0)

            def norm(i, permuted):
                if i:
                    dve.wait_ge(x_ready, i)
                else:
                    dve.wait_ge(x_loaded, 16)
                stt(out=xn[:, 0:D], in0=x_sb[:, 0, :], scalar=1.0, in1=x_sb[:, 0, :], op0=ALU.mult, op1=ALU.mult,
                    accum_out=sumsq[:, i, 0:1]).then_inc(sq_done, 1)
                dve.wait_ge(rstd_done, i + 1)
                dst = xn[:, 0:D]
                src = x_sb[:, 0, :]
                if permuted:
                    dst = dst.rearrange("p (k j) -> p k j", k=KC)
                    src = src.rearrange("p (j k) -> p k j", k=KC)
                ts(dst, src, rstd[:, i, 0:1], None, ALU.mult).then_inc(xn_done, 1)

            def low(dst, full, hi):
                return tt(dst, full, hi.bitcast(F32), ALU.subtract)

            def split_channels():
                def lo(q):
                    t, kq = q // 4, q % 4
                    at = (slice(None), slice(4 * kq, 4 * kq + 4), slice(t * P, (t + 1) * P))
                    dve.wait_ge(normed_hi, q + 1)
                    low(hT[1][at], normed[:, q % 2, :].rearrange("p (k s) -> p k s", k=4), hT[0][at]).then_inc(xT_out, 1)

                for q in range(8):
                    kq = q % 4
                    dve.wait_ge(xT_done, q + 1)
                    if q >= 2:
                        dve.wait_ge(xT_out, q - 1)
                    tt(normed[:, q % 2, :].rearrange("p (k s) -> p k s", k=4), ps[:, q, :].rearrange("p (k s) -> p k s", k=4),
                       norm_cols[:, 0, 4 * kq:4 * kq + 4].unsqueeze(2).to_broadcast([P, 4, P]), ALU.mult).then_inc(normed_f, 1)
                    if q:
                        lo(q - 1)
                lo(7)

            def normed_channels(n, col):
                for q in range(8):
                    t, kq = q // 4, q % 4
                    dve.wait_ge(xT_done, 8 * n + q + 1)
                    w = norm_cols[:, col, 4 * kq:4 * kq + 4].unsqueeze(2).to_broadcast([P, 4, P])
                    tt(hT32[:, 4 * kq:4 * kq + 4, t * P:(t + 1) * P], ps[:, q, :].rearrange("p (k s) -> p k s", k=4),
                       w, ALU.mult).then_inc(xT_out, 1)

            def wait_job(name):
                wait_for_job(dve, name)

            norm(0, True)
            dve.wait_ge(const_in, 16 * 12)
            split_channels()

            conv_ops = [(chunks, i, w) for chunks in DVE_CHUNKS for w in range(TAPS) for i in range(3)]

            def convolve(first, last):
                for n in range(first, last):
                    chunks, i, w = conv_ops[n]
                    c = chunks[i]
                    tap = cw_sb[:, w * CC + c:w * CC + c + 1]
                    if w == 0:
                        ts(conv[:, c, :], uT[:, c, 0:SEQ], tap, vec_sb[:, V_CB + c:V_CB + c + 1], ALU.mult, ALU.add) \
                            .then_inc(conv_step, 1)
                    else:
                        dve.wait_ge(conv_step, n - 2)
                        stt(out=conv[:, c, :], in0=uT[:, c, w:w + SEQ], scalar=tap, in1=conv[:, c, :],
                            op0=ALU.mult, op1=ALU.add).then_inc(conv_step, 1)

            at = [0, 0]

            def split_to(end, taps=0):
                for u in range(at[0], end):
                    b, n = u // 2, 2 * (KVW + IKW) if u // 2 in kvi_at else HALF
                    dve.wait_ge(mixer_hi, u + 1)
                    low(split_lo[:, u % SPLITS, 0:n], raw_half(b % RING, u % 2, n), split_hi[:, u % SPLITS, 0:n]) \
                        .then_inc(mixer_lo, 1)
                    more = min(taps, len(conv_ops) - at[1])
                    convolve(at[1], at[1] + more)
                    at[1] += more
                at[0] = end

            def split_past(name, taps=0):
                split_to(min(STREAM_END[name] + SPLITS, STREAM_END["wa3"]), taps)

            dve.wait_ge(vec_out, 1)
            for i in range(2):
                split_past(f"g{i}", 3 * i)
                wait_job(f"a{i}")
                dve.wait_ge(th_done, i + 1)
                stt(out=uT[:, 4 * i:4 * i + 4, PAD:PAD + SEQ], in0=th_glu, scalar=1.0,
                    in1=ps[:, 4 * i:4 * i + 2, :].rearrange("p b (c s) -> p (b c) s", s=SEQ),
                    op0=ALU.add, op1=ALU.mult).then_inc(u_done, 1)
                dve.wait_ge(u_done, i + 1)
            split_past("kvi", 3)
            wait_job("kvi")
            dve.wait_ge(kvi_out, 2)
            dve.wait_ge(head_rs, 1)
            for t in range(NT):
                ts(k_sb[:, t, :], ps[:, 4 + t, 0:P], ksq[:, 4 + t:5 + t], None, ALU.mult).then_inc(k_scaled, 1)
            split_past("iq1", 3)

            def normalise_q(i):
                for t in range(NT):
                    dve.wait_ge(qsq_done, NT * i + t + 1)
                    nc.vector.tensor_reduce(hsq[:, t, 4 * i:4 * i + 4],
                                            qn[:, t, 512 * i:512 * i + 512].rearrange("p (h d) -> p h d", h=4),
                                            X, ALU.add).then_inc(hsq_done, 1)
                for t in range(NT):
                    dve.wait_ge(head_rs, 2 + NT * i + t)
                    r = hrs[:, t, 4 * i:4 * i + 4].unsqueeze(2).to_broadcast([P, 4, HD])
                    tt(qn[:, t, 512 * i:512 * i + 512].rearrange("p (h d) -> p h d", h=4),
                       ps[:, 2 * i + t, :].rearrange("p (h d) -> p h d", h=4), r, ALU.mult).then_inc(qn_done, 1)

            n = 0
            for i in range(12):
                t, heads = indexer_heads(i)
                S = (t + 1) * P
                dve.wait_ge(relu_done, i + 1)
                for m, h in enumerate(heads):
                    start = n in (0, IH)
                    if not start:
                        dve.wait_ge(score_step, n)
                    last = stt(out=score[:, t, 0:S], in0=il_relu[:, i % 2, m * S:(m + 1) * S], scalar=iw_sb[:, t, h:h + 1],
                               in1=causal[:, SEQ - S:SEQ] if start else score[:, t, 0:S], op0=ALU.mult, op1=ALU.add)
                    last.then_inc(score_step, 1)
                    n += 1
                split_to(STREAM_END["iq1"] + SPLITS + i + 1, 3)
                if i == 9:
                    normalise_q(0)

            convolve(at[1], DVE_TAPS)
            dve.wait_ge(conv_step, DVE_TAPS)
            wait_job("mean")
            ts(mean_sb, ps[:, 6, 0:SEQ], 1.0 / CCH, None, ALU.mult).then_inc(ln_step, 1)
            dve.wait_ge(ln_step, 1)
            tt(conv, conv, mean_sb.unsqueeze(1).to_broadcast([P, CC, SEQ]), ALU.subtract).then_inc(ln_step, 1)

            dve.wait_ge(score_step, n)
            n = 0
            for r in range(TOPK // 8):
                for t in range(NT):
                    S = (t + 1) * P
                    src = picked if r else score
                    if r:
                        dve.wait_ge(topk_step, n - 2)
                    nc.vector.max(top8[:, t, :], src[:, t, 0:S]).then_inc(topk_step, 1)
                    n += 1
                    dve.wait_ge(topk_step, n)
                    nc.vector.match_replace(picked[:, t, 0:S], top8[:, t, :], src[:, t, 0:S], TAKEN).then_inc(topk_step, 1)
                    n += 1
                if r < 4:
                    split_to(STREAM_END["iq1"] + SPLITS + 12 + r + 1)
                if r == 4:
                    wait_job("var")
                    ts(rvar, ps[:, 7, 0:SEQ], 1.0 / CCH, EPS, ALU.mult, ALU.add).then_inc(ln_step, 1)
            dve.wait_ge(topk_step, n)
            for t in range(NT):
                S = (t + 1) * P
                ts(picked[:, t, 0:S], picked[:, t, 0:S], TAKEN, -NEG, ALU.is_equal, ALU.mult).then_inc(topk_step, 1)
            dve.wait_ge(topk_step, n + 2)
            for t in range(NT):
                S = (t + 1) * P
                stt(out=picked[:, t, 0:S], in0=picked[:, t, 0:S], scalar=NEG, in1=causal[:, SEQ - S:SEQ],
                    op0=ALU.add, op1=ALU.add).then_inc(topk_step, 1)
            dve.wait_ge(topk_step, n + 4)
            normalise_q(1)
            dve.wait_ge(ln_pool, 1)
            tt(conv, conv, rvar.unsqueeze(1).to_broadcast([P, CC, SEQ]), ALU.mult).then_inc(ln_step, 1)
            dve.wait_ge(bias_out, 1)
            for t, (dst, src) in enumerate(((logits0, bias_sb[:, :, P:SEQ]), (bias_sb, bias_sb))):
                S = (t + 1) * P
                tt(dst, src, picked[:, t, 0:S].unsqueeze(1).to_broadcast([P, HEADS, S]), ALU.add).then_inc(logit_step, 1)
                dve.wait_ge(logit_step, t + 1)

            flat0 = logits0.rearrange("p h s -> p (h s)")
            flat1 = bias_sb.rearrange("p h s -> p (h s)")
            dve.wait_ge(logit_step, 2)
            for t, (flat, lg, banks) in enumerate(((flat0, logits0, (0, 2)), (flat1, bias_sb, (2, 6)))):
                wait_job(f"lg{t}")
                src = ps[:, banks[0]:banks[1], :].rearrange("p b n -> p (b n)")
                stt(out=flat, in0=src, scalar=HD ** -0.5, in1=flat, op0=ALU.mult, op1=ALU.add).then_inc(logit_step, 1)
                dve.wait_ge(logit_step, 3 + 3 * t)
                nc.vector.tensor_reduce(hms[:, t, :], lg, X, ALU.max).then_inc(logit_step, 1)
                dve.wait_ge(logit_step, 4 + 3 * t)
                ts(smax[:, t, :], hms[:, t, :], -1.0, None, ALU.mult).then_inc(logit_step, 1)

            dve.wait_ge(th_conv_done, 1)
            stt(out=conv, in0=th_conv, scalar=1.0, in1=conv, op0=ALU.add, op1=ALU.mult).then_inc(conv_done, 1)
            dve.wait_ge(conv_hi_done, 1)
            low(convT[1], conv, convT[0]).then_inc(conv_done, 1)

            def add_x(n, t, bank):
                cols = x_sb[:, t, n * 512:(n + 1) * 512]
                tt(cols, ps[:, bank, :], cols, ALU.add).then_inc(x_added, 1)

            def normalise(t, lg):
                dve.wait_ge(exp_done, t + 1)
                nc.vector.reciprocal(srec[:, t, :], ssum[:, t, :]).then_inc(prob_step, 1)
                dve.wait_ge(prob_step, t + 1)
                tt(lg, lg, srec[:, t, :].unsqueeze(2).to_broadcast([P, HEADS, (t + 1) * P]), ALU.mult).then_inc(prob_done, 1)

            normalise(0, logits0)
            normalise(1, bias_sb)
            for n in range(4):
                split_past(f"wc{n}")
                wait_job(f"wc{n}")
                for t, bank in enumerate(BANKS[f"wc{n}"]):
                    add_x(n, t, bank)
            for i in range(4):
                t, hq = i // 2, i % 2
                part = (slice(None), slice(4 * hq, 4 * hq + 4), slice(t * P, (t + 1) * P))
                dve.wait_ge(oT_out, i + 1)
                low(attnT[1][part], ps[:, BANKS[f"oT{i}"][0], :].rearrange("p (h s) -> p h s", h=4), attnT[0][part]) \
                    .then_inc(attn_lo, 1)
            for n in range(4):
                split_past(f"wa{n}")
                wait_job(f"wa{n}")
                if n == 0:
                    dve.wait_ge(x_added, 8)
                for t, bank in enumerate(BANKS[f"wa{n}"]):
                    add_x(n, t, bank)
            dve.wait_ge(x_added, 16)
            tick_off().then_inc(x_ready, 1)

            def moe_dve(l):
                m = moe[l]
                norm(1 if l == 0 else 3, True)
                normed_channels(1 + l, 1 + l)
                steps = [0]

                def chain(ins):
                    steps[0] += 1
                    ins.then_inc(m["route_step"], 1)
                    dve.wait_ge(m["route_step"], steps[0])

                def first_max(dst, src, val):
                    chain(nc.vector.tensor_reduce(val, src, X, ALU.max))
                    chain(tt(t4a, src, val.to_broadcast([P, NT, 4]), ALU.is_equal))
                    chain(tt(t4a, t4a, prio.unsqueeze(1).to_broadcast([P, NT, 4]), ALU.mult))
                    chain(nc.vector.tensor_reduce(gmax, t4a, X, ALU.max))
                    chain(tt(dst, t4a, gmax.to_broadcast([P, NT, 4]), ALU.is_equal))

                col = lambda i: stat[:, i, :].unsqueeze(2)
                dve.wait_ge(m["router_done"], 1)
                src = ps[:, 2, 0:64].rearrange("p (t c) -> p t c", t=NT)[:, :, 0:20]
                chain(tt(lgt, src, router_b[:, l, :].unsqueeze(1).to_broadcast([P, NT, 20]), ALU.add))
                glog = lgt[:, :, 0:NG]
                chain(nc.vector.tensor_reduce(col(0), glog, X, ALU.max))
                chain(tt(oneh, glog, col(0).to_broadcast([P, NT, NG]), ALU.subtract))
                tick_off().then_inc(m["exp_in"], 1)
                dve.wait_ge(m["exp_out"], 1)
                chain(nc.vector.tensor_reduce(col(1), ex_g, X, ALU.add))
                chain(nc.vector.reciprocal(col(2), col(1)))
                first_max(oneh, glog, col(0))
                tick_off().then_inc(m["rank_in"], 1)
                p4 = prod.rearrange("p t (g e) -> p t g e", g=NG)
                chain(tt(p4, lgt[:, :, NG:20].rearrange("p t (g e) -> p t g e", g=NG),
                         oneh.unsqueeze(3).to_broadcast([P, NT, NG, EPG]), ALU.mult))
                chain(nc.vector.tensor_reduce(el, prod.rearrange("p t (g e) -> p t e g", g=NG), X, ALU.add))
                first_max(sel1, el, col(3))
                chain(stt(out=t4b, in0=sel1, scalar=NEG, in1=el, op0=ALU.mult, op1=ALU.add))
                first_max(sel2, t4b, col(4))
                chain(tt(el, el, col(3).to_broadcast([P, NT, EPG]), ALU.subtract))
                tick_off().then_inc(m["exp_in"], 1)
                chain(tt(sel1, sel1, sel2, ALU.add))
                dve.wait_ge(m["exp_out"], 2)
                chain(tt(wgt, ex_e, sel1, ALU.mult))
                chain(nc.vector.tensor_reduce(col(5), wgt, X, ALU.add))
                chain(nc.vector.reciprocal(col(6), col(5)))
                chain(tt(col(6), col(6), col(2), ALU.mult))
                chain(tt(wgt, wgt, col(6).to_broadcast([P, NT, EPG]), ALU.mult))
                chain(ts(wgt, wgt, 0.5, None, ALU.mult))
                c4 = comb[:, :, 0:NE].rearrange("p t (g e) -> p t g e", g=NG)
                chain(tt(c4, wgt.unsqueeze(2).to_broadcast([P, NT, NG, EPG]),
                         oneh.unsqueeze(3).to_broadcast([P, NT, NG, EPG]), ALU.mult))
                nc.vector.tensor_copy(comb[:, :, NE:2 * NE], comb[:, :, 0:NE])
                nc.vector.memset(comb[:, :, 2 * NE:], 0.0)
                dve.wait_ge(m["rank_done"], 1)
                rank = ps[:, BANK_T, 0:16].rearrange("p (t c) -> p t c", t=NT)[:, :, 0:NG]
                chain(stt(out=rank_in[:, :, 0:NG], in0=rank, scalar=1.0, in1=oneh, op0=ALU.add, op1=ALU.mult))
                chain(ts(rank_in[:, :, NG:2 * NG], rank_in[:, :, 0:NG], -1.0 - P, None, ALU.add))
                chain(ts(rank_in[:, :, 0:NG], rank_in[:, :, 0:NG], -1.0, None, ALU.add))
                nc.vector.memset(rank_in[:, :, 2 * NG:], -1.0)
                chain(nc.vector.tensor_reduce(cnt[:, 0:1], ps[:, BANK_T, 16:16 + NG], X, ALU.max))
                chain(ts(cnt[:, 1:2], cnt[:, 0:1], float(P), float(NG), ALU.is_gt, ALU.mult))
                chain(nc.vector.tensor_copy(npass_i[:, 2 * l + 1:2 * l + 2], cnt[:, 1:2]))
                chain(ts(cnt[:, 2:3], cnt[:, 1:2], float(NG), None, ALU.add))
                chain(nc.vector.tensor_copy(npass_i[:, 2 * l:2 * l + 1], cnt[:, 2:3]))
                tick_off().then_inc(m["x_moved"], 1)
                tick_off().then_inc(m["route_done"], 1)

                def pick_tokens(p):
                    nc.vector.tensor_copy(comb_now, comb[:, :, bass.ds(p * EPG, EPG)])
                    for t in range(NT):
                        last = ts(pick[:, t, :], slot_no, rank_in[:, t, bass.ds(p, 1)], None, ALU.is_equal)
                    last.then_inc(m["pick_ready"], 1)

                def slots_in(p, q):
                    dve.wait_ge(m["gathered"], p * 4 + (q + 1))
                    if q >= 2:
                        dve.wait_ge(m["gather_out"], p * 4 + (q - 1))
                    w = norm_cols[:, 1 + l, 4 * q:4 * q + 4].unsqueeze(2).to_broadcast([P, 4, P])
                    tt(slots_f[:, q % 2, :].rearrange("p (k s) -> p k s", k=4),
                       ps[:, GATHER_BANK[q], :].rearrange("p (k s) -> p k s", k=4), w, ALU.mult).then_inc(m["slots_in"], 1)

                def slots_lo(p, q):
                    dve.wait_ge(m["slots_hi"], p * 4 + (q + 1))
                    part = (slice(None), slice(4 * q, 4 * q + 4))
                    low(hgT[1][part], slots_f[:, q % 2, :].rearrange("p (k s) -> p k s", k=4), hgT[0][part]) \
                        .then_inc(m["gather_out"], 1)

                def normed_slots(p):
                    for q in range(4):
                        slots_in(p, q)
                        if q:
                            slots_lo(p, q - 1)
                    slots_lo(p, 3)

                pick_tokens(0)
                normed_slots(0)
                n = dve.value_load(npass_i[0:1, 2 * l:2 * l + 1], min_val=NG, max_val=2 * NG)
                with dve.Fori(0, n) as p:
                    def split(first, last):
                        for u in range(first, last):
                            dve.wait_ge(m["hi"], p * (2 * PASS_BLOCKS) + (u + 1))
                            low(split_lo[:, u % SPLITS, :], raw_half(moe_slot(l, u // 2), u % 2), split_hi[:, u % SPLITS, :]) \
                                .then_inc(m["lo"], 1)

                    def gate(e):
                        dve.wait_ge(m["th_gate_done"], p * EPG + (e + 1))
                        stt(out=gated[:, e % 2, :], in0=th_gate[:, e % 2, :], scalar=1.0, in1=ps[:, e % 2, :],
                            op0=ALU.add, op1=ALU.mult).then_inc(m["gated_done"], 1)

                    def times_up(e):
                        dve.wait_ge(m["gated_done"], p * EPG + (e + 1))
                        dve.wait_ge(m["misc_out"], p + 1)
                        unit_done(dve, l, p, e, "u")
                        by_j = lambda t: t.rearrange("p (j k) -> p j k", k=FC)
                        stt(out=act.rearrange("p (k j) -> p j k", k=FC), in0=by_j(gated[:, e % 2, :]),
                            scalar=comb_slot[:, e:e + 1], in1=by_j(ps[:, 2, :]), op0=ALU.mult, op1=ALU.mult) \
                            .then_inc(m["act_done"], 1)

                    def turned_lo(e):
                        dve.wait_ge(m["actT_hi"], p * EPG + (e + 1))
                        low(actT[1], ps[:, BANK_T, :].rearrange("p (k s) -> p k s", k=FC), actT[0]).then_inc(m["actT_out"], 1)

                    split(0, 13)
                    gate(0)
                    split(13, 20)
                    times_up(0)
                    for e in range(1, EPG):
                        at = 8 * UNITS.index((e, "g"))
                        split(at + 4, at + 10)
                        turned_lo(e - 1)
                        split(at + 10, at + 12)
                        if e == 1:
                            dve.wait_ge(m["misc_done"], p + 1)
                            pick_tokens(p + 1)
                        split(at + 12, at + 13)
                        gate(e)
                        if e < EPG - 1:
                            split(at + 13, at + 28)
                            times_up(e)
                    split(at + 13, 92)
                    times_up(EPG - 1)
                    slots_in(p + 1, 0)
                    slots_in(p + 1, 1)
                    slots_lo(p + 1, 0)
                    slots_in(p + 1, 2)
                    slots_lo(p + 1, 1)
                    slots_lo(p + 1, 2)
                    turned_lo(EPG - 1)
                    split(92, 94)
                    slots_in(p + 1, 3)
                    slots_lo(p + 1, 3)
                    split(94, 96)
                    for i in range(8):
                        t, b = i // 4, i % 4
                        dve.wait_ge(m["scattered"], p * 8 + (i + 1))
                        cols = x_sb[:, t, b * 512:(b + 1) * 512]
                        tt(cols, ps[:, BANK_Y + b, :], cols, ALU.add).then_inc(m["x_moved"], 1)
                dve.wait_ge(m["x_moved"], n * 8 + 1)
                tick_off().then_inc(x_ready, 1)

            moe_dve(0)

            norm(2, False)
            dve.wait_ge(scale_in, 32)
            for i in range(8):
                dve.wait_ge(dT_done, i + 1)
                w = vec_sb[:, V_POOL + 2 * i:V_POOL + 2 * i + 2].unsqueeze(2).to_broadcast([P, 2, SEQ])
                if i >= 2:
                    dve.wait_ge(dT_out, i - 1)
                if i == 0:
                    dve.wait_ge(dT_done, 8)
                pool3 = lambda j: pooled[:, j % 2, :].rearrange("p (c s) -> p c s", c=2)
                tt(pool3(i), ps[:, i, :].rearrange("p (c s) -> p c s", c=2), w, ALU.mult).then_inc(pooled_f, 1)
                for j in ([i - 1] if i else []) + ([7] if i == 7 else []):
                    dve.wait_ge(pooled_hi, j + 1)
                    low(dT[1][:, 2 * j:2 * j + 2, :], pool3(j), dT[0][:, 2 * j:2 * j + 2, :]).then_inc(dT_out, 1)
            for i in range(8):
                g, t = i // 2, i % 2
                for u in range(*((0, 4) if i == 0 else (i + 3, i + 4) if i <= 4 else (0, 0))):
                    dve.wait_ge(pool_hi, u + 1)
                    low(split_lo[:, u % SPLITS, :], raw_half((POOL0 + u // 2) % RING, u % 2), split_hi[:, u % SPLITS, :]) \
                        .then_inc(pool_lo, 1)
                dve.wait_ge(mix_done, i + 1)
                if i >= 2:
                    dve.wait_ge(mix_step, 2 * i - 2)
                tt(mixed[:, i % 2, :], ps[:, i, :], scale_bc[:, g * 512:(g + 1) * 512], ALU.mult).then_inc(mix_step, 1)
                dve.wait_ge(mix_step, 2 * i + 1)
                cols = x_sb[:, t, g * 512:(g + 1) * 512]
                tt(cols, mixed[:, i % 2, :], cols, ALU.add).then_inc(mix_step, 1)
            dve.wait_ge(mix_step, 16)
            tick_off().then_inc(x_ready, 1)

            moe_dve(1)

        @block.tensor
        def _(pe):
            mm = nc.tensor.matmul

            def turn(dst, src, n=P):
                return nc.tensor.transpose(dst, src, ident[0:n, 0:n])

            pe.wait_ge(const_in, 16 * 12)
            pe.wait_ge(rows_in, 16 * 10)
            pe.wait_ge(set_up, 1)
            turn(ps[:, 0, 0:V_ROWS], vec_rows[0:V_ROWS, 0, :], V_ROWS)
            for h in range(2):
                last = turn(ps[:, 0, 64 + h * CW_HALF:64 + (h + 1) * CW_HALF], vec_rows[0:CW_HALF, 1 + h, :], CW_HALF)
            last.then_inc(vec_done, 1)
            mm(ps[0:HEADS, 1, :], rel_sb, one_hot, start=True, stop=True).then_inc(vec_done, 1)
            pe.wait_ge(vec_out, 2)

            def turn_x(i, n):
                pe.wait_ge(xn_done, NT * (i + 1))
                for q in range(8):
                    t, kq = q // 4, q % 4
                    for k in range(4 * kq, 4 * kq + 4):
                        last = turn(ps[:, q, (k % 4) * P:(k % 4 + 1) * P], xn[:, t * D + k * P:t * D + (k + 1) * P])
                    last.then_inc(xT_done, 1)
                pe.wait_ge(xT_out, 8 * (n + 1))

            def start_job(name):
                for b in BANKS[name]:
                    if (owner := owner_before(name, b)) is not None:
                        signal, count = emptied(owner)
                        pe.wait_ge(signal, count)

            def product(out, stationary, moving, start, stop, **how):
                (sh, sl), (mh, ml) = stationary, moving
                mm(out, sh, mh, start=start, stop=False, **how)
                mm(out, sh, ml, start=False, stop=False, **how)
                return mm(out, sl, mh, start=False, stop=stop, **how)

            def pick_parts(parts, *index):
                return [part[index] for part in parts]

            ALL = slice(None)
            stream = [0]

            def next_unit(k, n, off=0):
                pe.wait_ge(mixer_lo, stream[0] + 1)
                slot = stream[0] % SPLITS
                stream[0] += 1
                return unit(slot, k, n)

            def unit(slot, k, n, off=0):
                return [w[:, slot, off:off + k * n].rearrange("p (k n) -> p k n", k=k) for w in (split_hi, split_lo)]

            def channels_job(name):
                start_job(name)
                for q in range(8):
                    w = next_unit(2, 512)
                    for k in range(2):
                        first, end = q == 0 and k == 0, q == 7 and k == 1
                        for c in range(4):
                            last = product(ps[:, BANKS[name][c // 2], (c % 2) * SEQ:(c % 2 + 1) * SEQ],
                                           pick_parts(w, ALL, k, slice(c * P, (c + 1) * P)), pick_parts(hT, ALL, 2 * q + k),
                                           first and c % 2 == 0, end, skip_group_check=True)
                    last.then_inc(mixer_used, 1)

            def tokens_job(name, between=lambda q: None):
                start_job(name)
                for q in range(8):
                    between(q)
                    w = next_unit(2, 512)
                    for k in range(2):
                        for t, b in enumerate(BANKS[name]):
                            last = product(ps[:, b, :], pick_parts(hT, ALL, 2 * q + k, slice(t * P, (t + 1) * P)),
                                           pick_parts(w, ALL, k), q == 0 and k == 0, q == 7 and k == 1)
                    last.then_inc(mixer_used, 1)

            def kvi_job():
                start_job("kvi")
                for q in range(8):
                    kv = next_unit(2, KVW)
                    ki = unit(q % SPLITS, 2, IKW, 2 * KVW)
                    for k in range(2):
                        first, end = q == 0 and k == 0, q == 7 and k == 1
                        for t in range(NT):
                            h = pick_parts(hT, ALL, 2 * q + k, slice(t * P, (t + 1) * P))
                            product(ps[:, 4 + t, 0:KVW], h, pick_parts(kv, ALL, k), first, end, skip_group_check=True)
                            last = product(ps[:, 4 + t, KVW:KVW + IKW], h, pick_parts(ki, ALL, k), False, end,
                                           skip_group_check=True)
                    last.then_inc(mixer_used, 1)

            def out_job(name, parts):
                start_job(name)
                for q in range(4):
                    w = next_unit(2, 512)
                    for k in range(2):
                        for t, b in enumerate(BANKS[name]):
                            last = product(ps[:, b, :], pick_parts(parts, ALL, 2 * q + k, slice(t * P, (t + 1) * P)),
                                           pick_parts(w, ALL, k), q == 0 and k == 0, q == 3 and k == 1)
                    last.then_inc(mixer_used, 1)

            turn_x(0, 0)
            for i in range(2):
                channels_job(f"a{i}")
                channels_job(f"g{i}")
            start_job("flip")
            pe.wait_ge(bias_loaded, 16)
            for c in range(4):
                last = mm(ps[:, c, :], upside, bias_up[:, 2 * c:2 * c + 2, :].rearrange("p h s -> p (h s)"),
                          start=True, stop=True)
            last.then_inc(job_done, 1)
            kvi_job()
            channels_job("iq0")
            start_job("kT")
            pe.wait_ge(k_scaled, 2)
            for t in range(NT):
                turn(ps[:, 0, t * P:(t + 1) * P], k_sb[:, t, :])
            for t in range(NT):
                last = turn(ps[:, 0, SEQ + t * P:SEQ + (t + 1) * P], ik2[:, t, :])
            last.then_inc(job_done, 1)
            channels_job("iq1")
            pe.wait_ge(iq_out, 2)
            pe.wait_ge(kT_out, 1)

            def indexer(i):
                start_job(f"il{i}")
                t, heads = indexer_heads(i)
                S = (t + 1) * P
                for m, h in enumerate(heads):
                    rows = slice((h % 2) * ID, (h % 2 + 1) * ID)
                    last = mm(ps[:, BANKS[f"il{i}"][0], m * S:(m + 1) * S], iqT[rows, h // 2, t * P:(t + 1) * P],
                              ikT[rows, 0:S], start=True, stop=True)
                last.then_inc(job_done, 1)

            def channel_sum(name, src):
                start_job(name)
                for c in range(CC):
                    last = mm(ps[:, BANKS[name][0], 0:SEQ], ones[:], src[:, c, :], start=(c == 0), stop=(c == CC - 1))
                last.then_inc(job_done, 1)

            def beside_q1(q):
                if q < 4:
                    indexer(8 + q)
                if q == 5:
                    pe.wait_ge(conv_step, DVE_TAPS)
                    pe.wait_ge(pool_step, 2 * len(POOL_CHUNKS) * TAPS)
                    channel_sum("mean", conv)

            tokens_job("q0", indexer)
            tokens_job("q1", beside_q1)
            pe.wait_ge(y_half, 1)
            channel_sum("var", vsq)
            for i in range(4):
                start_job(f"qT{i}")
                t, hq = i // 2, i % 2
                pe.wait_ge(qn_done, 2 * hq + t + 1)
                for h in range(4):
                    last = turn(ps[:, 4 + i, h * P:(h + 1) * P], qn[:, t, (4 * hq + h) * HD:(4 * hq + h + 1) * HD])
                last.then_inc(job_done, 1)
            for t in range(NT):
                start_job(f"lg{t}")
                S = (t + 1) * P
                per = 512 // S
                pe.wait_ge(qT_out, 2 * t + 2)
                for h in range(HEADS):
                    last = mm(ps[:, BANKS[f"lg{t}"][h // per], (h % per) * S:(h % per + 1) * S],
                              qT[:, h, t * P:(t + 1) * P], kT[:, 0:S], start=True, stop=True)
                last.then_inc(job_done, 1)
            pe.wait_ge(conv_done, 2)
            for n in range(4):
                out_job(f"wc{n}", convT)
            for i in range(6):
                start_job(f"pT{i}")
                t, st, hq = (0, 0, i) if i < 2 else (1, (i - 2) // 2, i % 2)
                pe.wait_ge(prob_done, t + 1)
                lg = (logits0, bias_sb)[t]
                for h in range(4):
                    last = turn(ps[:, BANKS[f"pT{i}"][0], h * P:(h + 1) * P], lg[:, 4 * hq + h, st * P:(st + 1) * P])
                last.then_inc(job_done, 1)
            for i in range(4):
                start_job(f"oT{i}")
                t, hq = i // 2, i % 2
                pe.wait_ge(pT_out, 2 + 4 * t)
                for st in range(t + 1):
                    probs = pT1[:, st, hq * 512:(hq + 1) * 512] if t else pT0[:, hq * 512:(hq + 1) * 512]
                    last = mm(ps[:, BANKS[f"oT{i}"][0], :], v_sb[:, st, :], probs, start=(st == 0), stop=(st == t))
                last.then_inc(job_done, 1)
            pe.wait_ge(attn_lo, 4)
            for n in range(4):
                out_job(f"wa{n}", attnT)

            def moe_pe(l):
                m = moe[l]
                turn_x(1 if l == 0 else 3, 1 + l)
                for t in range(NT):
                    for k in range(KC):
                        last = mm(ps[:, 2, 32 * t:32 * t + 20], hT32[:, k, t * P:(t + 1) * P], router_w[:, l, k, :],
                                  start=(k == 0), stop=(k == KC - 1))
                last.then_inc(m["router_done"], 1)
                pe.wait_ge(m["rank_in"], 1)
                mm(ps[:, BANK_T, 0:NG], before, oneh[:, 0, :], start=True, stop=True)
                mm(ps[:, BANK_T, 8:8 + NG], ones[:], oneh[:, 0, :], start=True, stop=False)
                mm(ps[:, BANK_T, 8:8 + NG], before, oneh[:, 1, :], start=False, stop=True)
                mm(ps[:, BANK_T, 16:16 + NG], ones[:], oneh[:, 0, :], start=True, stop=False)
                mm(ps[:, BANK_T, 16:16 + NG], ones[:], oneh[:, 1, :], start=False, stop=True).then_inc(m["rank_done"], 1)

                def gather(p, quads=range(4)):
                    pe.wait_ge(m["pick_ready"], p + 1)
                    for q in quads:
                        if q >= 2:
                            pe.wait_ge(m["slots_in"], p * 4 + (q - 1 if GATHER_BANK[q] == GATHER_BANK[q - 2] else q))
                        for k in range(4 * q, 4 * q + 4):
                            for t in range(NT):
                                last = mm(ps[:, GATHER_BANK[q], (k % 4) * P:(k % 4 + 1) * P],
                                          xn[:, t * D + k * P:t * D + (k + 1) * P], pick[:, t, :],
                                          start=(t == 0), stop=(t == NT - 1))
                        last.then_inc(m["gathered"], 1)

                pe.wait_ge(m["route_done"], 1)
                gather(0)
                pe.sem_inc(m["used"], SPLITS)
                n = pe.value_load(npass_i[0:1, 2 * l:2 * l + 1], min_val=NG, max_val=2 * NG)
                with pe.Fori(0, n) as p:
                    unit_no = [0]

                    def weights(k, n):
                        u = unit_no[0]
                        unit_no[0] += 1
                        pe.wait_ge(m["lo"], p * (2 * PASS_BLOCKS) + (u + 1))
                        return unit(u % SPLITS, k, n)

                    def project(bank, between=lambda q: None):
                        for q in range(8):
                            w = weights(2, 512)
                            for k in range(2):
                                last = product(ps[:, bank, :], pick_parts(hgT, ALL, 2 * q + k), pick_parts(w, ALL, k),
                                               q == 0 and k == 0, q == 7 and k == 1)
                            last.then_inc(m["used"], 1)
                            between(q)

                    def turn_act(e):
                        pe.wait_ge(m["act_done"], p * EPG + (e + 1))
                        if e == 0:
                            pe.wait_ge(m["misc_out"], p + 1)
                        if e == EPG - 1:
                            pe.wait_ge(m["slots_in"], p * 4 + 6)
                        for k in range(FC):
                            last = turn(ps[:, BANK_T, k * P:(k + 1) * P], act[:, k * P:(k + 1) * P])
                        last.then_inc(m["actT_done"], 1)

                    def down(e):
                        pe.wait_ge(m["actT_out"], p * EPG + (e + 1))
                        if e == 0:
                            pe.wait_ge(m["x_moved"], p * 8 + 1)
                        for k in range(FC):
                            for half in range(2):
                                w = weights(2, 512)
                                for n in range(2):
                                    last = product(ps[:, BANK_Y + 2 * half + n, :], pick_parts(actT, ALL, k),
                                                   pick_parts(w, ALL, n), e == 0 and k == 0, e == EPG - 1 and k == FC - 1)
                                last.then_inc(m["used"], 1)

                    pe.wait_ge(m["gather_out"], p * 4 + 4)
                    for t in range(NT):
                        turn(ps[:, BANK_T, t * P:(t + 1) * P], pick[:, t, :])
                    for t in range(NT):
                        last = mm(ps[:, BANK_T, SEQ:SEQ + EPG], pick[:, t, :], comb_now[:, t, :],
                                  start=(t == 0), stop=(t == NT - 1))
                    last.then_inc(m["misc_done"], 1)
                    for e, kind in UNITS:
                        if kind == "g":
                            project(e % 2, lambda q: turn_act(e - 1) if e and q == 5 else None)
                        elif kind == "u":
                            project(BANK_U)
                            if e == EPG - 1:
                                gather(p + 1, range(3))
                                turn_act(e)
                                gather(p + 1, range(3, 4))
                        else:
                            down(e)
                    for i in range(8):
                        t, b = i // 4, i % 4
                        if t == 0:
                            pe.wait_ge(m["y_out"], p * 4 + (b + 1))
                        else:
                            pe.wait_ge(m["x_moved"], p * 8 + (b + 2))
                        mm(ps[:, BANK_Y + b, :], pickT[:, t, :], y_sb[:, b * 512:(b + 1) * 512],
                           start=True, stop=True).then_inc(m["scattered"], 1)

            moe_pe(0)

            pe.wait_ge(xn_done, NT * 3)
            pe.wait_ge(scale_in, 32)
            for c in range(KC):
                bank, off, g = c // 2, (c % 2) * SEQ, c // 4
                mm(ps[:, bank, off:off + SEQ], xn[:, c * P:(c + 1) * P], band[:, 0, g * SEQ:(g + 1) * SEQ],
                   start=True, stop=False)
                last = mm(ps[:, bank, off + P:off + SEQ], xn[:, D + c * P:D + (c + 1) * P],
                          band[:, 1, g * SEQ + P:(g + 1) * SEQ], start=False, stop=True)
                if c % 2:
                    last.then_inc(dT_done, 1)
            for g in range(NG):
                for h in range(2):
                    pe.wait_ge(pool_lo, 2 * g + h + 1)
                pe.wait_ge(dT_out, 8 if g == 0 else 2 * g + 2)
                for t in range(NT):
                    for h in range(2):
                        w = unit((2 * g + h) % SPLITS, 2, 512)
                        for k in range(2):
                            last = product(ps[:, 2 * g + t, :], pick_parts(dT, ALL, 4 * g + 2 * h + k, slice(t * P, (t + 1) * P)),
                                           pick_parts(w, ALL, k), h == 0 and k == 0, h == 1 and k == 1)
                    last.then_inc(mix_done, 1)

            moe_pe(1)


def shape_constants():
    i = np.arange(P)
    before = (i[:, None] < i[None, :]).astype(np.float32)
    slots = np.broadcast_to(i.astype(np.float32), (P, P))
    s = np.arange(SEQ)
    causal = np.where(s[None, :] - P <= i[:, None], 0.0, NEG).astype(np.float32)
    prio = np.broadcast_to(np.array([4, 3, 2, 1, 0, 0, 0, 0], np.float32), (P, 8))
    const = np.concatenate([np.eye(P, dtype=np.float32), before, slots, causal, prio, np.eye(P, dtype=np.float32)[::-1]], axis=1)
    dist = np.maximum(255 - np.arange(512), 0)
    exact = BUCKETS // 2
    large = exact + (np.log(np.maximum(dist, 1).astype(np.float32) / exact) / np.float32(np.log(128 / exact))
                     * (BUCKETS - exact)).astype(np.int32)
    bucket = np.where(dist < exact, dist, np.minimum(large, BUCKETS - 1))
    one_hot = (np.arange(BUCKETS)[:, None] == bucket[None, :]).astype(np.float32)
    t = np.arange(SEQ)
    band = np.zeros((SEQ, NG, SEQ), np.float32)
    for g, w in enumerate(WINDOWS):
        d = t[None, :] - t[:, None]
        band[:, g] = np.where((d >= 0) & (d < w), 1.0 / np.minimum(t + 1, w)[None, :], 0.0) - (d == 0)
    band = band.reshape(NT, P, NG * SEQ).transpose(1, 0, 2)
    return {"const": np.ascontiguousarray(const), "one_hot": one_hot, "band": np.ascontiguousarray(band)}


def kernel(**inputs):
    import concourse.bacc as bacc
    from concourse.bass_utils import run_bass_kernel_spmd

    nc = bacc.Bacc("TRN2", target_bir_lowering=False, num_devices=1)
    arrays = {f"in_{n}": np.ascontiguousarray(v) for n, v in inputs.items()}
    arrays |= {f"in_{n}": v for n, v in shape_constants().items()}
    aps = {n[3:]: nc.dram_tensor(n, v.shape, mybir.dt.from_np(v.dtype), kind="ExternalInput").ap()
           for n, v in arrays.items()}
    aps["out"] = nc.dram_tensor("out_0", (1, SEQ, D), F32, kind="ExternalOutput").ap()
    build(nc, aps)
    r = run_bass_kernel_spmd(nc, [arrays], core_ids=[0])
    return r.results[0]["out_0"]
```

```python
from contextlib import ExitStack

import numpy as np

import concourse.bass as bass
from concourse import mybir

ALU = mybir.AluOpType
ACT = mybir.ActivationFunctionType
F32 = mybir.dt.float32
I32 = mybir.dt.int32
F32R = mybir.dt.float32r
X = mybir.AxisListType.X

P = 128
D = 2048
SEQ = 256
NT = SEQ // P
KC = D // P
HEADS, HD = 8, 128
IH, ID = 16, 64
TOPK = SEQ // 4
BUCKETS = 32
TAPS, CCH = 31, 1024
CC = CCH // P
PAD = TAPS - 1
WINDOWS = (2, 4, 8, 16)
NG, EPG = 4, 4
NE = NG * EPG
FF = 512
FC = FF // P
EPS = 1e-6
NEG = -1e30
TAKEN = -3e38

Q0 = 0
K0 = 1024
IQ0 = 1280
IK0 = 2304
GA0 = 2384
GG0 = 3408
KVW = 256
IKW = 80

RING = 8
BLK = 4 * 512
HALF = BLK // 2
SPLITS = 4
ROUND = NG * EPG * 12
PASS_BLOCKS = EPG * 12
UNITS = [(0, "g"), (0, "u"), (1, "g"), (0, "d"), (1, "u"), (2, "g"), (1, "d"), (2, "u"), (3, "g"), (2, "d"),
         (3, "u"), (3, "d")]
BANK_U, BANK_T, BANK_Y = 2, 3, 4
GATHER_BANK = (0, 1, 0, 1)
SCATTER_AT = (1, 3, 5, 7, 9, 11, 13, 14)
NPASS = 2 * NG + 1

V_CB, V_LG, V_LB, V_QN, V_KN = 0, CC, 2 * CC, 3 * CC, 3 * CC + 1
V_ROWS = 3 * CC + 2
CW_ROWS = TAPS * CC
CW_HALF = CW_ROWS // 2


def mixer0_jobs():
    jobs = [("kvi", (0, 1)), ("iq0", (4, 5)), ("kT", (6,)), ("iq1", (0, 1)), ("flip", (2, 3, 4, 5))]
    jobs += [(f"il{i}", (6 + i % 2,)) for i in range(12)]
    jobs += [("a0", (2, 3)), ("g0", (4, 5)), ("q0", (0, 1)), ("q1", (2, 3))]
    jobs += [(f"qT{i}", ((6, 7, 0, 1)[i],)) for i in range(4)]
    jobs += [("lg0", (6, 7)), ("lg1", (0, 1, 2, 3)), ("a1", (4, 5)), ("g1", (6, 7))]
    jobs += [(f"pT{i}", (i % 4,)) for i in range(6)]
    jobs += [(f"oT{i}", ((2, 3, 0, 1)[i],)) for i in range(4)]
    jobs += [("wa0", (2, 3)), ("wa1", (0, 1)), ("wa2", (4, 5)), ("wa3", (6, 7)), ("mean", (2,)), ("var", (3,)), ("rstd", (2,))]
    jobs += [("wc0", (0, 1)), ("wc1", (4, 5)), ("wc2", (6, 7)), ("wc3", (0, 1))]
    return jobs


JOBS = mixer0_jobs()
JOB_AT = {name: i for i, (name, _) in enumerate(JOBS)}
BANKS = dict(JOBS)


STREAM = [(name, 4) for name in ("kvi", "iq0", "iq1", "a0", "g0", "q0", "q1", "a1", "g1")]
STREAM += [(f"wa{n}", 2) for n in range(4)] + [(f"wc{n}", 2) for n in range(4)]
STREAM_END = {name: sum(2 * k for _, k in STREAM[:i + 1]) for i, (name, _) in enumerate(STREAM)}


def job_number(name):
    return sum(n not in STREAM_END for n, _ in JOBS[:JOB_AT[name] + 1])


def owner_before(name, bank):
    before = [n for n, banks in JOBS[:JOB_AT[name]] if bank in banks]
    return before[-1] if before else None


def indexer_heads(i):
    if i < 4:
        return 0, [8 * (i // 2) + 2 * m + i % 2 for m in range(4)]
    i -= 4
    return 1, [4 * (i // 2) + 2 * m + i % 2 for m in range(2)]


def build(nc, a):
    x_in, out = a["x"], a["out"]
    ctx = ExitStack()
    with ctx:
        def sb(name, shape, dt=F32):
            return ctx.enter_context(nc.sbuf_tensor(name, shape, dt))

        def sem(name):
            return ctx.enter_context(nc.semaphore(name))

        x_sb = sb("x_sb", [P, NT, D])
        xn = sb("xn", [P, NT * D])
        split_hi = sb("split_hi", [P, SPLITS, HALF], F32R)
        split_lo = sb("split_lo", [P, SPLITS, HALF], F32R)
        cat = sb("cat", [P, 4 * D], F32R)
        ring = sb("ring", [P, RING, BLK])
        const_sb = sb("const_sb", [P, 4 * P + SEQ + 8])
        vec_sb = sb("vec_sb", [P, V_ROWS])
        cw_sb = sb("cw_sb", [P, CW_ROWS])
        router_w = sb("router_w", [P, KC, 20])
        router_b = sb("router_b", [P, 20])
        ones = sb("ones", [P, P])
        sumsq = sb("sumsq", [P, 4, NT])
        part_sq = sb("part_sq", [P, 4, NT, 4])
        meansq = sb("meansq", [P, 4, NT])
        rstd = sb("rstd", [P, 4, NT])
        minus_half = sb("minus_half", [P, 8])
        tick = sb("tick", [P, 24])
        upside = const_sb[:, 3 * P + SEQ + 8:]
        ident = const_sb[:, 0:P]
        before = const_sb[:, P:2 * P]
        slot_no = const_sb[:, 2 * P:3 * P]
        causal = const_sb[:, 3 * P:3 * P + SEQ]
        prio = const_sb[:, 3 * P + SEQ:3 * P + SEQ + 4]

        pickT = sb("pickT", [P, NT, P], F32R)

        WORK = 9968
        work = sb("work", [P, WORK])

        def cut(at, *shape):
            n = int(np.prod(shape))
            assert at + n <= WORK, (at, n)
            flat = work[:, at:at + n]
            if len(shape) == 2:
                flat = flat.rearrange("p (a b) -> p a b", b=shape[1])
            if len(shape) == 3:
                flat = flat.rearrange("p (a b c) -> p a b c", b=shape[1], c=shape[2])
            return flat, at + n

        STAGES = 3
        GAIN_AT = CC * (PAD + SEQ) + CC * SEQ
        gain, _ = cut(GAIN_AT, D)
        uT, o = cut(0, CC, PAD + SEQ)
        conv, o = cut(o, CC, SEQ)
        iqT, o = cut(o, CC, SEQ)
        ikT, o = cut(o, SEQ)
        kT, o = cut(o, SEQ)
        v_sb, o = cut(o, NT, P)
        k_sb, o = cut(o, NT, P)
        ik2, o = cut(o, NT, P)
        iw_sb, o = cut(o, NT, IH)
        il_relu, o = cut(o, 2, 512)
        tap_out = k_sb.rearrange("p t d -> p (t d)").rearrange("p (i s) -> p i s", s=SEQ)
        tap_out2 = ik2.rearrange("p t d -> p (t d)")
        score, o = cut(o, NT, SEQ)
        picked, o = cut(o, NT, SEQ)
        top8, o = cut(o, NT, 8)
        ksq, o = cut(o, 8)
        hsq, o = cut(o, NT, HEADS)
        hms, o = cut(o, NT, HEADS)
        hrs, o = cut(o, NT, HEADS)
        smax, o = cut(o, NT, HEADS)
        ssum, o = cut(o, NT, HEADS)
        srec, o = cut(o, NT, HEADS)
        bias_sb = xn[:, NT * HEADS * HD:].rearrange("p (h s) -> p h s", h=HEADS)
        logits0 = il_relu.rearrange("p a b -> p (a b)").rearrange("p (h s) -> p h s", h=HEADS)
        bias_up = uT.rearrange("p a b -> p (a b)")[:, 0:HEADS * SEQ].rearrange("p (h s) -> p h s", h=HEADS)
        th_glu = logits0.rearrange("p h s -> p (h s)").rearrange("p (c s) -> p c s", s=SEQ)
        th_conv = uT.rearrange("p a b -> p (a b)")[:, 0:CC * SEQ].rearrange("p (h s) -> p h s", h=CC)
        mean_sb = il_relu[:, 0, 0:SEQ]
        rvar = top8[:, 0, 0:NT]
        rstd_conv = top8[:, 0, NT:2 * NT]
        rstd_diag = il_relu[:, 1, 0:SEQ].rearrange("p (t s) -> p t s", t=NT)
        vsq = iqT
        products = [tap_out[:, 0, :], tap_out2, il_relu[:, 0, SEQ:], il_relu[:, 1, SEQ:]]
        qn = xn[:, 0:NT * HEADS * HD].rearrange("p (t c) -> p t c", t=NT)
        qT = iqT
        pT0 = qn.rearrange("p t c -> p (t c)")[:, 0:HEADS * P]
        pT1 = iqT.rearrange("p a b -> p (a b)").rearrange("p (s c) -> p s c", s=2)

        def cat_cut(at, a, b):
            return [cat[:, at + i * a * b:at + (i + 1) * a * b].rearrange("p (a b) -> p a b", b=b) for i in range(2)]

        hT = cat_cut(0, KC, SEQ)
        convT = cat_cut(0, CC, SEQ)
        attnT = cat_cut(2 * D, HEADS, SEQ)
        dT = cat_cut(0, KC, SEQ)
        hgT = cat_cut(0, KC, P)
        actT = cat_cut(2 * D, FC, P)
        y = [cat[:, (2 + i) * D:(3 + i) * D] for i in range(2)]

        scale_bc = gain
        next_gain, o2 = cut(0, D)
        mixed, o2 = cut(o2, 2, 512)
        band, _ = cut(GAIN_AT + D + STAGES * 512, NT, 4 * SEQ)

        hT32, _ = cut(0, KC, SEQ)
        stage, end = cut(GAIN_AT + D, STAGES, 512)
        th_gate, o3 = cut(0, 2, 512)
        gated, o3 = cut(o3, 2, 512)
        act, o3 = cut(o3, 512)
        pick, o3 = cut(o3, NT, P)
        comb_now, o3 = cut(o3, NT, EPG)
        comb_slot, o3 = cut(o3, EPG)
        lgt, o3 = cut(o3, NT, 20)
        oneh, o3 = cut(o3, NT, NG)
        sel1, o3 = cut(o3, NT, NG)
        sel2, o3 = cut(o3, NT, NG)
        t4a, o3 = cut(o3, NT, NG)
        t4b, o3 = cut(o3, NT, NG)
        el, o3 = cut(o3, NT, EPG)
        ex_g, o3 = cut(o3, NT, NG)
        ex_e, o3 = cut(o3, NT, EPG)
        wgt, o3 = cut(o3, NT, EPG)
        prod, o3 = cut(o3, NT, NE)
        comb, o3 = cut(o3, NT, NPASS * EPG)
        rank_in, o3 = cut(o3, NT, NPASS)
        gmax, o3 = cut(o3, NT, 1)
        stat, o3 = cut(o3, 8, NT)
        cnt, o3 = cut(o3, NG)
        assert o3 <= GAIN_AT
        vec_rows = conv.rearrange("p a b -> p (a b)")[:, 0:3 * P].rearrange("p (a b) -> p a b", a=3)
        one_hot = conv.rearrange("p a b -> p (a b)")[0:BUCKETS, 512:1024]
        rel_sb = conv.rearrange("p a b -> p (a b)")[0:BUCKETS, 1024:1024 + HEADS]
        bias_row = conv.rearrange("p a b -> p (a b)")[0:HEADS, 1536:2048]
        npass_i = sb("npass_i", [P, 4], I32)

        ps = ctx.enter_context(nc.psum_tensor("ps", [P, 8, 512], F32))
        bias_dram = nc.dram_tensor("bias_dram", [HEADS, 512], F32, kind="Internal").ap()

        DVE_CHUNKS = ((0, 1), (4, 5))
        POOL_CHUNKS, SHARED_CHUNKS = (3, 2), (6, 7)
        DVE_TAPS = 4 * TAPS
        POOL_STEPS = 2 * TAPS * len(POOL_CHUNKS)
        SHARED_TAPS = TAPS * len(SHARED_CHUNKS)

        router_in = sem("router_in")
        rows_in = sem("rows_in")
        x_loaded = [sem(f"x_loaded{t}") for t in range(NT)]
        scale_in = sem("scale_in")
        band_in = sem("band_in")
        next_gain_in = sem("next_gain_in")
        bias_stored = sem("bias_stored")
        bias_loaded = sem("bias_loaded")
        bias_out = sem("bias_out")
        x_stored = sem("x_stored")
        down_started = sem("down_started")
        set_up = sem("set_up")
        vec_done = sem("vec_done")
        vec_out = sem("vec_out")
        sq_done = sem("sq_done")
        sum_done = sem("sum_done")
        ms_done = sem("ms_done")
        rstd_done = sem("rstd_done")
        xn_done = sem("xn_done")
        xT_done = sem("xT_done")
        xT_out = sem("xT_out")
        job_done = sem("job_done")
        th_done = sem("th_done")
        u_done = sem("u_done")
        conv_step = sem("conv_step")
        pool_step = sem("pool_step")
        kvi_out = sem("kvi_out")
        k_scaled = sem("k_scaled")
        kT_out = sem("kT_out")
        iq_out = sem("iq_out")
        head_ms = sem("head_ms")
        head_rs = sem("head_rs")
        relu_done = sem("relu_done")
        score_step = sem("score_step")
        topk_step = sem("topk_step")
        qsq_done = sem("qsq_done")
        hsq_done = sem("hsq_done")
        qn_done = sem("qn_done")
        qT_out = sem("qT_out")
        logit_step = sem("logit_step")
        exp_done = sem("exp_done")
        prob_step = sem("prob_step")
        prob_done = sem("prob_done")
        pT_out = sem("pT_out")
        oT_out = sem("oT_out")
        attn_lo = sem("attn_lo")
        ln_step = sem("ln_step")
        ln_pool = sem("ln_pool")
        th_conv_done = sem("th_conv_done")
        conv_done = sem("conv_done")
        x_added = sem("x_added")
        dT_done = sem("dT_done")
        dT_out = sem("dT_out")
        mix_done = sem("mix_done")
        mix_step = sem("mix_step")
        mixer_in = [sem(f"mixer_in{s}") for s in range(RING)]
        mixer_hi = sem("mixer_hi")
        mixer_lo = sem("mixer_lo")
        mixer_used = sem("mixer_used")
        pool_hi = sem("pool_hi")
        pool_lo = sem("pool_lo")
        normed_hi = sem("normed_hi")
        conv_hi = sem("conv_hi")
        conv_lo = sem("conv_lo")
        ident_in = sem("ident_in")
        gain_in = sem("gain_in")
        tap_made = sem("tap_made")
        diag_done = sem("diag_done")
        gained = sem("gained")
        squared = sem("squared")
        pooled_hi = sem("pooled_hi")
        pool_in = [sem(f"pool_in{s}") for s in range(NG)]
        moe = []
        for l in range(2):
            moe.append({n: sem(f"{n}_{l}") for n in (
                "router_done", "route_step", "exp_out", "exp_in", "rank_done", "route_done", "pick_ready", "gathered", "gather_out",
                "rank_in", "misc_done", "misc_out", "th_gate_done", "gated_done", "act_done",
                "actT_done", "actT_out", "slots_hi",
                "actT_hi", "staged", "y_hi", "y_lo", "scattered", "x_moved", "hi", "lo", "used")})
            moe[l]["in"] = [sem(f"moe_in{l}_{s}") for s in range(RING)]

        w_in = a["w_in_e"][0].rearrange("(p k) n -> p k n", k=KC)
        w_out = a["w_out_e"][0].rearrange("(c p) n -> p c n", p=P)

        def in_block(kq, col, n):
            return lambda slot: [(ring[:, slot, 0:4 * n].rearrange("p (k n) -> p k n", k=4),
                                  w_in[:, 4 * kq:4 * kq + 4, col:col + n])]

        def kvi_block(kq):
            def parts(slot):
                out = []
                for h in range(2):
                    rows = slice(4 * kq + 2 * h, 4 * kq + 2 * h + 2)
                    mid, end = h * HALF + 2 * KVW, h * HALF + 2 * (KVW + IKW)
                    out.append((ring[:, slot, h * HALF:mid].rearrange("p (k n) -> p k n", k=2), w_in[:, rows, K0:K0 + KVW]))
                    out.append((ring[:, slot, mid:end].rearrange("p (k n) -> p k n", k=2), w_in[:, rows, IK0:IK0 + IKW]))
                return out
            return parts

        def out_block(cq, n):
            return lambda slot: [(ring[:, slot, :].rearrange("p (k n) -> p k n", k=4),
                                  w_out[:, 4 * cq:4 * cq + 4, n * 512:n * 512 + 512])]

        mixer_blocks = [kvi_block(kq) for kq in range(4)]
        for col in (IQ0, IQ0 + 512, GA0, GG0, Q0, Q0 + 512, GA0 + 512, GG0 + 512):
            mixer_blocks += [in_block(kq, col, 512) for kq in range(4)]
        for half in (0, 2):
            mixer_blocks += [out_block(half + q, n) for n in range(4) for q in range(2)]
        NMIX = len(mixer_blocks)
        MOE0 = [NMIX, NMIX + ROUND + NG]
        POOL0 = NMIX + ROUND
        kvi_at = range(4)

        def mixer_landed(b):
            return 16 * sum(4 if c in kvi_at else 1 for c in range(b % RING, b + 1, RING))

        def raw_half(slot, half, n=HALF):
            return ring[:, slot, half * HALF:half * HALF + n]

        def moe_source(l, g, j):
            e, kind = UNITS[j // 4]
            name, rows = {"g": ("w_gate", KC), "u": ("w_up", KC), "d": ("w_down", FC)}[kind]
            w = a[name][l].rearrange("e (p k) n -> p e (k n)", k=rows)
            return w[:, bass.ds(g * EPG + e, 1), (j % 4) * BLK:(j % 4 + 1) * BLK]

        def unit_done(eng, l, p, e, kind):
            eng.wait_ge(moe[l]["used"], p * (2 * PASS_BLOCKS) + (8 * (UNITS.index((e, kind)) + 1) + SPLITS))

        def moe_slot(l, j):
            return (MOE0[l] + j) % RING

        def wait_for_job(eng, name):
            if name in STREAM_END:
                eng.wait_ge(mixer_used, STREAM_END[name])
            else:
                eng.wait_ge(job_done, job_number(name))

        heads_before = [0]
        for i in range(12):
            heads_before.append(heads_before[-1] + len(indexer_heads(i)[1]))

        def emptied(name):
            kind, i = name.rstrip("0123456789"), int(name[-1] if name[-1].isdigit() else 0)
            if name in ("il10", "il11"):
                i = int(name[2:])
            return {"a": (u_done, i + 1), "g": (th_done, i + 1), "flip": (bias_out, 1), "kvi": (k_scaled, 2), "iq": (iq_out, i + 1),
                    "kT": (kT_out, 1), "il": (relu_done, i + 1), "q": (qn_done, 2 * i + 2), "qT": (qT_out, i + 1),
                    "lg": (logit_step, 3 + 3 * i), "mean": (ln_step, 1), "var": (ln_step, 4), "rstd": (ln_step, 8),
                    "wa": (x_added, 2 * i + 2), "wc": (x_added, 2 * i + 10), "pT": (pT_out, i + 1),
                    "oT": (attn_lo, i + 1)}[kind]

        def load_router(eng, l):
            for cols, name in ((slice(0, NG), "group"), (slice(NG, 20), "expert")):
                eng.dma_start(router_w[:, :, cols], a[f"router_{name}_w"][l].rearrange("(p k) g -> p k g", k=KC)) \
                    .then_inc(router_in, 16)
                eng.dma_start(router_b[:, cols], a[f"router_{name}_b"][l:l + 1, :].partition_broadcast(P)) \
                    .then_inc(router_in, 16)

        block = ctx.enter_context(nc.Block())

        @block.sync
        def _(sp):
            for t in range(NT):
                sp.dma_start(x_sb[:, t, :], x_in[0, t * P:(t + 1) * P, :]).then_inc(x_loaded[t], 16)
            sp.dma_start(gain, a["mix_norm_e"].partition_broadcast(P)).then_inc(gain_in, 16)

            def small_loads():
                for dst, name in ((rel_sb, "rel_bias"), (one_hot, "one_hot")):
                    sp.dma_start(dst, a[name]).then_inc(rows_in, 16)
                row = lambda name, n: a[name][0].rearrange("(c p) -> c p", p=P)
                for at, src, n in ((V_CB, row("conv_b_e", CC), CC), (V_LG, row("conv_ln_g_e", CC), CC),
                                   (V_LB, row("conv_ln_b_e", CC), CC), (V_QN, a["q_norm_e"], 1),
                                   (V_KN, a["k_norm_e"], 1)):
                    sp.dma_start(vec_rows[at:at + n, 0, :], src).then_inc(rows_in, 16)
                taps = a["conv_w_e"][0].rearrange("w (c p) -> (w c) p", p=P)
                for h in range(2):
                    sp.dma_start(vec_rows[0:CW_HALF, 1 + h, :], taps[h * CW_HALF:(h + 1) * CW_HALF, :]).then_inc(rows_in, 16)
                load_router(sp, 0)

            for b, parts in enumerate(mixer_blocks):
                s = b % RING
                if b == RING:
                    small_loads()
                if b >= RING:
                    sp.wait_ge(mixer_lo, 2 * (b - RING + 1))
                for dst, src in parts(s):
                    sp.dma_start(dst, src).then_inc(mixer_in[s], 16)

            def load_moe(l, g, j):
                sp.dma_start(ring[:, moe_slot(l, j):moe_slot(l, j) + 1, :], moe_source(l, g, j)) \
                    .then_inc(moe[l]["in"][moe_slot(l, j)], 16)

            def stream_round(l, base):
                split = moe[l]["lo"]
                with sp.Fori(0, NG - 1) as g:
                    for j in range(RING, PASS_BLOCKS):
                        sp.wait_ge(split, g * (2 * PASS_BLOCKS) + 2 * (base + j - RING + 1))
                        if UNITS[j // 4] == (0, "d") and j % 4 == 0:
                            sp.sem_inc(down_started, 1)
                        load_moe(l, g, j)
                    for j in range(RING):
                        sp.wait_ge(split, g * (2 * PASS_BLOCKS) + 2 * (base + PASS_BLOCKS + j - RING + 1))
                        load_moe(l, g + 1, j)
                for j in range(RING, PASS_BLOCKS):
                    sp.wait_ge(split, 2 * ((NG - 1) * PASS_BLOCKS + base + j - RING + 1))
                    load_moe(l, NG - 1, j)

            for l in range(2):
                for j in range(RING):
                    owner = MOE0[l] + j - RING
                    if l == 0:
                        sp.wait_ge(mixer_lo, 2 * (owner + 1))
                    elif owner < POOL0:
                        sp.wait_ge(moe[0]["lo"], splits_more + 2 * (owner - MOE0[0] + 1))
                    else:
                        sp.wait_ge(pool_lo, 2 * (owner - POOL0 + 1))
                    load_moe(l, 0, j)
                stream_round(l, 0)
                sp.wait_ge(moe[l]["route_done"], 1)
                more = sp.value_load(npass_i[0:1, 2 * l + 1:2 * l + 2], min_val=0, max_val=NG)
                with sp.If(more > 0):
                    for j in range(RING):
                        sp.wait_ge(moe[l]["lo"], 2 * (ROUND + j - RING + 1))
                        load_moe(l, 0, j)
                    stream_round(l, ROUND)
                if l == 0:
                    splits_more = more * (2 * PASS_BLOCKS)
                    for g in range(NG):
                        sp.wait_ge(moe[0]["lo"], splits_more + 2 * (ROUND - RING + g + 1))
                        sp.dma_start(ring[:, (POOL0 + g) % RING, :].rearrange("p (k n) -> p k n", k=4),
                                     a["pool_w_o"][0, g].rearrange("(k p) n -> p k n", p=P)) \
                            .then_inc(pool_in[g], 16)
                else:
                    for i in range(8):
                        t, b = i // 4, i % 4
                        sp.wait_ge(moe[1]["x_moved"], more * 8 + (8 * (NG - 1) + i + 2))
                        cols = slice(b * 512, (b + 1) * 512)
                        sp.dma_start(out[0, t * P:(t + 1) * P, cols], x_sb[:, t, cols]).then_inc(x_stored, 16)
            sp.wait_ge(x_stored, 16 * 8)

        @block.gpsimd
        def _(pool):
            def root(i):
                pool.wait_ge(sum_done, i + 1)
                nc.gpsimd.tensor_scalar(meansq[:, i], sumsq[:, i], 1.0 / D, EPS, ALU.mult, ALU.add) \
                    .then_inc(ms_done, 1)
                pool.wait_ge(ms_done, i + 1)
                nc.gpsimd.tensor_tensor(rstd[:, i], meansq[:, i], minus_half[:, 0:NT], ALU.pow) \
                    .then_inc(rstd_done, 1)

            def head_root(n, dst, tmp, src, width):
                nc.gpsimd.tensor_scalar(tmp, src, 1.0 / HD, EPS, ALU.mult, ALU.add).then_inc(head_ms, 1)
                pool.wait_ge(head_ms, n + 1)
                nc.gpsimd.tensor_tensor(dst, tmp, minus_half[:, 0:width], ALU.pow).then_inc(head_rs, 1)

            pool.wait_ge(set_up, 1)
            root(0)
            steps = [0]

            def step(ins):
                ins.then_inc(pool_step, 1)
                steps[0] += 1

            def convolve(c, first, last):
                times = lambda w: step(nc.gpsimd.tensor_tensor(
                    (tap_out[:, 0, :], tap_out2)[w % 2], uT[:, c, w:w + SEQ],
                    cw_sb[:, w * CC + c:w * CC + c + 1].to_broadcast([P, SEQ]), ALU.mult))
                pool.wait_ge(u_done, c // 4 + 1)
                times(first)
                for w in range(first, last):
                    if w + 1 < last:
                        if w > first:
                            pool.wait_ge(pool_step, steps[0])
                        times(w + 1)
                    pool.wait_ge(pool_step, steps[0] - (w + 1 < last))
                    before = conv[:, c, :] if w else vec_sb[:, V_CB + c:V_CB + c + 1].to_broadcast([P, SEQ])
                    step(nc.gpsimd.tensor_tensor(conv[:, c, :], (tap_out[:, 0, :], tap_out2)[w % 2], before, ALU.add))
                pool.wait_ge(pool_step, steps[0])

            pool.wait_ge(kvi_out, 2)
            head_root(0, ksq[:, 4:6], ksq[:, 2:4], ksq[:, 0:2], 2)
            pool.wait_ge(vec_out, 1)
            for i in range(2):
                convolve(POOL_CHUNKS[0], 16 * i, (16, TAPS)[i])
                for t in range(NT):
                    pool.wait_ge(hsq_done, NT * i + t + 1)
                    heads = slice(4 * i, 4 * i + 4)
                    head_root(1 + NT * i + t, hrs[:, t, heads], hms[:, t, heads], hsq[:, t, heads], 4)
            convolve(POOL_CHUNKS[1], 0, TAPS)
            for n in range(SHARED_TAPS):
                c, w = SHARED_CHUNKS[n % 2], n // 2
                pool.wait_ge(tap_made, n + 1)
                if w:
                    pool.wait_ge(pool_step, steps[0] - 1)
                before = conv[:, c, :] if w else vec_sb[:, V_CB + c:V_CB + c + 1].to_broadcast([P, SEQ])
                step(nc.gpsimd.tensor_tensor(conv[:, c, :], products[n % 4], before, ALU.add))
            pool.wait_ge(ln_step, 4)
            nc.gpsimd.tensor_tensor(rstd_conv, rvar, minus_half[:, 0:NT], ALU.pow).then_inc(ln_pool, 1)

            def add_passes(l):
                m = moe[l]
                pool.wait_ge(m["route_done"], 1)
                n = pool.value_load(npass_i[0:1, 2 * l:2 * l + 1], min_val=NG, max_val=2 * NG)
                with pool.Fori(1, n) as p:
                    for i in range(8):
                        t, b = i // 4, i % 4
                        pool.wait_ge(m["staged"], (p - 1) * 8 + (i + 1))
                        cols = x_sb[:, t, b * 512:(b + 1) * 512]
                        nc.gpsimd.tensor_tensor(cols, stage[:, i % STAGES, :], cols, ALU.add).then_inc(m["x_moved"], 1)

            root(1)
            add_passes(0)
            root(2)
            root(3)
            add_passes(1)

        @block.scalar
        def _(act):
            def copy(out, in_, scale=1.0):
                return nc.scalar.activation(out, in_, ACT.Copy, scale=scale)

            act.dma_start(const_sb[:], a["const"]).then_inc(ident_in, 16)

            def norm(i, blocks):
                for t, b, signal, count in blocks:
                    act.wait_ge(signal, count)
                    nc.scalar.activation(xn[:, t * D + b * 512:t * D + (b + 1) * 512], x_sb[:, t, b * 512:(b + 1) * 512],
                                         ACT.Square, accum_out=part_sq[:, i, t, b:b + 1]).then_inc(sq_done, 1)

            def load_gain(i, row):
                act.wait_ge(xn_done, 4 * i)
                act.dma_start(gain, row.partition_broadcast(P)).then_inc(gain_in, 16)

            norm(0, [(t, b, x_loaded[t], 16) for t in range(NT) for b in range(4)])

            def wait_job(name):
                wait_for_job(act, name)

            at = [0]

            def split_to(end):
                for u in range(at[0], end):
                    b, n = u // 2, 2 * (KVW + IKW) if u // 2 in kvi_at else HALF
                    if u % 2 == 0:
                        act.wait_ge(mixer_in[b % RING], mixer_landed(b))
                    if u >= SPLITS:
                        act.wait_ge(mixer_used, u - SPLITS + 1)
                    copy(split_hi[:, u % SPLITS, 0:n], raw_half(b % RING, u % 2, n)).then_inc(mixer_hi, 1)
                at[0] = end

            def split_past(name, more):
                split_to(STREAM_END[name] + more)

            for q in range(8):
                t, kq = q // 4, q % 4
                act.wait_ge(xT_done, q + 1)
                copy(hT[0][:, 4 * kq:4 * kq + 4, t * P:(t + 1) * P],
                     ps[:, q, :].rearrange("p (k s) -> p k s", k=4)).then_inc(normed_hi, 1)
            split_to(6)
            act.wait_ge(vec_done, 1)
            copy(vec_sb[:, 0:V_LG], ps[:, 2, 0:V_LG])
            copy(vec_sb[:, V_LG:V_QN], ps[:, 2, V_LG:V_QN], 0.5)
            copy(vec_sb[:, V_QN:V_ROWS], ps[:, 2, V_QN:V_ROWS])
            copy(cw_sb[:], ps[:, 2, 64:64 + CW_ROWS], 0.5).then_inc(vec_out, 1)
            act.wait_ge(vec_done, 2)
            copy(bias_row, ps[0:HEADS, 3, :]).then_inc(vec_out, 1)
            act.wait_ge(vec_out, 2)
            act.dma_start(bias_dram, bias_row).then_inc(bias_stored, 16)

            split_past("kvi", 1)
            wait_job("kvi")
            copy(v_sb, ps[:, 0:2, P:2 * P])
            for h in range(2):
                copy(ik2[:, :, h * ID:(h + 1) * ID], ps[:, 0:2, KVW:KVW + ID])
            copy(iw_sb, ps[:, 0:2, KVW + ID:KVW + IKW], IH ** -0.5 * ID ** -0.5).then_inc(kvi_out, 1)
            for t in range(NT):
                sq = nc.scalar.activation(il_relu[:, t, 0:P], ps[:, t, 0:P], ACT.Square, accum_out=ksq[:, t:t + 1])
            sq.then_inc(kvi_out, 1)
            split_past("kvi", 4)
            act.wait_ge(bias_stored, 16)
            act.dma_start(bias_up, bass.AP(tensor=bias_dram.tensor, offset=0,
                                           ap=[[1, P], [512, HEADS], [1, SEQ]])).then_inc(bias_loaded, 16)
            split_past("kvi", 5)
            wait_job("kT")
            copy(kT, ps[:, 6, 0:SEQ], vec_sb[:, V_KN:V_KN + 1])
            copy(ikT, ps[:, 6, SEQ:2 * SEQ]).then_inc(kT_out, 1)

            def iq_copy(i):
                wait_job(f"iq{i}")
                first = BANKS[f"iq{i}"][0]
                copy(iqT[:, 4 * i:4 * i + 4, :].rearrange("p c s -> p (c s)"),
                     ps[:, first:first + 2, :].rearrange("p b n -> p (b n)")).then_inc(iq_out, 1)

            split_past("iq0", 1)
            iq_copy(0)
            split_past("iq0", 6)
            wait_job("flip")
            copy(bias_sb.rearrange("p h s -> p (h s)"), ps[:, 2:6, :].rearrange("p b n -> p (b n)")).then_inc(bias_out, 1)
            split_past("iq1", 1)
            iq_copy(1)
            for i in range(12):
                split_past("iq1", 3 + i)
                wait_job(f"il{i}")
                if i >= 2:
                    act.wait_ge(score_step, heads_before[i - 1])
                nc.scalar.activation(il_relu[:, i % 2, :], ps[:, BANKS[f"il{i}"][0], :], ACT.Relu).then_inc(relu_done, 1)

            def gate_tanh(i):
                wait_job(f"g{i}")
                first = BANKS[f"g{i}"][0]
                nc.scalar.activation(th_glu, ps[:, first:first + 2, :].rearrange("p b (c s) -> p (b c) s", s=SEQ),
                                     ACT.Tanh, scale=0.5).then_inc(th_done, 1)

            split_past("g0", 1)
            gate_tanh(0)

            def q_squares(i):
                wait_job(f"q{i}")
                for t in range(NT):
                    nc.scalar.activation(qn[:, t, 512 * i:512 * i + 512], ps[:, 2 * i + t, :], ACT.Square).then_inc(qsq_done, 1)

            split_past("q0", 1)
            q_squares(0)
            split_past("q1", 1)
            q_squares(1)

            for i in range(4):
                if i % 2 == 0:
                    split_past("q1", 5 + i // 2)
                t, hq = i // 2, i % 2
                wait_job(f"qT{i}")
                copy(qT[:, 4 * hq:4 * hq + 4, t * P:(t + 1) * P],
                     ps[:, BANKS[f"qT{i}"][0], :].rearrange("p (h s) -> p h s", h=4),
                     vec_sb[:, V_QN:V_QN + 1]).then_inc(qT_out, 1)

            for t, lg in enumerate((logits0, bias_sb)):
                split_past("a1", 2 * t)
                act.wait_ge(logit_step, 5 + 3 * t)
                for h in range(HEADS):
                    last = nc.scalar.activation(lg[:, h, :], lg[:, h, :], ACT.Exp, bias=smax[:, t, h:h + 1],
                                                accum_out=ssum[:, t, h:h + 1])
                last.then_inc(exp_done, 1)
            for t, lg in enumerate((logits0, bias_sb)):
                split_past("a1", 3 + 2 * t)
                act.wait_ge(prob_step, t + 1)
                for h in range(HEADS):
                    last = copy(lg[:, h, :], lg[:, h, :], srec[:, t, h:h + 1])
                last.then_inc(prob_done, 1)
            for i in range(6):
                if i % 2 == 0:
                    split_past("a1", 6 + i // 2)
                wait_job(f"pT{i}")
                dst = pT0[:, i * 512:(i + 1) * 512] if i < 2 else pT1[:, (i - 2) // 2, (i % 2) * 512:(i % 2) * 512 + 512]
                copy(dst, ps[:, BANKS[f"pT{i}"][0], :]).then_inc(pT_out, 1)
            split_past("g1", 2)
            for i in range(4):
                t, hq = i // 2, i % 2
                wait_job(f"oT{i}")
                copy(attnT[0][:, 4 * hq:4 * hq + 4, t * P:(t + 1) * P],
                     ps[:, BANKS[f"oT{i}"][0], :].rearrange("p (h s) -> p h s", h=4)).then_inc(oT_out, 1)
            gate_tanh(1)
            split_past("g1", 3)

            act.wait_ge(u_done, 2)
            act.wait_ge(pool_step, POOL_STEPS)
            for n in range(SHARED_TAPS):
                c, w = SHARED_CHUNKS[n % 2], n // 2
                if n >= len(products):
                    act.wait_ge(pool_step, POOL_STEPS + n - len(products) + 1)
                copy(products[n % 4], uT[:, c, w:w + SEQ], cw_sb[:, w * CC + c:w * CC + c + 1]).then_inc(tap_made, 1)
                if n % 4 == 3:
                    split_to(min(at[0] + 1, STREAM_END["wa3"]))
            split_past("wa3", 0)

            for h in range(2):
                act.wait_ge(ln_step, 2 + h)
                half = slice(4 * h, 4 * h + 4)
                nc.scalar.activation(vsq[:, half, :], conv[:, half, :], ACT.Square).then_inc(squared, 1)
            split_past("wa3", 4)

            def hi_of_conv(j):
                act.wait_ge(conv_done, j + 1)
                copy(convT[0][:, 2 * j:2 * j + 2, :], conv[:, 2 * j:2 * j + 2, :]).then_inc(conv_hi, 1)

            for j in range(4):
                act.wait_ge(ln_step, 5 + j)
                for c in (2 * j, 2 * j + 1):
                    last = nc.scalar.activation(conv[:, c, :], conv[:, c, :], ACT.Identity,
                                                scale=vec_sb[:, V_LG + c:V_LG + c + 1], bias=vec_sb[:, V_LB + c:V_LB + c + 1])
                last.then_inc(gained, 1)
                act.wait_ge(gained, j + 1)
                nc.scalar.activation(th_conv[:, 2 * j:2 * j + 2, :], conv[:, 2 * j:2 * j + 2, :], ACT.Tanh) \
                    .then_inc(th_conv_done, 1)
                if j:
                    hi_of_conv(j - 1)
            hi_of_conv(3)
            load_gain(1, a["ffn_norm"][0:1, :])
            split_to(STREAM_END["wc3"])

            def moe_act(l):
                m = moe[l]
                if l == 0:
                    norm(1, [(t, b, x_added, 8 + 2 * b + t + 1) for b in range(4) for t in range(NT)])
                else:
                    norm(3, [(t, b, mix_step, 4 * b + 2 * t + 2) for b in range(4) for t in range(NT)])
                if l == 1:
                    act.wait_ge(xn_done, 4 * 4)
                for q in range(0, 8, 2):
                    t, kq = q // 4, q % 4
                    act.wait_ge(xT_done, 8 * (1 + l) + q + 1)
                    copy(hT32[:, 4 * kq:4 * kq + 4, t * P:(t + 1) * P], ps[:, q, :].rearrange("p (k s) -> p k s", k=4)) \
                        .then_inc(xT_out, 1)

                def split(p, first, last):
                    for u in range(first, last):
                        if u % 2 == 0:
                            act.wait_ge(m["in"][moe_slot(l, u // 2)],
                                        p * (16 * PASS_BLOCKS // RING) + 16 * (u // 2 // RING + 1))
                        act.wait_ge(m["used"], p * (2 * PASS_BLOCKS) + (u + 1))
                        copy(split_hi[:, u % SPLITS, :], raw_half(moe_slot(l, u // 2), u % 2)).then_inc(m["hi"], 1)

                split(0, 0, 4)
                act.wait_ge(m["exp_in"], 1)
                nc.scalar.activation(ex_g, oneh, ACT.Exp).then_inc(m["exp_out"], 1)
                act.wait_ge(m["exp_in"], 2)
                nc.scalar.activation(ex_e, el, ACT.Exp).then_inc(m["exp_out"], 1)
                def slots_hi(p, q):
                    act.wait_ge(m["gathered"], p * 4 + (q + 1))
                    copy(hgT[0][:, 4 * q:4 * q + 4, :], ps[:, GATHER_BANK[q], :].rearrange("p (k s) -> p k s", k=4)) \
                        .then_inc(m["slots_hi"], 1)

                for q in range(4):
                    slots_hi(0, q)
                act.wait_ge(m["route_done"], 1)
                if l == 0:
                    load_gain(2, a["mix_norm_o"])
                    act.dma_start(band, a["band"]).then_inc(band_in, 16)
                    load_router(act, 1)

                def y_hi():
                    for b in range(4):
                        copy(y[0][:, b * 512:(b + 1) * 512], ps[:, BANK_Y + b, :]).then_inc(m["y_hi"], 1)

                def one_pass(p, first_pass=False):
                    def turned(e):
                        act.wait_ge(m["actT_done"], p * EPG + (e + 1))
                        copy(actT[0], ps[:, BANK_T, :].rearrange("p (k s) -> p k s", k=FC)).then_inc(m["actT_hi"], 1)

                    def tanh(e):
                        unit_done(act, l, p, e, "g")
                        nc.scalar.activation(th_gate[:, e % 2, :], ps[:, e % 2, :], ACT.Tanh, scale=0.5) \
                            .then_inc(m["th_gate_done"], 1)

                    if not first_pass:
                        split(p, 0, 4)
                        y_hi()
                    for u in range(4, 19):
                        split(p, u, u + 1)
                        if not first_pass and u - 3 in SCATTER_AT:
                            i = SCATTER_AT.index(u - 3)
                            act.wait_ge(m["scattered"], (p - 1) * 8 + (i + 1))
                            if i == 0:
                                act.wait_ge(m["x_moved"], (p - 1) * 8 + 1)
                            if i >= STAGES:
                                act.wait_ge(m["x_moved"], (p - 1) * 8 + (i - STAGES + 2))
                            copy(stage[:, i % STAGES, :], ps[:, BANK_Y + i % 4, :]).then_inc(m["staged"], 1)
                        if u == 10:
                            tanh(0)
                    act.wait_ge(m["misc_done"], p + 1)
                    copy(pickT[:], ps[:, BANK_T, 0:NT * P].rearrange("p (t s) -> p t s", t=NT))
                    copy(comb_slot, ps[:, BANK_T, NT * P:NT * P + EPG]).then_inc(m["misc_out"], 1)
                    for e in range(1, EPG):
                        gate = 8 * UNITS.index((e, "g"))
                        split(p, 19 if e == 1 else gate - 4, gate + 10)
                        turned(e - 1)
                        split(p, gate + 10, gate + 12)
                        tanh(e)
                        if e < EPG - 1:
                            split(p, gate + 12, gate + 20)
                    split(p, gate + 12, 92)
                    for q in range(3):
                        slots_hi(p + 1, q)
                    turned(EPG - 1)
                    split(p, 92, 94)
                    slots_hi(p + 1, 3)
                    split(p, 94, 96)

                more = act.value_load(npass_i[0:1, 2 * l + 1:2 * l + 2], min_val=0, max_val=NG)
                n = act.value_load(npass_i[0:1, 2 * l:2 * l + 1], min_val=NG, max_val=2 * NG)
                one_pass(0, True)
                with act.Fori(1, n) as p:
                    one_pass(p)
                unit_done(act, l, more + (NG - 1), EPG - 1, "d")
                y_hi()
                if l == 0:
                    norm(2, [(t, b, m["x_moved"], more * 8 + (8 * (NG - 1) + 4 * t + b + 2)) for t in range(NT) for b in range(4)])

            moe_act(0)
            act.dma_start(next_gain, a["ffn_norm"][1:2, :].partition_broadcast(P)).then_inc(next_gain_in, 16)
            act.wait_ge(xn_done, 4 * 3)
            act.dma_start(scale_bc, a["pool_scale_o"][0:1, :].partition_broadcast(P)).then_inc(scale_in, 16)
            for u in range(2 * NG):
                if u == SPLITS:
                    for i in range(8):
                        act.wait_ge(dT_done, i + 1)
                        copy(dT[0][:, 2 * i:2 * i + 2, :], ps[:, i, :].rearrange("p (c s) -> p c s", c=2)).then_inc(pooled_hi, 1)
                if u % 2 == 0:
                    act.wait_ge(pool_in[u // 2], 16)
                if u >= SPLITS:
                    act.wait_ge(mix_done, 2 * (u // 2 - 1))
                copy(split_hi[:, u % SPLITS, :], raw_half((POOL0 + u // 2) % RING, u % 2)).then_inc(pool_hi, 1)
            moe_act(1)

        @block.vector
        def _(dve):
            tt = nc.vector.tensor_tensor
            ts = nc.vector.tensor_scalar
            stt = nc.vector.scalar_tensor_tensor

            nc.vector.memset(minus_half[:], -0.5)
            nc.vector.memset(ones[:], 1.0).then_inc(set_up, 1)

            ticks = [0]

            def tick_off():
                ticks[0] += 1
                return nc.vector.memset(tick[:, ticks[0] - 1:ticks[0]], 0.0)

            def norm(i, permuted):
                dve.wait_ge(sq_done, 8 * (i + 1))
                nc.vector.tensor_reduce(sumsq[:, i, :], part_sq[:, i], X, ALU.add).then_inc(sum_done, 1)
                if i == 3:
                    dve.wait_ge(next_gain_in, 16)
                else:
                    dve.wait_ge(gain_in, 16 * (i + 1))
                dve.wait_ge(rstd_done, i + 1)
                for n in range(4):
                    t, h = (n // 2, n % 2) if permuted else (n % 2, n // 2)
                    dst, src, by = xn[:, t * D:(t + 1) * D], x_sb[:, t, :], next_gain if i == 3 else gain
                    if permuted:
                        half = slice(8 * h, 8 * h + 8)
                        dst = dst.rearrange("p (k j) -> p k j", k=KC)[:, half, :]
                        src, by = [z.rearrange("p (j k) -> p k j", k=KC)[:, half, :] for z in (src, by)]
                    else:
                        half = slice(h * D // 2, (h + 1) * D // 2)
                        dst, src, by = dst[:, half], src[:, half], by[:, half]
                    stt(out=dst, in0=src, scalar=rstd[:, i, t:t + 1], in1=by, op0=ALU.mult, op1=ALU.mult).then_inc(xn_done, 1)

            def low(dst, full, hi):
                return tt(dst, full, hi.bitcast(F32), ALU.subtract)

            def split_channels():
                for q in range(8):
                    t, kq = q // 4, q % 4
                    at = (slice(None), slice(4 * kq, 4 * kq + 4), slice(t * P, (t + 1) * P))
                    dve.wait_ge(normed_hi, q + 1)
                    low(hT[1][at], ps[:, q, :].rearrange("p (k s) -> p k s", k=4), hT[0][at]).then_inc(xT_out, 1)

            def turned_channels(n):
                for q in range(1, 8, 2):
                    t, kq = q // 4, q % 4
                    dve.wait_ge(xT_done, 8 * n + q + 1)
                    nc.vector.tensor_copy(hT32[:, 4 * kq:4 * kq + 4, t * P:(t + 1) * P],
                                          ps[:, q, :].rearrange("p (k s) -> p k s", k=4)).then_inc(xT_out, 1)

            def wait_job(name):
                wait_for_job(dve, name)

            norm(0, True)
            split_channels()

            conv_ops = [(chunks[i], w) for chunks in DVE_CHUNKS for w in range(TAPS) for i in range(2)]

            def convolve(first, last):
                for n in range(first, last):
                    c, w = conv_ops[n]
                    tap = cw_sb[:, w * CC + c:w * CC + c + 1]
                    if w == 0:
                        ts(conv[:, c, :], uT[:, c, 0:SEQ], tap, vec_sb[:, V_CB + c:V_CB + c + 1], ALU.mult, ALU.add) \
                            .then_inc(conv_step, 1)
                    else:
                        dve.wait_ge(conv_step, n - 1)
                        stt(out=conv[:, c, :], in0=uT[:, c, w:w + SEQ], scalar=tap, in1=conv[:, c, :],
                            op0=ALU.mult, op1=ALU.add).then_inc(conv_step, 1)

            at = [0, 0]
            taps_open = [DVE_TAPS // 2]

            def split_to(end, taps=0):
                for u in range(at[0], end):
                    b, n = u // 2, 2 * (KVW + IKW) if u // 2 in kvi_at else HALF
                    dve.wait_ge(mixer_hi, u + 1)
                    low(split_lo[:, u % SPLITS, 0:n], raw_half(b % RING, u % 2, n), split_hi[:, u % SPLITS, 0:n]) \
                        .then_inc(mixer_lo, 1)
                    more = min(taps, taps_open[0] - at[1])
                    convolve(at[1], at[1] + more)
                    at[1] += more
                at[0] = end

            def split_past(name, more, taps=0):
                split_to(STREAM_END[name] + more, taps)

            def gated_input(i):
                wait_job(f"a{i}")
                dve.wait_ge(th_done, i + 1)
                first = BANKS[f"a{i}"][0]
                stt(out=uT[:, 4 * i:4 * i + 4, PAD:PAD + SEQ], in0=th_glu, scalar=1.0,
                    in1=ps[:, first:first + 2, :].rearrange("p b (c s) -> p (b c) s", s=SEQ),
                    op0=ALU.add, op1=ALU.mult).then_inc(u_done, 1)
                dve.wait_ge(u_done, i + 1)

            def normalise_q(i):
                for t in range(NT):
                    dve.wait_ge(qsq_done, NT * i + t + 1)
                    nc.vector.tensor_reduce(hsq[:, t, 4 * i:4 * i + 4],
                                            qn[:, t, 512 * i:512 * i + 512].rearrange("p (h d) -> p h d", h=4),
                                            X, ALU.add).then_inc(hsq_done, 1)
                for t in range(NT):
                    dve.wait_ge(head_rs, 2 + NT * i + t)
                    r = hrs[:, t, 4 * i:4 * i + 4].unsqueeze(2).to_broadcast([P, 4, HD])
                    tt(qn[:, t, 512 * i:512 * i + 512].rearrange("p (h d) -> p h d", h=4),
                       ps[:, 2 * i + t, :].rearrange("p (h d) -> p h d", h=4), r, ALU.mult).then_inc(qn_done, 1)

            split_past("kvi", 2)
            wait_job("kvi")
            dve.wait_ge(kvi_out, 2)
            dve.wait_ge(head_rs, 1)
            for t in range(NT):
                ts(k_sb[:, t, :], ps[:, t, 0:P], ksq[:, 4 + t:5 + t], None, ALU.mult).then_inc(k_scaled, 1)
            split_past("iq0", 7)
            dve.wait_ge(bias_out, 1)
            nc.vector.memset(uT[:, :, 0:PAD], 0.0)
            dve.wait_ge(ident_in, 16)

            n = 0
            for i in range(12):
                split_past("iq1", 4 + i)
                t, heads = indexer_heads(i)
                S = (t + 1) * P
                dve.wait_ge(relu_done, i + 1)
                for m, h in enumerate(heads):
                    start = n in (0, IH)
                    if not start:
                        dve.wait_ge(score_step, n)
                    last = stt(out=score[:, t, 0:S], in0=il_relu[:, i % 2, m * S:(m + 1) * S], scalar=iw_sb[:, t, h:h + 1],
                               in1=causal[:, SEQ - S:SEQ] if start else score[:, t, 0:S], op0=ALU.mult, op1=ALU.add)
                    last.then_inc(score_step, 1)
                    n += 1

            dve.wait_ge(score_step, n)
            n = 0
            for r in range(TOPK // 8):
                split_past("g0", r)
                if r == 2:
                    gated_input(0)
                for t in range(NT):
                    S = (t + 1) * P
                    src = picked if r else score
                    if r:
                        dve.wait_ge(topk_step, n - 2)
                    nc.vector.max(top8[:, t, :], src[:, t, 0:S]).then_inc(topk_step, 1)
                    n += 1
                    dve.wait_ge(topk_step, n)
                    nc.vector.match_replace(picked[:, t, 0:S], top8[:, t, :], src[:, t, 0:S], TAKEN).then_inc(topk_step, 1)
                    n += 1
            split_past("q0", 0)
            dve.wait_ge(topk_step, n)
            for t in range(NT):
                S = (t + 1) * P
                ts(picked[:, t, 0:S], picked[:, t, 0:S], TAKEN, -NEG, ALU.is_equal, ALU.mult).then_inc(topk_step, 1)
            dve.wait_ge(topk_step, n + 2)
            for t in range(NT):
                S = (t + 1) * P
                stt(out=picked[:, t, 0:S], in0=picked[:, t, 0:S], scalar=NEG, in1=causal[:, SEQ - S:SEQ],
                    op0=ALU.add, op1=ALU.add).then_inc(topk_step, 1)
            split_past("q0", 1)
            dve.wait_ge(topk_step, n + 4)
            for t, (dst, src) in enumerate(((logits0, bias_sb[:, :, P:SEQ]), (bias_sb, bias_sb))):
                S = (t + 1) * P
                tt(dst, src, picked[:, t, 0:S].unsqueeze(1).to_broadcast([P, HEADS, S]), ALU.add).then_inc(logit_step, 1)
                dve.wait_ge(logit_step, t + 1)
            dve.wait_ge(vec_out, 1)
            split_past("q0", 3, 2)
            normalise_q(0)
            split_past("q1", 2, 3)
            normalise_q(1)
            split_past("q1", 7, 3)

            flat0 = logits0.rearrange("p h s -> p (h s)")
            flat1 = bias_sb.rearrange("p h s -> p (h s)")
            for t, (flat, lg) in enumerate(((flat0, logits0), (flat1, bias_sb))):
                wait_job(f"lg{t}")
                first, end = BANKS[f"lg{t}"][0], BANKS[f"lg{t}"][-1] + 1
                src = ps[:, first:end, :].rearrange("p b n -> p (b n)")
                stt(out=flat, in0=src, scalar=HD ** -0.5, in1=flat, op0=ALU.mult, op1=ALU.add).then_inc(logit_step, 1)
                dve.wait_ge(logit_step, 3 + 3 * t)
                nc.vector.tensor_reduce(hms[:, t, :], lg, X, ALU.max).then_inc(logit_step, 1)
                dve.wait_ge(logit_step, 4 + 3 * t)
                ts(smax[:, t, :], hms[:, t, :], -1.0, None, ALU.mult).then_inc(logit_step, 1)
                split_past("a1", 1 + t, 2)
            for t in range(NT):
                split_past("a1", 2 + 2 * t, 2)
                dve.wait_ge(exp_done, t + 1)
                nc.vector.reciprocal(srec[:, t, :], ssum[:, t, :]).then_inc(prob_step, 1)
            split_past("g1", 2, 3)
            for i in range(4):
                t, hq = i // 2, i % 2
                part = (slice(None), slice(4 * hq, 4 * hq + 4), slice(t * P, (t + 1) * P))
                dve.wait_ge(oT_out, i + 1)
                low(attnT[1][part], ps[:, BANKS[f"oT{i}"][0], :].rearrange("p (h s) -> p h s", h=4), attnT[0][part]) \
                    .then_inc(attn_lo, 1)
            convolve(at[1], DVE_TAPS // 2)
            at[1] = DVE_TAPS // 2
            gated_input(1)
            taps_open[0] = DVE_TAPS

            def add_x(n, t, bank):
                cols = x_sb[:, t, n * 512:(n + 1) * 512]
                tt(cols, ps[:, bank, :], cols, ALU.add).then_inc(x_added, 1)

            def add_job(name):
                wait_job(name)
                for t, bank in enumerate(BANKS[name]):
                    add_x(int(name[-1]), t, bank)

            for n in range(3):
                split_past(f"wa{n}", 2, 4)
                add_job(f"wa{n}")
            split_past("wa3", 0, 4)

            convolve(at[1], DVE_TAPS)
            wait_job("mean")
            ts(mean_sb, ps[:, BANKS["mean"][0], 0:SEQ], 1.0 / CCH, None, ALU.mult).then_inc(ln_step, 1)
            dve.wait_ge(ln_step, 1)
            for h in range(2):
                half = conv[:, 4 * h:4 * h + 4, :]
                tt(half, half, mean_sb.unsqueeze(1).to_broadcast([P, 4, SEQ]), ALU.subtract).then_inc(ln_step, 1)
            split_past("wa3", 4)
            wait_job("var")
            ts(rvar, ps[:, BANKS["var"][0], 0:NT], 1.0 / CCH, EPS, ALU.mult, ALU.add).then_inc(ln_step, 1)
            dve.wait_ge(ln_pool, 1)
            for t in range(NT):
                ts(rstd_diag[:, t, :], ident, rstd_conv[:, t:t + 1], None, ALU.mult).then_inc(diag_done, 1)
            add_job("wa3")

            def scale_conv(j):
                if j == 0:
                    wait_job("rstd")
                two = conv[:, 2 * j:2 * j + 2, :]
                tt(two, two, ps[:, BANKS["rstd"][0], 0:SEQ].unsqueeze(1).to_broadcast([P, 2, SEQ]), ALU.mult).then_inc(ln_step, 1)

            def silu(j):
                dve.wait_ge(th_conv_done, j + 1)
                two = conv[:, 2 * j:2 * j + 2, :]
                stt(out=two, in0=th_conv[:, 2 * j:2 * j + 2, :], scalar=1.0, in1=two, op0=ALU.add, op1=ALU.mult) \
                    .then_inc(conv_done, 1)

            def lo_of_conv(j):
                dve.wait_ge(conv_hi, j + 1)
                two = slice(2 * j, 2 * j + 2)
                low(convT[1][:, two, :], conv[:, two, :], convT[0][:, two, :]).then_inc(conv_lo, 1)

            scale_conv(0)
            scale_conv(1)
            silu(0)
            scale_conv(2)
            silu(1)
            lo_of_conv(0)
            scale_conv(3)
            silu(2)
            lo_of_conv(1)
            silu(3)
            lo_of_conv(2)
            lo_of_conv(3)
            for n in range(4):
                split_past(f"wc{n}", min(2, 4 * (3 - n)))
                if n == 0:
                    dve.wait_ge(x_added, 8)
                add_job(f"wc{n}")

            def moe_dve(l):
                m = moe[l]
                norm(1 if l == 0 else 3, True)
                if l == 1:
                    dve.wait_ge(xn_done, 4 * 4)
                turned_channels(1 + l)

                def split(p, first, last):
                    for u in range(first, last):
                        dve.wait_ge(m["hi"], p * (2 * PASS_BLOCKS) + (u + 1))
                        low(split_lo[:, u % SPLITS, :], raw_half(moe_slot(l, u // 2), u % 2), split_hi[:, u % SPLITS, :]) \
                            .then_inc(m["lo"], 1)

                split(0, 0, 4)
                steps = [0]

                def chain(ins):
                    steps[0] += 1
                    ins.then_inc(m["route_step"], 1)
                    dve.wait_ge(m["route_step"], steps[0])

                def first_max(dst, src, val):
                    chain(nc.vector.tensor_reduce(val, src, X, ALU.max))
                    chain(tt(t4a, src, val.to_broadcast([P, NT, 4]), ALU.is_equal))
                    chain(tt(t4a, t4a, prio.unsqueeze(1).to_broadcast([P, NT, 4]), ALU.mult))
                    chain(nc.vector.tensor_reduce(gmax, t4a, X, ALU.max))
                    chain(tt(dst, t4a, gmax.to_broadcast([P, NT, 4]), ALU.is_equal))

                col = lambda i: stat[:, i, :].unsqueeze(2)
                dve.wait_ge(m["router_done"], 1)
                dve.wait_ge(router_in, 16 * 4 * (l + 1))
                src = ps[:, 2, 0:64].rearrange("p (t c) -> p t c", t=NT)[:, :, 0:20]
                chain(tt(lgt, src, router_b[:].unsqueeze(1).to_broadcast([P, NT, 20]), ALU.add))
                glog = lgt[:, :, 0:NG]
                chain(nc.vector.tensor_reduce(col(0), glog, X, ALU.max))
                chain(tt(oneh, glog, col(0).to_broadcast([P, NT, NG]), ALU.subtract))
                tick_off().then_inc(m["exp_in"], 1)
                dve.wait_ge(m["exp_out"], 1)
                chain(nc.vector.tensor_reduce(col(1), ex_g, X, ALU.add))
                chain(nc.vector.reciprocal(col(2), col(1)))
                first_max(oneh, glog, col(0))
                tick_off().then_inc(m["rank_in"], 1)
                p4 = prod.rearrange("p t (g e) -> p t g e", g=NG)
                chain(tt(p4, lgt[:, :, NG:20].rearrange("p t (g e) -> p t g e", g=NG),
                         oneh.unsqueeze(3).to_broadcast([P, NT, NG, EPG]), ALU.mult))
                chain(nc.vector.tensor_reduce(el, prod.rearrange("p t (g e) -> p t e g", g=NG), X, ALU.add))
                dve.wait_ge(m["rank_done"], 1)
                rank = ps[:, BANK_T, 0:16].rearrange("p (t c) -> p t c", t=NT)[:, :, 0:NG]
                chain(stt(out=rank_in[:, :, 0:NG], in0=rank, scalar=1.0, in1=oneh, op0=ALU.add, op1=ALU.mult))
                chain(ts(rank_in[:, :, NG:2 * NG], rank_in[:, :, 0:NG], -1.0 - P, None, ALU.add))
                chain(ts(rank_in[:, :, 0:NG], rank_in[:, :, 0:NG], -1.0, None, ALU.add))
                nc.vector.memset(rank_in[:, :, 2 * NG:], -1.0)
                for t in range(NT):
                    last = ts(pick[:, t, :], slot_no, rank_in[:, t, 0:1], None, ALU.is_equal)
                last.then_inc(m["pick_ready"], 1)
                first_max(sel1, el, col(3))
                chain(stt(out=t4b, in0=sel1, scalar=NEG, in1=el, op0=ALU.mult, op1=ALU.add))
                first_max(sel2, t4b, col(4))
                chain(tt(el, el, col(3).to_broadcast([P, NT, EPG]), ALU.subtract))
                tick_off().then_inc(m["exp_in"], 1)
                chain(tt(sel1, sel1, sel2, ALU.add))
                dve.wait_ge(m["exp_out"], 2)
                chain(tt(wgt, ex_e, sel1, ALU.mult))
                chain(nc.vector.tensor_reduce(col(5), wgt, X, ALU.add))
                chain(nc.vector.reciprocal(col(6), col(5)))
                chain(tt(col(6), col(6), col(2), ALU.mult))
                chain(tt(wgt, wgt, col(6).to_broadcast([P, NT, EPG]), ALU.mult))
                chain(ts(wgt, wgt, 0.5, None, ALU.mult))
                c4 = comb[:, :, 0:NE].rearrange("p t (g e) -> p t g e", g=NG)
                chain(tt(c4, wgt.unsqueeze(2).to_broadcast([P, NT, NG, EPG]),
                         oneh.unsqueeze(3).to_broadcast([P, NT, NG, EPG]), ALU.mult))
                nc.vector.tensor_copy(comb[:, :, NE:2 * NE], comb[:, :, 0:NE])
                nc.vector.memset(comb[:, :, 2 * NE:], 0.0)
                chain(nc.vector.tensor_reduce(cnt[:, 0:1], ps[:, BANK_T, 16:16 + NG], X, ALU.max))
                chain(ts(cnt[:, 1:2], cnt[:, 0:1], float(P), float(NG), ALU.is_gt, ALU.mult))
                chain(nc.vector.tensor_copy(npass_i[:, 2 * l + 1:2 * l + 2], cnt[:, 1:2]))
                chain(ts(cnt[:, 2:3], cnt[:, 1:2], float(NG), None, ALU.add))
                chain(nc.vector.tensor_copy(npass_i[:, 2 * l:2 * l + 1], cnt[:, 2:3]))
                nc.vector.tensor_copy(comb_now, comb[:, :, 0:EPG])
                tick_off().then_inc(m["x_moved"], 1)
                tick_off().then_inc(m["route_done"], 1)

                def pick_tokens(p):
                    nc.vector.tensor_copy(comb_now, comb[:, :, bass.ds(p * EPG, EPG)])
                    for t in range(NT):
                        last = ts(pick[:, t, :], slot_no, rank_in[:, t, bass.ds(p, 1)], None, ALU.is_equal)
                    last.then_inc(m["pick_ready"], 1)

                def slots_lo(p, q):
                    dve.wait_ge(m["slots_hi"], p * 4 + (q + 1))
                    part = (slice(None), slice(4 * q, 4 * q + 4))
                    low(hgT[1][part], ps[:, GATHER_BANK[q], :].rearrange("p (k s) -> p k s", k=4), hgT[0][part]) \
                        .then_inc(m["gather_out"], 1)

                def y_lo(p, b):
                    dve.wait_ge(m["y_hi"], p * 4 + (b + 1))
                    cols = slice(b * 512, (b + 1) * 512)
                    low(y[1][:, cols], ps[:, BANK_Y + b, :], y[0][:, cols]).then_inc(m["y_lo"], 1)

                def add_y(p, i):
                    t, b = i // 4, i % 4
                    dve.wait_ge(m["scattered"], p * 8 + (i + 1))
                    cols = x_sb[:, t, b * 512:(b + 1) * 512]
                    tt(cols, ps[:, BANK_Y + b, :], cols, ALU.add).then_inc(m["x_moved"], 1)

                for q in range(4):
                    slots_lo(0, q)

                def one_pass(p, first_pass=False):
                    def gate(e):
                        dve.wait_ge(m["th_gate_done"], p * EPG + (e + 1))
                        stt(out=gated[:, e % 2, :], in0=th_gate[:, e % 2, :], scalar=1.0, in1=ps[:, e % 2, :],
                            op0=ALU.add, op1=ALU.mult).then_inc(m["gated_done"], 1)

                    def times_up(e):
                        dve.wait_ge(m["gated_done"], p * EPG + (e + 1))
                        dve.wait_ge(m["misc_out"], p + 1)
                        unit_done(dve, l, p, e, "u")
                        by_j = lambda t: t.rearrange("p (j k) -> p j k", k=FC)
                        stt(out=act.rearrange("p (k j) -> p j k", k=FC), in0=by_j(gated[:, e % 2, :]),
                            scalar=comb_slot[:, e:e + 1], in1=by_j(ps[:, 2, :]), op0=ALU.mult, op1=ALU.mult) \
                            .then_inc(m["act_done"], 1)

                    def turned_lo(e):
                        dve.wait_ge(m["actT_hi"], p * EPG + (e + 1))
                        low(actT[1], ps[:, BANK_T, :].rearrange("p (k s) -> p k s", k=FC), actT[0]).then_inc(m["actT_out"], 1)

                    if not first_pass:
                        split(p, 0, 4)
                    for i in range(12):
                        if not first_pass and i < 4:
                            y_lo(p - 1, i)
                        split(p, 4 + i, 5 + i)
                        if i == 8:
                            gate(0)
                    split(p, 16, 20)
                    times_up(0)
                    for e in range(1, EPG):
                        at = 8 * UNITS.index((e, "g"))
                        split(p, at + 4, at + 10)
                        turned_lo(e - 1)
                        split(p, at + 10, at + 12)
                        if e == 1:
                            dve.wait_ge(m["misc_done"], p + 1)
                            pick_tokens(p + 1)
                        split(p, at + 12, at + 13)
                        gate(e)
                        if e < EPG - 1:
                            split(p, at + 13, at + 28)
                            times_up(e)
                    split(p, at + 13, 92)
                    times_up(EPG - 1)
                    for q in range(3):
                        slots_lo(p + 1, q)
                    turned_lo(EPG - 1)
                    split(p, 92, 94)
                    slots_lo(p + 1, 3)
                    split(p, 94, 96)

                more = dve.value_load(npass_i[0:1, 2 * l + 1:2 * l + 2], min_val=0, max_val=NG)
                n = dve.value_load(npass_i[0:1, 2 * l:2 * l + 1], min_val=NG, max_val=2 * NG)
                one_pass(0, True)
                with dve.Fori(1, n) as p:
                    one_pass(p)
                for b in range(4):
                    y_lo(more + (NG - 1), b)
                dve.wait_ge(m["x_moved"], more * 8 + (8 * (NG - 1) + 1))
                for i in range(8):
                    add_y(more + (NG - 1), i)

            moe_dve(0)

            norm(2, False)
            dve.wait_ge(scale_in, 16)

            def pool_split(u):
                dve.wait_ge(pool_hi, u + 1)
                low(split_lo[:, u % SPLITS, :], raw_half((POOL0 + u // 2) % RING, u % 2), split_hi[:, u % SPLITS, :]) \
                    .then_inc(pool_lo, 1)

            for u in range(SPLITS):
                pool_split(u)
            for i in range(8):
                dve.wait_ge(pooled_hi, i + 1)
                low(dT[1][:, 2 * i:2 * i + 2, :], ps[:, i, :].rearrange("p (c s) -> p c s", c=2), dT[0][:, 2 * i:2 * i + 2, :]) \
                    .then_inc(dT_out, 1)
            for i in range(8):
                g, t = i // 2, i % 2
                if 1 <= i <= SPLITS:
                    pool_split(SPLITS + i - 1)
                dve.wait_ge(mix_done, i + 1)
                if i >= 2:
                    dve.wait_ge(mix_step, 2 * i - 2)
                tt(mixed[:, i % 2, :], ps[:, i, :], scale_bc[:, g * 512:(g + 1) * 512], ALU.mult).then_inc(mix_step, 1)
                dve.wait_ge(mix_step, 2 * i + 1)
                cols = x_sb[:, t, g * 512:(g + 1) * 512]
                tt(cols, mixed[:, i % 2, :], cols, ALU.add).then_inc(mix_step, 1)

            moe_dve(1)

        @block.tensor
        def _(pe):
            mm = nc.tensor.matmul

            def turn(dst, src, n=P):
                return nc.tensor.transpose(dst, src, ident[0:n, 0:n])

            pe.wait_ge(ident_in, 16)
            pe.wait_ge(set_up, 1)

            def turn_vectors():
                pe.wait_ge(rows_in, 16 * 9)
                turn(ps[:, 2, 0:V_ROWS], vec_rows[0:V_ROWS, 0, :], V_ROWS)
                for h in range(2):
                    last = turn(ps[:, 2, 64 + h * CW_HALF:64 + (h + 1) * CW_HALF], vec_rows[0:CW_HALF, 1 + h, :], CW_HALF)
                last.then_inc(vec_done, 1)
                mm(ps[0:HEADS, 3, :], rel_sb, one_hot, start=True, stop=True).then_inc(vec_done, 1)

            def turn_x(i, n):
                for q in range(8):
                    t, kq = q // 4, q % 4
                    if kq % 2 == 0:
                        pe.wait_ge(xn_done, 4 * i + 2 * t + kq // 2 + 1)
                    for k in range(4 * kq, 4 * kq + 4):
                        last = turn(ps[:, q, (k % 4) * P:(k % 4 + 1) * P], xn[:, t * D + k * P:t * D + (k + 1) * P])
                    last.then_inc(xT_done, 1)
                pe.wait_ge(xT_out, 8 * (n + 1))

            def start_job(name):
                for b in BANKS[name]:
                    if (owner := owner_before(name, b)) is not None:
                        signal, count = emptied(owner)
                        pe.wait_ge(signal, count)

            def product(out, stationary, moving, start, stop, **how):
                (sh, sl), (mh, ml) = stationary, moving
                mm(out, sh, mh, start=start, stop=False, **how)
                mm(out, sh, ml, start=False, stop=False, **how)
                return mm(out, sl, mh, start=False, stop=stop, **how)

            def pick_parts(parts, *index):
                return [part[index] for part in parts]

            ALL = slice(None)
            stream = [0]

            def next_unit(k, n, off=0):
                pe.wait_ge(mixer_lo, stream[0] + 1)
                slot = stream[0] % SPLITS
                stream[0] += 1
                return unit(slot, k, n)

            def unit(slot, k, n, off=0):
                return [w[:, slot, off:off + k * n].rearrange("p (k n) -> p k n", k=k) for w in (split_hi, split_lo)]

            def channels_job(name, between=lambda q: None):
                start_job(name)
                for q in range(8):
                    between(q)
                    w = next_unit(2, 512)
                    for k in range(2):
                        first, end = q == 0 and k == 0, q == 7 and k == 1
                        for c in range(4):
                            last = product(ps[:, BANKS[name][c // 2], (c % 2) * SEQ:(c % 2 + 1) * SEQ],
                                           pick_parts(w, ALL, k, slice(c * P, (c + 1) * P)), pick_parts(hT, ALL, 2 * q + k),
                                           first and c % 2 == 0, end, skip_group_check=True)
                    last.then_inc(mixer_used, 1)

            def tokens_job(name, between=lambda q: None):
                start_job(name)
                for q in range(8):
                    between(q)
                    w = next_unit(2, 512)
                    for k in range(2):
                        for t, b in enumerate(BANKS[name]):
                            last = product(ps[:, b, :], pick_parts(hT, ALL, 2 * q + k, slice(t * P, (t + 1) * P)),
                                           pick_parts(w, ALL, k), q == 0 and k == 0, q == 7 and k == 1)
                    last.then_inc(mixer_used, 1)

            def kvi_job():
                start_job("kvi")
                for q in range(8):
                    if q == 4:
                        turn_vectors()
                    kv = next_unit(2, KVW)
                    ki = unit(q % SPLITS, 2, IKW, 2 * KVW)
                    for k in range(2):
                        first, end = q == 0 and k == 0, q == 7 and k == 1
                        for t in range(NT):
                            h = pick_parts(hT, ALL, 2 * q + k, slice(t * P, (t + 1) * P))
                            product(ps[:, t, 0:KVW], h, pick_parts(kv, ALL, k), first, end, skip_group_check=True)
                            last = product(ps[:, t, KVW:KVW + IKW], h, pick_parts(ki, ALL, k), False, end,
                                           skip_group_check=True)
                    last.then_inc(mixer_used, 1)

            def out_job(name, parts, between=lambda q: None):
                start_job(name)
                for q in range(4):
                    between(q)
                    w = next_unit(2, 512)
                    for k in range(2):
                        for t, b in enumerate(BANKS[name]):
                            last = product(ps[:, b, :], pick_parts(parts, ALL, 2 * q + k, slice(t * P, (t + 1) * P)),
                                           pick_parts(w, ALL, k), q == 0 and k == 0, q == 3 and k == 1)
                    last.then_inc(mixer_used, 1)

            def turn_k():
                start_job("kT")
                pe.wait_ge(k_scaled, 2)
                for t in range(NT):
                    turn(ps[:, 6, t * P:(t + 1) * P], k_sb[:, t, :])
                for t in range(NT):
                    last = turn(ps[:, 6, SEQ + t * P:SEQ + (t + 1) * P], ik2[:, t, :])
                last.then_inc(job_done, 1)

            def flip_bias():
                start_job("flip")
                pe.wait_ge(vec_out, 2)
                pe.wait_ge(bias_loaded, 16)
                for c in range(4):
                    last = mm(ps[:, 2 + c, :], upside, bias_up[:, 2 * c:2 * c + 2, :].rearrange("p h s -> p (h s)"),
                              start=True, stop=True)
                last.then_inc(job_done, 1)

            def indexer(i):
                start_job(f"il{i}")
                t, heads = indexer_heads(i)
                S = (t + 1) * P
                for m, h in enumerate(heads):
                    rows = slice((h % 2) * ID, (h % 2 + 1) * ID)
                    last = mm(ps[:, BANKS[f"il{i}"][0], m * S:(m + 1) * S], iqT[rows, h // 2, t * P:(t + 1) * P],
                              ikT[rows, 0:S], start=True, stop=True)
                last.then_inc(job_done, 1)

            def turn_q(i):
                start_job(f"qT{i}")
                t, hq = i // 2, i % 2
                pe.wait_ge(qn_done, 2 * hq + t + 1)
                for h in range(4):
                    last = turn(ps[:, BANKS[f"qT{i}"][0], h * P:(h + 1) * P], qn[:, t, (4 * hq + h) * HD:(4 * hq + h + 1) * HD])
                last.then_inc(job_done, 1)

            def logits(t):
                start_job(f"lg{t}")
                S = (t + 1) * P
                per = 512 // S
                pe.wait_ge(qT_out, 2 * t + 2)
                for h in range(HEADS):
                    last = mm(ps[:, BANKS[f"lg{t}"][h // per], (h % per) * S:(h % per + 1) * S],
                              qT[:, h, t * P:(t + 1) * P], kT[:, 0:S], start=True, stop=True)
                last.then_inc(job_done, 1)

            def turn_probs(i):
                start_job(f"pT{i}")
                t, st, hq = (0, 0, i) if i < 2 else (1, (i - 2) // 2, i % 2)
                pe.wait_ge(prob_done, t + 1)
                lg = (logits0, bias_sb)[t]
                for h in range(4):
                    last = turn(ps[:, BANKS[f"pT{i}"][0], h * P:(h + 1) * P], lg[:, 4 * hq + h, st * P:(st + 1) * P])
                last.then_inc(job_done, 1)

            def attend(i):
                start_job(f"oT{i}")
                t, hq = i // 2, i % 2
                pe.wait_ge(pT_out, 2 + 4 * t)
                for st in range(t + 1):
                    probs = pT1[:, st, hq * 512:(hq + 1) * 512] if t else pT0[:, hq * 512:(hq + 1) * 512]
                    last = mm(ps[:, BANKS[f"oT{i}"][0], :], v_sb[:, st, :], probs, start=(st == 0), stop=(st == t))
                last.then_inc(job_done, 1)

            def channel_sum(name, src, h):
                if h == 0:
                    start_job(name)
                for c in range(4 * h, 4 * h + 4):
                    last = mm(ps[:, BANKS[name][0], 0:SEQ], ones[:], src[:, c, :], start=(c == 0), stop=(c == CC - 1))
                if h:
                    last.then_inc(job_done, 1)

            def squares_sum(h):
                if h == 0:
                    start_job("var")
                for t in range(NT):
                    for c in range(4 * h, 4 * h + 4):
                        last = mm(ps[:, BANKS["var"][0], t:t + 1], vsq[:, c, t * P:(t + 1) * P], ones[:, 0:1],
                                  start=(c == 0 and t == 0), stop=(c == CC - 1), skip_group_check=True)
                if h:
                    last.then_inc(job_done, 1)

            def beside_iq0(q):
                if q == 3:
                    turn_k()

            def beside_iq1(q):
                if q == 4:
                    flip_bias()

            def beside_a0(q):
                if q == 2:
                    pe.wait_ge(iq_out, 2)
                    pe.wait_ge(kT_out, 1)
                if q >= 2:
                    indexer(q - 2)

            def beside_g0(q):
                if q < 6:
                    indexer(6 + q)

            def beside_a1(q):
                if q in (3, 4):
                    turn_q(2 * q - 6)
                    turn_q(2 * q - 5)
                if q in (5, 6):
                    logits(q - 5)

            def beside_g1(q):
                if q == 4:
                    turn_probs(0)
                    turn_probs(1)
                if q in (6, 7):
                    turn_probs(2 * q - 10)
                    turn_probs(2 * q - 9)

            def beside_wa3(q):
                if q == 2:
                    pe.wait_ge(conv_step, DVE_TAPS // 2)
                    pe.wait_ge(pool_step, POOL_STEPS)
                    channel_sum("mean", conv, 0)

            turn_x(0, 0)
            kvi_job()
            channels_job("iq0", beside_iq0)
            channels_job("iq1", beside_iq1)
            channels_job("a0", beside_a0)
            channels_job("g0", beside_g0)
            tokens_job("q0")
            tokens_job("q1")
            channels_job("a1", beside_a1)
            channels_job("g1", beside_g1)
            for i in range(4):
                attend(i)
            pe.wait_ge(attn_lo, 4)
            for n in range(3):
                out_job(f"wa{n}", attnT)
            out_job("wa3", attnT, beside_wa3)
            pe.wait_ge(conv_step, DVE_TAPS)
            pe.wait_ge(pool_step, POOL_STEPS + SHARED_TAPS)
            channel_sum("mean", conv, 1)
            for h in range(2):
                pe.wait_ge(squared, h + 1)
                squares_sum(h)
            start_job("rstd")
            pe.wait_ge(diag_done, NT)
            for t in range(NT):
                last = mm(ps[:, BANKS["rstd"][0], t * P:(t + 1) * P], ones[:], rstd_diag[:, t, :], start=True, stop=True)
            last.then_inc(job_done, 1)
            out_job("wc0", convT, lambda q: pe.wait_ge(conv_lo, q + 1))
            for n in range(1, 4):
                out_job(f"wc{n}", convT)
            
            def moe_pe(l):
                m = moe[l]
                pe.sem_inc(m["used"], SPLITS)
                turn_x(1 if l == 0 else 3, 1 + l)
                pe.wait_ge(router_in, 16 * 4 * (l + 1))
                for t in range(NT):
                    for k in range(KC):
                        last = mm(ps[:, 2, 32 * t:32 * t + 20], hT32[:, k, t * P:(t + 1) * P], router_w[:, k, :],
                                  start=(k == 0), stop=(k == KC - 1))
                last.then_inc(m["router_done"], 1)
                pe.wait_ge(m["rank_in"], 1)
                mm(ps[:, BANK_T, 0:NG], before, oneh[:, 0, :], start=True, stop=True)
                mm(ps[:, BANK_T, 8:8 + NG], ones[:], oneh[:, 0, :], start=True, stop=False)
                mm(ps[:, BANK_T, 8:8 + NG], before, oneh[:, 1, :], start=False, stop=True)
                mm(ps[:, BANK_T, 16:16 + NG], ones[:], oneh[:, 0, :], start=True, stop=False)
                mm(ps[:, BANK_T, 16:16 + NG], ones[:], oneh[:, 1, :], start=False, stop=True).then_inc(m["rank_done"], 1)

                def gather(p, quads=range(4)):
                    pe.wait_ge(m["pick_ready"], p + 1)
                    for q in quads:
                        if q >= 2:
                            pe.wait_ge(m["gather_out"], p * 4 + (q - 1))
                        for k in range(4 * q, 4 * q + 4):
                            for t in range(NT):
                                last = mm(ps[:, GATHER_BANK[q], (k % 4) * P:(k % 4 + 1) * P],
                                          xn[:, t * D + k * P:t * D + (k + 1) * P], pick[:, t, :],
                                          start=(t == 0), stop=(t == NT - 1))
                        last.then_inc(m["gathered"], 1)

                gather(0)
                pe.wait_ge(m["route_done"], 1)

                def scatter(p, i, last_pass=False):
                    t, b = i // 4, i % 4
                    if t == 0:
                        pe.wait_ge(m["y_lo"], p * 4 + (b + 1))
                    elif last_pass:
                        pe.wait_ge(m["x_moved"], p * 8 + (b + 2))
                    else:
                        pe.wait_ge(m["staged"], p * 8 + (b + 1))
                    for part in range(2):
                        last = mm(ps[:, BANK_Y + b, :], pickT[:, t, :], y[part][:, b * 512:(b + 1) * 512],
                                  start=part == 0, stop=part == 1)
                    last.then_inc(m["scattered"], 1)

                def one_pass(p, first_pass=False):
                    unit_no = [0]

                    def weights(k, n):
                        u = unit_no[0]
                        unit_no[0] += 1
                        pe.wait_ge(m["lo"], p * (2 * PASS_BLOCKS) + (u + 1))
                        return unit(u % SPLITS, k, n)

                    def project(bank, between=lambda q: None):
                        for q in range(8):
                            w = weights(2, 512)
                            for k in range(2):
                                last = product(ps[:, bank, :], pick_parts(hgT, ALL, 2 * q + k), pick_parts(w, ALL, k),
                                               q == 0 and k == 0, q == 7 and k == 1)
                            last.then_inc(m["used"], 1)
                            between(q)

                    def turn_act(e):
                        pe.wait_ge(m["act_done"], p * EPG + (e + 1))
                        if e == 0:
                            pe.wait_ge(m["misc_out"], p + 1)
                        for k in range(FC):
                            last = turn(ps[:, BANK_T, k * P:(k + 1) * P], act[:, k * P:(k + 1) * P])
                        last.then_inc(m["actT_done"], 1)

                    def down(e):
                        pe.wait_ge(m["actT_out"], p * EPG + (e + 1))
                        if e == 0 and not first_pass:
                            pe.wait_ge(m["staged"], p * 8)
                        for k in range(FC):
                            for half in range(2):
                                w = weights(2, 512)
                                for n in range(2):
                                    last = product(ps[:, BANK_Y + 2 * half + n, :], pick_parts(actT, ALL, k),
                                                   pick_parts(w, ALL, n), e == 0 and k == 0, e == EPG - 1 and k == FC - 1)
                                last.then_inc(m["used"], 1)

                    pe.wait_ge(m["gather_out"], p * 4 + 4)

                    def beside_first(u):
                        if not first_pass and u in SCATTER_AT:
                            scatter(p - 1, SCATTER_AT.index(u))
                        if u == 15:
                            for t in range(NT):
                                turn(ps[:, BANK_T, t * P:(t + 1) * P], pick[:, t, :])
                            for t in range(NT):
                                last = mm(ps[:, BANK_T, SEQ:SEQ + EPG], pick[:, t, :], comb_now[:, t, :],
                                          start=(t == 0), stop=(t == NT - 1))
                            last.then_inc(m["misc_done"], 1)

                    for e, kind in UNITS:
                        if kind == "g":
                            project(e % 2, (lambda q: turn_act(e - 1) if q == 5 else None) if e else beside_first)
                        elif kind == "u":
                            project(BANK_U, (lambda q: None) if e else (lambda q: beside_first(8 + q)))
                            if e == EPG - 1:
                                gather(p + 1, range(3))
                                turn_act(e)
                                gather(p + 1, range(3, 4))
                        else:
                            down(e)

                more = pe.value_load(npass_i[0:1, 2 * l + 1:2 * l + 2], min_val=0, max_val=NG)
                n = pe.value_load(npass_i[0:1, 2 * l:2 * l + 1], min_val=NG, max_val=2 * NG)
                one_pass(0, True)
                with pe.Fori(1, n) as p:
                    one_pass(p)
                for i in range(8):
                    scatter(more + (NG - 1), i, True)

            moe_pe(0)

            pe.wait_ge(band_in, 16)
            for c in range(KC):
                if c % 8 == 0:
                    pe.wait_ge(xn_done, 4 * 2 + 2 * (c // 8) + 2)
                bank, off, g = c // 2, (c % 2) * SEQ, c // 4
                mm(ps[:, bank, off:off + SEQ], xn[:, c * P:(c + 1) * P], band[:, 0, g * SEQ:(g + 1) * SEQ],
                   start=True, stop=False)
                last = mm(ps[:, bank, off + P:off + SEQ], xn[:, D + c * P:D + (c + 1) * P],
                          band[:, 1, g * SEQ + P:(g + 1) * SEQ], start=False, stop=True)
                if c % 2:
                    last.then_inc(dT_done, 1)
            for g in range(NG):
                for h in range(2):
                    pe.wait_ge(pool_lo, 2 * g + h + 1)
                pe.wait_ge(dT_out, 8 if g == 0 else 2 * g + 2)
                for t in range(NT):
                    for h in range(2):
                        w = unit((2 * g + h) % SPLITS, 2, 512)
                        for k in range(2):
                            last = product(ps[:, 2 * g + t, :], pick_parts(dT, ALL, 4 * g + 2 * h + k, slice(t * P, (t + 1) * P)),
                                           pick_parts(w, ALL, k), h == 0 and k == 0, h == 1 and k == 1)
                    last.then_inc(mix_done, 1)

            moe_pe(1)


def shape_constants():
    i = np.arange(P)
    before = (i[:, None] < i[None, :]).astype(np.float32)
    slots = np.broadcast_to(i.astype(np.float32), (P, P))
    s = np.arange(SEQ)
    causal = np.where(s[None, :] - P <= i[:, None], 0.0, NEG).astype(np.float32)
    prio = np.broadcast_to(np.array([4, 3, 2, 1, 0, 0, 0, 0], np.float32), (P, 8))
    const = np.concatenate([np.eye(P, dtype=np.float32), before, slots, causal, prio, np.eye(P, dtype=np.float32)[::-1]], axis=1)
    dist = np.maximum(255 - np.arange(512), 0)
    exact = BUCKETS // 2
    large = exact + (np.log(np.maximum(dist, 1).astype(np.float32) / exact) / np.float32(np.log(128 / exact))
                     * (BUCKETS - exact)).astype(np.int32)
    bucket = np.where(dist < exact, dist, np.minimum(large, BUCKETS - 1))
    one_hot = (np.arange(BUCKETS)[:, None] == bucket[None, :]).astype(np.float32)
    t = np.arange(SEQ)
    band = np.zeros((SEQ, NG, SEQ), np.float32)
    for g, w in enumerate(WINDOWS):
        d = t[None, :] - t[:, None]
        band[:, g] = np.where((d >= 0) & (d < w), 1.0 / np.minimum(t + 1, w)[None, :], 0.0) - (d == 0)
    band = band.reshape(NT, P, NG * SEQ).transpose(1, 0, 2)
    return {"const": np.ascontiguousarray(const), "one_hot": one_hot, "band": np.ascontiguousarray(band)}


def kernel(**inputs):
    import concourse.bacc as bacc
    from concourse.bass_utils import run_bass_kernel_spmd

    nc = bacc.Bacc("TRN2", target_bir_lowering=False, num_devices=1)
    arrays = {f"in_{n}": np.ascontiguousarray(v) for n, v in inputs.items()}
    arrays |= {f"in_{n}": v for n, v in shape_constants().items()}
    aps = {n[3:]: nc.dram_tensor(n, v.shape, mybir.dt.from_np(v.dtype), kind="ExternalInput").ap()
           for n, v in arrays.items()}
    aps["out"] = nc.dram_tensor("out_0", (1, SEQ, D), F32, kind="ExternalOutput").ap()
    build(nc, aps)
    r = run_bass_kernel_spmd(nc, [arrays], core_ids=[0])
    return r.results[0]["out_0"]
```
